# Optimizing a Trainium2 kernel written in Bass

```python
import math
import jax
import jax.numpy as jnp
from jax import lax
import numpy as np

D_MODEL = 1024
BATCH = 1
SEQ = 256
DEPTH = 4

CHUNK = 64
N_MIXERS = 3
HEAD_DIM = 64
N_HEADS = D_MODEL // HEAD_DIM
D_FF = -(-8 * D_MODEL // (3 * 256)) * 256
RMS_EPS = 1e-6
ROPE_THETA = 10000.0
RW_DECAY_LORA = max(32, int(round(1.8 * D_MODEL ** 0.5 / 32)) * 32)
RW_AAA_LORA = max(32, int(round(1.8 * D_MODEL ** 0.5 / 32)) * 32)
RW_MV_LORA = max(32, int(round(1.3 * D_MODEL ** 0.5 / 32)) * 32)
RW_GATE_LORA = max(32, int(round(0.6 * D_MODEL ** 0.8 / 32)) * 32)
RW_GN_EPS = HEAD_DIM * 1e-5
SB_QBLOCK = 128
DS_TOPK_MAX = 256
DS_IDX_HEADS = 8
DS_IDX_DIM = 64
DS_QBLOCK = CHUNK
DS_IN_WIDTH = 3 * D_MODEL + DS_IDX_HEADS * DS_IDX_DIM + DS_IDX_DIM + DS_IDX_HEADS
N_RWKV = (DEPTH + 2) // 3
N_SB = (DEPTH + 1) // 3
N_DSA = DEPTH // 3


def rms_norm(x, g):
    xf = x.astype(jnp.float32)
    y = xf * lax.rsqrt(jnp.mean(xf * xf, axis=-1, keepdims=True) + RMS_EPS)
    return (y * g.astype(jnp.float32)).astype(x.dtype)

def rope(x, pos):
    half = x.shape[-1] // 2
    inv = 1.0 / (ROPE_THETA ** (jnp.arange(half, dtype=jnp.float32) / half))
    ang = pos.astype(jnp.float32)[:, None] * inv[None, :]
    cos = jnp.cos(ang)[None, :, None, :]
    sin = jnp.sin(ang)[None, :, None, :]
    xf = x.astype(jnp.float32)
    x1, x2 = xf[..., :half], xf[..., half:]
    return jnp.concatenate([x1 * cos - x2 * sin, x1 * sin + x2 * cos], axis=-1).astype(x.dtype)

def swiglu(h, w_gu, w_down):
    g, u = jnp.split(h @ w_gu, 2, axis=-1)
    return (jax.nn.silu(g) * u) @ w_down

def rwkv7_time_mix(h, v_first, mix, w_rkv, w0, w1, w2, a0, a1, a2, g1, g2, k_k, k_a, r_k, ln_w, ln_b, w_out, v_res):
    B, S, D = h.shape
    f32 = jnp.float32
    shifted = jnp.pad(h, ((0, 0), (1, 0), (0, 0)))[:, :-1]
    xm = h[:, :, None, :] + (shifted - h)[:, :, None, :] * mix
    rkv = jnp.einsum('bsjd,jde->bsje', xm[:, :, :3], w_rkv)
    r, k, v = rkv[:, :, 0], rkv[:, :, 1], rkv[:, :, 2]
    xv, xw, xa, xg = xm[:, :, 2], xm[:, :, 3], xm[:, :, 4], xm[:, :, 5]
    logw = -jax.nn.softplus(-(w0 + jnp.tanh(xw @ w1) @ w2).astype(f32)) - 0.5
    decay = jnp.exp(-jnp.exp(logw))
    a = jax.nn.sigmoid((a0 + (xa @ a1) @ a2).astype(f32))
    g = jax.nn.sigmoid(xg @ g1) @ g2
    v_layer = v
    if v_res is not None:
        v0, v1, v2 = v_res
        v = v + (v_first - v) * jax.nn.sigmoid(v0 + (xv @ v1) @ v2)

    def heads(t):
        return t.astype(f32).reshape(B, S, N_HEADS, HEAD_DIM)

    kk = heads(k * k_k)
    kk = kk * lax.rsqrt(jnp.maximum(jnp.sum(kk * kk, axis=-1, keepdims=True), 1e-24))
    k = k.astype(f32) * (1.0 + (a - 1.0) * k_a)
    rh, kh, vh, wh, ah = heads(r), heads(k), heads(v), heads(decay), heads(a)

    def step(state, inp):
        r_t, w_t, k_t, v_t, kk_t, a_t = inp
        sa = jnp.einsum('bhvk,bhk->bhv', state, kk_t)
        state = (state * w_t[:, :, None, :]
                 - sa[..., None] * (kk_t * a_t)[:, :, None, :]
                 + v_t[..., None] * k_t[:, :, None, :])
        return state, jnp.einsum('bhvk,bhk->bhv', state, r_t)

    def tmaj(t):
        return jnp.moveaxis(t, 1, 0)

    s0 = jnp.zeros((B, N_HEADS, HEAD_DIM, HEAD_DIM), f32)
    _, y = lax.scan(step, s0, (tmaj(rh), tmaj(wh), tmaj(kh), tmaj(vh), tmaj(kk), tmaj(ah)))
    y = jnp.moveaxis(y, 0, 1)
    mu = jnp.mean(y, axis=-1, keepdims=True)
    var = jnp.mean(jnp.square(y - mu), axis=-1, keepdims=True)
    y = ((y - mu) * lax.rsqrt(var + RW_GN_EPS)).reshape(B, S, D) * ln_w + ln_b
    y = y + (jnp.sum(rh * kh * r_k, axis=-1, keepdims=True) * vh).reshape(B, S, D)
    out = (y * g).astype(h.dtype) @ w_out
    return out, v_layer

def stick_breaking_attention(h, w_qkv, w_out):
    B, S, D = h.shape
    f32 = jnp.float32
    qkv = (h @ w_qkv).reshape(B, S, 3, N_HEADS, HEAD_DIM)
    q = qkv[:, :, 0].astype(f32) * HEAD_DIM ** -0.5
    k = qkv[:, :, 1].astype(f32)
    v = qkv[:, :, 2]
    nb = S // SB_QBLOCK
    q_blocks = jnp.moveaxis(q.reshape(B, nb, SB_QBLOCK, N_HEADS, HEAD_DIM), 1, 0)
    kpos = jnp.arange(S)

    def block(args):
        q_b, i = args
        qpos = i * SB_QBLOCK + jnp.arange(SB_QBLOCK)
        earlier = kpos[None, :] < qpos[:, None]
        z = jnp.einsum('bqhd,bshd->bhqs', q_b, k)
        log_1m = jnp.where(earlier, jax.nn.log_sigmoid(-z), 0.0)
        between = lax.cumsum(log_1m, axis=3, reverse=True) - log_1m
        att = jnp.where(earlier, jnp.exp(jax.nn.log_sigmoid(z) + between), 0.0)
        return jnp.einsum('bhqs,bshd->bqhd', att.astype(v.dtype), v)

    o = lax.map(block, (q_blocks, jnp.arange(nb)))
    o = jnp.moveaxis(o, 0, 1).reshape(B, S, D)
    return o @ w_out

def dsa_attention(h, w_in, q_norm, k_norm, w_out):
    B, S, D = h.shape
    f32 = jnp.float32
    pos = jnp.arange(S)
    c3 = 3 * D
    c4 = c3 + DS_IDX_HEADS * DS_IDX_DIM
    c5 = c4 + DS_IDX_DIM
    q, k, v, qi, ki, wi = jnp.split(h @ w_in, [D, 2 * D, c3, c4, c5], axis=-1)
    q = rope(rms_norm(q.reshape(B, S, N_HEADS, HEAD_DIM), q_norm), pos)
    k = rope(rms_norm(k.reshape(B, S, N_HEADS, HEAD_DIM), k_norm), pos)
    v = v.reshape(B, S, N_HEADS, HEAD_DIM)
    qi = rope(qi.reshape(B, S, DS_IDX_HEADS, DS_IDX_DIM), pos)
    ki = rope(ki.reshape(B, S, 1, DS_IDX_DIM), pos)[:, :, 0]
    wi = wi * (DS_IDX_HEADS ** -0.5 * DS_IDX_DIM ** -0.5)
    n_sel = min(DS_TOPK_MAX, S // 4)
    nb = S // DS_QBLOCK

    def blocks(t):
        return jnp.moveaxis(t.reshape(B, nb, DS_QBLOCK, *t.shape[2:]), 1, 0)

    kpos = jnp.arange(S)

    def block(args):
        q_b, qi_b, wi_b, i = args
        qpos = i * DS_QBLOCK + jnp.arange(DS_QBLOCK)
        visible = kpos[None, :] < ((qpos // CHUNK + 1) * CHUNK)[:, None]
        idx = jnp.einsum('bqhd,bsd->bqhs', qi_b, ki)
        score = jnp.einsum('bqh,bqhs->bqs', wi_b, jax.nn.relu(idx)).astype(f32)
        score = jnp.where(visible[None], score, -jnp.inf)
        top_val, top_idx = lax.top_k(score, n_sel)
        valid = top_val > -jnp.inf
        k_sel = jax.vmap(lambda kb, ib: kb[ib])(k, top_idx)
        v_sel = jax.vmap(lambda vb, ib: vb[ib])(v, top_idx)
        logits = jnp.einsum('bqhd,bqkhd->bhqk', q_b, k_sel).astype(f32) * HEAD_DIM ** -0.5
        logits = jnp.where(valid[:, None], logits, -jnp.inf)
        p = jax.nn.softmax(logits, axis=-1)
        return jnp.einsum('bhqk,bqkhd->bqhd', p.astype(v.dtype), v_sel)

    o = lax.map(block, (blocks(q), blocks(qi), blocks(wi), jnp.arange(nb)))
    o = jnp.moveaxis(o, 0, 1).reshape(B, S, D)
    return o @ w_out

def first_inputs(seed: int = 0) -> dict:
    key = jax.random.key(seed)
    ks = iter(jax.random.split(key, 64))
    D, F, H, dh = D_MODEL, D_FF, N_HEADS, HEAD_DIM
    nA, nB, nC = N_RWKV, N_SB, N_DSA
    out_scale = D ** -0.5 / math.sqrt(2 * DEPTH)

    def nrm(shape, scale):
        return jax.random.normal(next(ks), shape, jnp.float32) * scale

    def unif(shape, lo, hi):
        return jax.random.uniform(next(ks), shape, jnp.float32, lo, hi)

    return {
        'x': nrm((BATCH, SEQ, D), 1.0),
        'norm_mix': 1.0 + nrm((DEPTH, D), 0.02),
        'norm_ffn': 1.0 + nrm((DEPTH, D), 0.02),
        'ffn_w_gu': nrm((DEPTH, D, 2 * F), D ** -0.5),
        'ffn_w_down': nrm((DEPTH, F, D), F ** -0.5 / math.sqrt(2 * DEPTH)),
        'rw_mix': unif((nA, 6, D), 0.0, 1.0),
        'rw_w_rkv': nrm((nA, 3, D, D), D ** -0.5),
        'rw_w0': unif((nA, D), -5.0, 1.0),
        'rw_w1': nrm((nA, D, RW_DECAY_LORA), D ** -0.5),
        'rw_w2': nrm((nA, RW_DECAY_LORA, D), 0.1 * RW_DECAY_LORA ** -0.5),
        'rw_a0': nrm((nA, D), 0.1),
        'rw_a1': nrm((nA, D, RW_AAA_LORA), D ** -0.5),
        'rw_a2': nrm((nA, RW_AAA_LORA, D), 0.3 * RW_AAA_LORA ** -0.5),
        'rw_g1': nrm((nA, D, RW_GATE_LORA), D ** -0.5),
        'rw_g2': nrm((nA, RW_GATE_LORA, D), RW_GATE_LORA ** -0.5),
        'rw_v0': 1.0 + nrm((nA - 1, D), 0.1),
        'rw_v1': nrm((nA - 1, D, RW_MV_LORA), D ** -0.5),
        'rw_v2': nrm((nA - 1, RW_MV_LORA, D), 0.3 * RW_MV_LORA ** -0.5),
        'rw_k_k': 0.85 + nrm((nA, D), 0.05),
        'rw_k_a': 1.0 + nrm((nA, D), 0.05),
        'rw_r_k': nrm((nA, H, dh), 0.1),
        'rw_ln_w': 1.0 + nrm((nA, D), 0.02),
        'rw_ln_b': nrm((nA, D), 0.02),
        'rw_w_out': nrm((nA, D, D), out_scale),
        'sb_w_qkv': nrm((nB, D, 3 * D), D ** -0.5),
        'sb_w_out': nrm((nB, D, D), out_scale),
        'ds_w_in': nrm((nC, D, DS_IN_WIDTH), D ** -0.5),
        'ds_q_norm': 1.0 + nrm((nC, dh), 0.02),
        'ds_k_norm': 1.0 + nrm((nC, dh), 0.02),
        'ds_w_out': nrm((nC, D, D), out_scale),
    }

def first_block(x, norm_mix, norm_ffn, ffn_w_gu, ffn_w_down,
              rw_mix, rw_w_rkv, rw_w0, rw_w1, rw_w2, rw_a0, rw_a1, rw_a2, rw_g1, rw_g2,
              rw_v0, rw_v1, rw_v2, rw_k_k, rw_k_a, rw_r_k, rw_ln_w, rw_ln_b, rw_w_out,
              sb_w_qkv, sb_w_out,
              ds_w_in, ds_q_norm, ds_k_norm, ds_w_out):
    v_first = None
    for i in range(DEPTH):
        kind, j = i % N_MIXERS, i // N_MIXERS
        h = rms_norm(x, norm_mix[i])
        if kind == 0:
            v_res = None if j == 0 else (rw_v0[j - 1], rw_v1[j - 1], rw_v2[j - 1])
            y, v_layer = rwkv7_time_mix(h, v_first, rw_mix[j], rw_w_rkv[j], rw_w0[j], rw_w1[j], rw_w2[j],
                                        rw_a0[j], rw_a1[j], rw_a2[j], rw_g1[j], rw_g2[j],
                                        rw_k_k[j], rw_k_a[j], rw_r_k[j], rw_ln_w[j], rw_ln_b[j],
                                        rw_w_out[j], v_res)
            if j == 0:
                v_first = v_layer
        elif kind == 1:
            y = stick_breaking_attention(h, sb_w_qkv[j], sb_w_out[j])
        else:
            y = dsa_attention(h, ds_w_in[j], ds_q_norm[j], ds_k_norm[j], ds_w_out[j])
        x = x + y
        x = x + swiglu(rms_norm(x, norm_ffn[i]), ffn_w_gu[i], ffn_w_down[i])
    return x


DEPTH_2 = 2

H_NA = 4
H_DIL = 6
H_GQ = 6
H_GKV = 2
NA_W = H_NA * HEAD_DIM
DIL_W = H_DIL * HEAD_DIM
GQ_W = H_GQ * HEAD_DIM
GKV_W = H_GKV * HEAD_DIM
D_MIX = NA_W + DIL_W + GQ_W
D_IN = 3 * NA_W + 3 * DIL_W + GQ_W + 2 * GKV_W

GRID_W = 64
NA_KH_MAX = 8
NA_KW = 16
DIL_PATTERNS = ((128, 1), (512, 4), (2048, 16))
ROPE_THETA_2 = 500000.0
ROPE_DIMS = HEAD_DIM // 4
AXIAL_THETA = 10000.0
Q_BLK = 128
D_FF_2 = 2816
CONV_W = 3
EPS = 1e-6
NEG_INF = -1e30


def rms_norm_2(x, g):
    xf = x.astype(jnp.float32)
    y = xf * lax.rsqrt(jnp.mean(xf * xf, axis=-1, keepdims=True) + EPS)
    return (y * g.astype(jnp.float32)).astype(x.dtype)

def rope_cos_sin(pos, dim, theta):
    inv = theta ** (-jnp.arange(0, dim, 2, dtype=jnp.float32) / dim)
    ang = pos.astype(jnp.float32)[:, None] * inv[None, :]
    return jnp.cos(ang), jnp.sin(ang)

def rotate(x, cos, sin):
    half = x.shape[-1] // 2
    x1 = x[..., :half].astype(jnp.float32)
    x2 = x[..., half:].astype(jnp.float32)
    c = cos[None, :, None, :]
    s = sin[None, :, None, :]
    return jnp.concatenate([x1 * c - x2 * s, x2 * c + x1 * s], axis=-1).astype(x.dtype)

def partial_rotary(x, cos, sin):
    return jnp.concatenate([rotate(x[..., :ROPE_DIMS], cos, sin), x[..., ROPE_DIMS:]], axis=-1)

def axial_rotary(x, cos_r, sin_r, cos_c, sin_c):
    half = x.shape[-1] // 2
    return jnp.concatenate([rotate(x[..., :half], cos_r, sin_r), rotate(x[..., half:], cos_c, sin_c)], axis=-1)

def neighbourhood_tables(S):
    rows = S // GRID_W
    kh = min(NA_KH_MAX, rows)
    t = jnp.arange(S)
    r = t // GRID_W
    c = t % GRID_W
    r0 = jnp.clip(r - kh // 2, 0, rows - kh)
    c0 = jnp.clip(c - NA_KW // 2, 0, GRID_W - NA_KW)
    kr = r0[:, None] + jnp.arange(kh)[None, :]
    kc = c0[:, None] + jnp.arange(NA_KW)[None, :]
    idx = (kr[:, :, None] * GRID_W + kc[:, None, :]).reshape(S, kh * NA_KW)
    dr = (kr - r[:, None] + NA_KH_MAX - 1)[:, :, None]
    dc = (kc - c[:, None] + NA_KW - 1)[:, None, :]
    return idx, dr, dc

def neighbourhood_attention(q, k, v, rpb, idx, dr, dc):
    B, S, H, hd = q.shape
    nk = idx.shape[1]
    nb = S // Q_BLK
    scale = hd ** -0.5
    bias = rpb[:, dr, dc].reshape(H, S, nk).astype(jnp.float32)
    qb = q.reshape(B, nb, Q_BLK, H, hd).transpose(1, 0, 2, 3, 4)
    idxb = idx.reshape(nb, Q_BLK, nk)
    biasb = bias.reshape(H, nb, Q_BLK, nk).transpose(1, 0, 2, 3)

    def block(args):
        qi, ii, bi = args
        kg = k[:, ii]
        vg = v[:, ii]
        s = jnp.einsum('bqhd,bqkhd->bhqk', qi, kg).astype(jnp.float32) * scale + bi[None]
        p = jax.nn.softmax(s, axis=-1).astype(v.dtype)
        return jnp.einsum('bhqk,bqkhd->bqhd', p, vg)

    o = lax.map(block, (qb, idxb, biasb))
    return o.transpose(1, 0, 2, 3, 4).reshape(B, S, H * hd)

def dilated_tables(S):
    t = jnp.arange(S)
    idxs, valids = [], []
    for w, d in DIL_PATTERNS:
        n = (w // 2) // d
        pos = t[:, None] + (jnp.arange(-n, n + 1) * d)[None, :]
        valids.append((pos >= 0) & (pos < S))
        idxs.append(jnp.clip(pos, 0, S - 1))
    return tuple(idxs), tuple(valids)

def dilated_window_attention(q, k, v, idxs, valids):
    B, S, H, hd = q.shape
    nb = S // Q_BLK
    scale = hd ** -0.5
    qb = q.reshape(B, nb, Q_BLK, H, hd).transpose(1, 0, 2, 3, 4)
    idxb = tuple(i.reshape(nb, Q_BLK, -1) for i in idxs)
    valb = tuple(m.reshape(nb, Q_BLK, -1) for m in valids)

    def block(args):
        qi, ii, mm = args
        lses, outs = [], []
        for ig, mg in zip(ii, mm):
            kg = k[:, ig]
            vg = v[:, ig]
            s = jnp.einsum('bqhd,bqkhd->bhqk', qi, kg).astype(jnp.float32) * scale
            s = jnp.where(mg[None, None], s, NEG_INF)
            lse = jax.nn.logsumexp(s, axis=-1)
            p = jnp.exp(s - lse[..., None]).astype(v.dtype)
            outs.append(jnp.einsum('bhqk,bqkhd->bqhd', p, vg))
            lses.append(lse)
        wts = jax.nn.softmax(jnp.stack(lses), axis=0).astype(v.dtype)
        return jnp.einsum('gbhq,gbqhd->bqhd', wts, jnp.stack(outs))

    o = lax.map(block, (qb, idxb, valb))
    return o.transpose(1, 0, 2, 3, 4).reshape(B, S, H * hd)

def gqa_block_attention(q, k, v):
    B, S, Hq, hd = q.shape
    Hkv = k.shape[2]
    g = Hq // Hkv
    nb = S // Q_BLK
    scale = hd ** -0.5
    qb = q.reshape(B, nb, Q_BLK, Hkv, g, hd).transpose(1, 0, 2, 3, 4, 5)

    def block(qi):
        s = jnp.einsum('bqkgd,bskd->bkgqs', qi, k).astype(jnp.float32) * scale
        p = jax.nn.softmax(s, axis=-1).astype(v.dtype)
        return jnp.einsum('bkgqs,bskd->bqkgd', p, v)

    o = lax.map(block, qb)
    return o.transpose(1, 0, 2, 3, 4, 5).reshape(B, S, Hq * hd)

def depthwise_conv_centred(z, w, b):
    S = z.shape[1]
    pad = CONV_W // 2
    zp = jnp.pad(z, ((0, 0), (pad, pad), (0, 0)))
    out = zp[:, 0:S] * w[0] + b
    for j in range(1, CONV_W):
        out = out + zp[:, j:j + S] * w[j]
    return out

def mixer_sublayer(x, n1, w_in_l, qg, kg, rpb_l, og, w_out_l, tables):
    (na_idx, na_dr, na_dc, dil_idx, dil_val, cos1, sin1, cos_r, sin_r, cos_c, sin_c) = tables
    B, S, _ = x.shape
    h = rms_norm_2(x, n1)
    proj = h @ w_in_l
    sizes = (NA_W, NA_W, NA_W, DIL_W, DIL_W, DIL_W, GQ_W, GKV_W, GKV_W)
    cuts = [int(c) for c in np.cumsum(sizes)[:-1]]
    qa, ka, va, qd, kd, vd, qc, kc, vc = jnp.split(proj, cuts, axis=-1)

    def heads(z, n):
        return z.reshape(B, S, n, HEAD_DIM)

    qa = rms_norm_2(heads(qa, H_NA), qg[0])
    ka = rms_norm_2(heads(ka, H_NA), kg[0])
    out_a = neighbourhood_attention(qa, ka, heads(va, H_NA), rpb_l, na_idx, na_dr, na_dc)
    qd = partial_rotary(rms_norm_2(heads(qd, H_DIL), qg[1]), cos1, sin1)
    kd = partial_rotary(rms_norm_2(heads(kd, H_DIL), kg[1]), cos1, sin1)
    out_d = dilated_window_attention(qd, kd, heads(vd, H_DIL), dil_idx, dil_val)
    qc = axial_rotary(rms_norm_2(heads(qc, H_GQ), qg[2]), cos_r, sin_r, cos_c, sin_c)
    kc = axial_rotary(rms_norm_2(heads(kc, H_GKV), kg[2]), cos_r, sin_r, cos_c, sin_c)
    out_c = gqa_block_attention(qc, kc, heads(vc, H_GKV))

    mix = jnp.concatenate([
        rms_norm_2(out_a, og[:NA_W]),
        rms_norm_2(out_d, og[NA_W:NA_W + DIL_W]),
        rms_norm_2(out_c, og[NA_W + DIL_W:]),
    ], axis=-1)
    return x + mix @ w_out_l

def channel_sublayer(x, n2, w_gu, cw, cb, w_dn):
    h = rms_norm_2(x, n2)
    g, u = jnp.split(h @ w_gu, 2, axis=-1)
    g = depthwise_conv_centred(g, cw, cb)
    return x + (jax.nn.gelu(g, approximate=False) * u) @ w_dn

def second_inputs(seed: int = 0) -> dict:
    key = jax.random.key(seed)
    ks = jax.random.split(key, 13)

    def nrm(k, shape, s):
        return s * jax.random.normal(k, shape, jnp.float32)

    return {
        'x': nrm(ks[0], (BATCH, SEQ, D_MODEL), 1.0),
        'norm1_g': 1.0 + nrm(ks[1], (DEPTH_2, D_MODEL), 0.02),
        'w_in': nrm(ks[2], (DEPTH_2, D_MODEL, D_IN), D_MODEL ** -0.5),
        'q_norm_g': 1.0 + nrm(ks[3], (DEPTH_2, 3, HEAD_DIM), 0.02),
        'k_norm_g': 1.0 + nrm(ks[4], (DEPTH_2, 3, HEAD_DIM), 0.02),
        'rpb': nrm(ks[5], (DEPTH_2, H_NA, 2 * NA_KH_MAX - 1, 2 * NA_KW - 1), 0.1),
        'out_norm_g': 1.0 + nrm(ks[6], (DEPTH_2, D_MIX), 0.02),
        'w_out': nrm(ks[7], (DEPTH_2, D_MIX, D_MODEL), D_MIX ** -0.5),
        'norm2_g': 1.0 + nrm(ks[8], (DEPTH_2, D_MODEL), 0.02),
        'w_gate_up': nrm(ks[9], (DEPTH_2, D_MODEL, 2 * D_FF_2), D_MODEL ** -0.5),
        'conv_w': nrm(ks[10], (DEPTH_2, CONV_W, D_FF_2), CONV_W ** -0.5),
        'conv_b': nrm(ks[11], (DEPTH_2, D_FF_2), 0.02),
        'w_down': nrm(ks[12], (DEPTH_2, D_FF_2, D_MODEL), D_FF_2 ** -0.5),
    }

def second_block(x, norm1_g, w_in, q_norm_g, k_norm_g, rpb, out_norm_g, w_out, norm2_g, w_gate_up, conv_w, conv_b, w_down):
    S = x.shape[1]
    t = jnp.arange(S, dtype=jnp.int32)
    cos1, sin1 = rope_cos_sin(t, ROPE_DIMS, ROPE_THETA_2)
    cos_r, sin_r = rope_cos_sin(t // GRID_W, HEAD_DIM // 2, AXIAL_THETA)
    cos_c, sin_c = rope_cos_sin(t % GRID_W, HEAD_DIM // 2, AXIAL_THETA)
    na_idx, na_dr, na_dc = neighbourhood_tables(S)
    dil_idx, dil_val = dilated_tables(S)
    tables = (na_idx, na_dr, na_dc, dil_idx, dil_val, cos1, sin1, cos_r, sin_r, cos_c, sin_c)
    for l in range(DEPTH_2):
        x = mixer_sublayer(x, norm1_g[l], w_in[l], q_norm_g[l], k_norm_g[l], rpb[l],
                           out_norm_g[l], w_out[l], tables)
        x = channel_sublayer(x, norm2_g[l], w_gate_up[l], conv_w[l], conv_b[l], w_down[l])
    return x


def setup_inputs(seed=0):
    out = dict(first_inputs(seed))
    for name, value in second_inputs(seed + 1).items():
        if name != "x":
            out[name + "_2"] = value
    return out


def reference(
    x, norm_mix, norm_ffn, ffn_w_gu, ffn_w_down, rw_mix, rw_w_rkv, rw_w0, rw_w1, rw_w2, rw_a0,
    rw_a1, rw_a2, rw_g1, rw_g2, rw_v0, rw_v1, rw_v2, rw_k_k, rw_k_a, rw_r_k, rw_ln_w, rw_ln_b,
    rw_w_out, sb_w_qkv, sb_w_out, ds_w_in, ds_q_norm, ds_k_norm, ds_w_out, norm1_g_2, w_in_2,
    q_norm_g_2, k_norm_g_2, rpb_2, out_norm_g_2, w_out_2, norm2_g_2, w_gate_up_2, conv_w_2,
    conv_b_2, w_down_2,
):
    x = first_block(
        x, norm_mix, norm_ffn, ffn_w_gu, ffn_w_down, rw_mix, rw_w_rkv, rw_w0, rw_w1, rw_w2,
        rw_a0, rw_a1, rw_a2, rw_g1, rw_g2, rw_v0, rw_v1, rw_v2, rw_k_k, rw_k_a, rw_r_k, rw_ln_w,
        rw_ln_b, rw_w_out, sb_w_qkv, sb_w_out, ds_w_in, ds_q_norm, ds_k_norm, ds_w_out,
    )
    return second_block(
        x, norm1_g_2, w_in_2, q_norm_g_2, k_norm_g_2, rpb_2, out_norm_g_2, w_out_2, norm2_g_2,
        w_gate_up_2, conv_w_2, conv_b_2, w_down_2,
    )


_drawn_inputs = setup_inputs


def setup_inputs(seed=0):
    import zlib

    import numpy as np

    out = dict(_drawn_inputs(seed))
    spreads = {}
    factors = {'norm_ffn': 2.986,
     'rw_w1': 8.0,
     'rw_w2': 8.0,
     'rw_v0': 45.346,
     'rw_v1': 17.867,
     'rw_k_k': 4.075,
     'rw_ln_w': 5.504,
     'ds_q_norm': 8.0,
     'ds_k_norm': 8.0,
     'q_norm_g_2': 4.538,
     'k_norm_g_2': 4.429,
     'out_norm_g_2': 2.856,
     'norm2_g_2': 3.694,
     'conv_b_2': 5.477,
     'rw_v2': 6.867,
     'rpb_2': 3.196}
    for name, (base, spread) in spreads.items():
        noise = np.random.default_rng([zlib.crc32(name.encode()), seed]).standard_normal(out[name].shape)
        drawn = base * np.exp(spread * noise) if base else spread * noise
        out[name] = jnp.asarray(drawn.astype(out[name].dtype))
    for name, factor in factors.items():
        out[name] = (out[name] * factor).astype(out[name].dtype)
    return out
```

```python
import numpy as np
import concourse.bass as bass
from concourse import mybir
from contextlib import ExitStack, contextmanager

D, S, P = 1024, 256, 128
KT = D // P
NT = S // P
NH, HD = 16, 64
F_FF = 2816
FT = F_FF // P
CH = 64
N_SEL, IDX_HEADS = 64, 8
GRID_W, NA_KW, NA_KH = 64, 16, 8
EPS, GN_EPS = 1e-6, 64e-5
KAPPA = float(np.exp(-0.5))
NEG = -1e30
TAKEN = -3e38
LORA_W, LORA_A, LORA_V, LORA_G = 64, 64, 32, 160

FULL = [("rwkv", 0), ("ffn", 0), ("stick", 0), ("ffn", 1), ("dsa", 0), ("ffn", 2), ("rwkv", 1), ("ffn", 3),
        ("multi", 0), ("ffn", 4), ("multi", 1), ("ffn", 5)]
PROJ = {"rwkv": 24, "stick": 24, "dsa": 30, "multi": 24}
UNITS = {"rwkv": 38, "stick": 32, "dsa": 38, "multi": 32, "ffn": 44}

TAB = {}
_at = 0
for _n, _w in [("ident", P), ("ones", P), ("tri", P), ("head_ones", P), ("head_mean", P),
               ("rot0", P), ("rot1", P), ("rot2", P), ("cos0", S), ("sin0", S), ("cos1", S), ("sin1", S),
               ("cos2", S), ("sin2", S), ("stick_neg", 3 * P), ("visible", 2 * S), ("dilated", 2 * S),
               ("scan_keep", S), ("rw_mask", 4 * P), ("eps", 1), ("gn_eps", 1), ("pair_neg", P),
               ("pair_neg_t", P)] + [(f"level{i}", P) for i in range(1, 7)]:
    TAB[_n] = (_at, _w)
    _at += _w
TAB_W = _at
VEC = {}
_at = 0
for _n, _w in ([(f"mix_g{i}", KT) for i in range(6)] + [(f"ffn_g{i}", KT) for i in range(6)]
               + [(f"{v}{j}", KT) for j in range(2) for v in
                  ("mix0_", "mix1_", "mix2_", "mix3_", "mix4_", "mix5_", "w0_", "a0_", "k_k_", "k_a_", "r_k_",
                   "ln_w_", "ln_b_")]
               + [("v0_", KT)] + [(f"gain{i}", 24) for i in range(3)] + [(f"out_g{i}", KT) for i in range(2)]
               + [(f"conv{i}", 4 * FT) for i in range(2)]):
    VEC[_n] = (_at, _w)
    _at += _w
VEC_W = _at


AHEAD = 3


class Steps:

    def __init__(self, eng, sem):
        self.eng, self.sem, self.n, self.off = eng, sem, 0, 0

    def did(self, ins):
        ins.then_inc(self.sem, 1)
        self.n += 1

    def settle(self):
        self.eng.wait_ge(self.sem, self.off + self.n)

    @contextmanager
    def repeat(self, count, per, first=0):
        with self.eng.Fori(first, first + count) as i:
            before, self.off = self.n, i * per - first * per
            yield i
            assert self.n - before == per, (self.n - before, per)
        self.n, self.off = before + count * per, 0


def plan_layers(layers):
    out, u, dn, proj, part, vt, heads, pairs = [], 0, 0, 4, 0, 0, 0, 0
    tiles = us = 0
    for kind, idx in layers:
        out.append(dict(kind=kind, idx=idx, u=u, us=us, d=dn, proj=proj, part=part, vt=vt, heads=heads, pairs=pairs,
                        tiles=tiles, rw=sum(o["kind"] == "rwkv" for o in out),
                        mixers=sum(o["kind"] != "ffn" for o in out),
                        hs=sum(o["kind"] != "rwkv" for o in out),
                        convs=sum(o["kind"] == "ffn" and o["idx"] >= 4 for o in out),
                        multis=sum(o["kind"] == "multi" for o in out)))
        u += UNITS[kind]
        us += UNITS[kind] - (3 if kind == "rwkv" else 0)
        part += 1
        if kind == "ffn":
            dn += FT
        else:
            proj += PROJ[kind]
            vt += 4
        if kind in ("dsa", "multi"):
            heads += NH
            tiles += 21 if kind == "dsa" else 16
        if kind in ("stick", "dsa", "multi"):
            pairs += NH // 2
    return out, u, dn


def build_program(nc, layers, x_in, wa, wd, tab_in, vec_in, na_in, out):
    f32 = mybir.dt.float32
    ALU, ACT, AX = mybir.AluOpType, mybir.ActivationFunctionType, mybir.AxisListType
    ds = bass.ds
    plan, n_units, n_downs = plan_layers(layers)
    PARTS = len(plan)
    ctx = ExitStack()
    with ctx:
        def sb(name, shape):
            return ctx.enter_context(nc.sbuf_tensor(name, shape, f32))

        xT = sb("xT", [P, KT, S])
        hT = sb("hT", [P, KT, S])
        sq = sb("sq", [P, KT, S])
        qkv = sb("qkv", [P, 29, S])
        vtok = sb("vtok", [P, NT, D])
        oT = sb("oT", [P, KT, S])
        end_oT = nc.sbuf_base
        ring_a = sb("ring_a", [P, 4, D])
        ring_d = sb("ring_d", [P, 2, D])
        tab = sb("tab_sb", [P, TAB_W])
        vec = sb("vec_sb", [P, VEC_W])
        planes = sb("planes", [P, 8, KT * S])
        end_planes = nc.sbuf_base
        v_first = sb("v_first", [P, KT, S])
        dec = sb("dec", [P, KT, 2, P + 1])
        work = sb("work", [P, 8, S])
        small = sb("small", [P, 64])

        f32r = mybir.dt.float32r
        PLANE = KT * S * 4

        def split(name, shape, offset):
            return nc.alloc_sbuf_tensor_at(name, shape, f32r, offset=offset)
        at_planes, at_vtok = end_planes - 8 * PLANE, end_oT - 2 * PLANE
        w_split = split("w_split", [P, 4, 2, D], at_planes)
        d_split = split("d_split", [P, 2, 2, D], at_planes + 4 * PLANE)
        act_split = split("act_split", [P, 2, 2, S], at_planes + 6 * PLANE)
        x_split = [split("h_split", [P, 2, KT, S], at_vtok),
                   split("x_split1", [P, 2, KT, S], at_planes + 4 * PLANE),
                   split("o_split", [P, 2, KT, S], at_planes + 6 * PLANE)]
        h_split = x_split[0]
        rw_o_split = split("rw_o_split", [P, 2, KT, S], end_oT - 2 * PLANE - 29 * S * 4)

        def T(name):
            a, w = TAB[name]
            return tab[:, a:a + w]

        def V(name, k=None):
            a, w = VEC[name]
            return vec[:, a:a + w] if k is None else vec[:, ds(k + a, 1)] if not isinstance(k, int) \
                else vec[:, a + k:a + k + 1]

        B = [ctx.enter_context(nc.psum_tensor(f"bank{i}", [P, 512], f32)) for i in range(8)]

        sems = {}

        class _S:
            pass
        for n in ("const_loaded x_loaded x_added sq_ready ssum_ready std_ready h_ready a_used d_used silu_ready "
                  "act_ready conv_ready dve_step act_step pool_step proj_evac vtok_done vtok_ready stored "
                  "z_done zm_ready ln_ready sp_ready cum_done lg_ready p_ready pv_done ot_evac "
                  "s_done sm_ready nmx_ready e_ready pn_ready t_done pt_ready "
                  "nr_in nr_mm nr_std qk_ready idx_mm idx_relu idx_added wi_mm wi_ready sel_ready na_loaded "
                  "on_sq on_sum on_std on_ready "
                  "xx_ready xm_ready lora1_mm lora1_ready lora2_mm lora2_ready kk_sq kk_sum kk_std kk_done "
                  "cs_ready dec_ready rk_ready rk_sum keys_ready kt_mm kt_ready factor_ready score_mm score_ready "
                  "inv_init lx_mm q_ready xn_mm xn_ready rhs_mm rhs_ready u_mm u_ready st_mm st_ready y_mm y_ready "
                  "w_hi w_lo dn_hi dn_lo h_raw h_hi act_raw act_hi xm_raw xm_hi o_raw o_hi o_ready "
                  "gn_mu gn_c gn_sq gn_var gn_std gn_ready kk_raw v_final bonus_ready mid_ready x_init").split():
            sems[n] = ctx.enter_context(nc.semaphore(n))
        a_loaded = [ctx.enter_context(nc.semaphore(f"a_loaded{i}")) for i in range(4)]
        d_loaded = [ctx.enter_context(nc.semaphore(f"d_loaded{i}")) for i in range(2)]
        s = sems
        N_CONST = 2

        block = ctx.enter_context(nc.Block())

        def zm_(h):
            return planes[:, 0, (h % 4) * 512:(h % 4) * 512 + 384]

        def ln_(h):
            return planes[:, 2, (h % 2) * 512:(h % 2) * 512 + 384]

        def lg_(h):
            return planes[:, 2, 1024 + (h % 2) * 512:1024 + (h % 2) * 512 + 384]

        def plane(j):
            return planes[:, j, :].rearrange("p (k t) -> p k t", k=KT)

        def norm_bank(m):
            return B[2] if m and plan[m - 1]["kind"] != "ffn" else B[6]

        CC = NT
        kk_, em, kb, bb, gate, bonus = plane(0), plane(3), plane(4), plane(5), plane(6), plane(7)
        kq = planes[:, 1:3, :].rearrange("p a (k c q t) -> p (a k) c q t", k=KT // 2, c=CC, q=2)
        sc = [qkv[:, 8 * c:8 * c + 8, :].rearrange("p a b -> p (a b)").rearrange("p (i n) -> p i n", i=4)
              for c in range(CC)]
        inv = [qkv[:, 16:24, :].rearrange("p a b -> p (a b)").rearrange("p (m i n) -> p m i n", m=4, i=4),
               planes[:, 3, :].rearrange("p (m i n) -> p m i n", m=4, i=4)]
        X, XT, Q, LT = range(4)
        sqf = sq[:, :, :].rearrange("p a b -> p (a b)")

        def lane(t, n):
            return t[:, n, :] if isinstance(n, int) else t[:, ds(n, 1), :]

        def heads_of(g):
            return [(i, 4 * g + i, 2 * g + i // 2, HD * (i % 2)) for i in range(4)]

        def four(name):
            a, w = TAB[name]
            return tab[:, a:a + w].unsqueeze(1).broadcast_to([P, 4, P])

        def two(name):
            a, w = TAB[name]
            return tab[:, a:a + w].unsqueeze(1).broadcast_to([P, 2, P])

        def rwkv_pe(pe, L, product, project, transpose_v, out_proj):
            mm, u, r = nc.tensor.matmul, L["u"], L["rw"]
            for j in range(3):
                pe.wait_ge(s["xm_ready"], 48 * r + 8 * (j + 1))
                project(L, 8 * j, 8, x_split[j])

            def loaded(n):
                pe.wait_ge(a_loaded[(u + n) % 4], 16 * ((u + n) // 4 + 1))
                return ring_a[:, (u + n) % 4, :]

            def low(n, dst, m):
                pe.wait_ge(s["w_lo"], L["us"] + n + 1)
                return product(dst[:, 0:S], w_split[:, (u + n) % 4, :, :], x_split[m])
            low(24, B[2], 2)
            pe.wait_ge(s["xm_ready"], 48 * r + 32)
            low(24, B[3], 0).then_inc(s["a_used"], 1)
            low(25, B[1], 0).then_inc(s["a_used"], 1)
            pe.wait_ge(s["xm_ready"], 48 * r + 40)
            low(26, B[0], 1)
            pe.wait_ge(s["xm_ready"], 48 * r + 48)
            pe.wait_ge(s["proj_evac"], L["proj"] + 24)
            low(26, B[4], 2).then_inc(s["a_used"], 1)
            w2a2, g2a, g2v2 = loaded(27), loaded(28), loaded(29)
            pe.wait_ge(s["lora1_ready"], r + 1)
            for n in range(KT):
                p, c = n % 2, slice(n * P, (n + 1) * P)
                if n >= 2:
                    pe.wait_ge(s["lora2_ready"], 8 * r + n - 1)
                mm(B[4 + 2 * p][:, 0:S], w2a2[0:64, c], work[0:64, 4, :], start=True, stop=True)
                mm(B[5 + 2 * p][:, 0:S], w2a2[64:128, c], work[64:128, 4, :], start=True, stop=True)
                mm(B[p][:, 0:S], g2a[:, c], work[:, 5, :], start=True, stop=False)
                last = mm(B[p][:, 0:S], g2v2[0:32, c], work[0:32, 6, :], start=False, stop=True)
                if L["idx"]:
                    last = mm(B[2 + p][:, 0:S], g2v2[32:64, c], work[32:64, 6, :], start=True, stop=True)
                last.then_inc(s["lora2_mm"], 1)
            pe.wait_ge(s["lora2_mm"], 8 * r + 8)
            pe.sem_inc(s["a_used"], 3)
            pe.wait_ge(s["lora2_ready"], 8 * r + 8)
            for n in range(KT):
                pe.wait_ge(s["kk_sq"], 8 * r + n + 1)
                if n >= 4:
                    pe.wait_ge(s["kk_std"], 8 * r + n - 3)
                mm(B[n % 4][:, 0:S], T("head_ones"), sq[:, n, :], start=True, stop=True).then_inc(s["kk_sum"], 1)
            for n in range(KT):
                pe.wait_ge(s["rk_ready"], 8 * r + n + 1)
                if n >= 4:
                    pe.wait_ge(s["bonus_ready"], 8 * r + n - 3)
                mm(B[4 + n % 4][:, 0:S], T("head_ones"), hT[:, n, :], start=True, stop=True)\
                    .then_inc(s["rk_sum"], 1)
            pe.wait_ge(s["v_final"], 8 * r + 8)
            pe.wait_ge(s["kk_std"], 8 * r + 8)
            transpose_v(L)
            pe.wait_ge(s["keys_ready"], 8 * r + 8)
            pe.wait_ge(s["bonus_ready"], 8 * r + 8)
            for g in range(4):
                if g >= 2:
                    pe.wait_ge(s["kt_ready"], 4 * r + g - 1)
                src = kb if g < 2 else bb
                for i in range(4):
                    last = nc.tensor.transpose(B[2 + g % 2][:, i * P:(i + 1) * P], src[:, 4 * (g % 2) + i, 0:P],
                                               T("ident"))
                last.then_inc(s["kt_mm"], 1)
            pe.wait_ge(s["vtok_ready"], L["vt"] + 4)
            pe.wait_ge(s["kt_ready"], 4 * r + 4)

            for g in range(4):
                G = 4 * r + g
                if g:
                    pe.wait_ge(s["y_ready"], 2 * G)
                for c in range(CC):
                    cs = slice(c * P, (c + 1) * P)
                    for i, h, n, po in heads_of(g):
                        if c:
                            pe.wait_ge(s["score_ready"], 8 * G + i + 1)
                        q = kq[po:po + HD, n, c, :, :].rearrange("p q t -> p (q t)")
                        mm(B[i][:, 0:S], kb[po:po + HD, n, cs], q, start=True, stop=True)
                        mm(B[i][:, S:2 * S], bb[po:po + HD, n, cs], q, start=True, stop=True)
                        o = (i // 2) * P
                        mm(B[6 - 2 * c + i % 2][:, o:o + P], kq[po:po + HD, n, c, 0, :], bb[po:po + HD, n, cs],
                           start=True, stop=True).then_inc(s["score_mm"], 1)
                for lv in range(1, 7):
                    for c in range(CC):
                        if lv == 1:
                            pe.wait_ge(s["inv_init"], 2 * G + c + 1)
                            if c == 0:
                                pe.wait_ge(s["score_ready"], 8 * G + 8)
                        else:
                            pe.wait_ge(s["xn_ready"], (6 * G + lv - 2) * 2 + c + 1)
                        for i in range(4):
                            last = mm(B[c][:, i * P:(i + 1) * P], inv[c][:, LT, i, :], inv[c][:, X, i, :],
                                      start=True, stop=True)
                        last.then_inc(s["lx_mm"], 1)
                    for c in range(CC):
                        pe.wait_ge(s["q_ready"], (6 * G + lv - 1) * 2 + c + 1)
                        if lv < 6:
                            for i in range(4):
                                mm(B[2 + c][:, i * P:(i + 1) * P], inv[c][:, XT, i, :], inv[c][:, Q, i, :],
                                   start=True, stop=True)
                        for i in range(4):
                            last = mm(B[4 + c][:, i * P:(i + 1) * P], inv[c][:, Q, i, :], inv[c][:, XT, i, :],
                                      start=True, stop=True)
                        last.then_inc(s["xn_mm"], 1)

                def right(c):
                    for i, h, n, po in heads_of(g):
                        b = B[6 + i % 2][:, c * P + (i // 2) * HD:c * P + (i // 2 + 1) * HD]
                        last = mm(b, sc[c][:, i, 0:P], vtok[:, c, h * HD:(h + 1) * HD], start=True, stop=(c == 0))
                        if c:
                            o = (i // 2) * HD
                            last = mm(b, kq[po:po + HD, n, 1, 0, :], work[po:po + HD, 4, o:o + HD],
                                      start=False, stop=True)
                    last.then_inc(s["rhs_mm"], 1)

                def solve(c):
                    pe.wait_ge(s["xn_ready"], (6 * G + 5) * 2 + c + 1)
                    pe.wait_ge(s["rhs_ready"], 2 * G + c + 1)
                    for i, h, n, po in heads_of(g):
                        o = (i % 2) * P + (i // 2) * HD
                        last = mm(B[c][:, i * HD:(i + 1) * HD], inv[c][:, XT, i, :], work[:, c, o:o + HD],
                                  start=True, stop=True)
                    last.then_inc(s["u_mm"], 1)

                def outputs(c):
                    pe.wait_ge(s["u_ready"], 2 * G + c + 1)
                    for i, h, n, po in heads_of(g):
                        o = c * S + (i // 2) * P
                        b = B[2 + i % 2][po:po + HD, o:o + P]
                        mm(b, vtok[:, c, h * HD:(h + 1) * HD], sc[c][:, i, P:2 * P], start=True, stop=False)
                        last = mm(b, work[:, 2 + c, i * HD:(i + 1) * HD], sc[c][:, i, 3 * P:4 * P],
                                  start=False, stop=(c == 0))
                        if c:
                            last = mm(b, work[po:po + HD, 4, (i // 2) * HD:(i // 2 + 1) * HD],
                                      kq[po:po + HD, n, 1, 1, :], start=False, stop=True)
                    last.then_inc(s["y_mm"], 1)

                right(0)
                solve(0)
                pe.wait_ge(s["u_ready"], 2 * G + 1)
                for i, h, n, po in heads_of(g):
                    b = B[4][po:po + HD, (i // 2) * HD:(i // 2 + 1) * HD]
                    mm(b, sqf[:, n * P + po:n * P + po + HD], vtok[:, 0, h * HD:(h + 1) * HD],
                       start=True, stop=False)
                    last = mm(b, sqf[:, D + n * P + po:D + n * P + po + HD],
                              work[:, 2, i * HD:(i + 1) * HD], start=False, stop=True)
                last.then_inc(s["st_mm"], 1)
                outputs(0)
                pe.wait_ge(s["st_ready"], G + 1)
                pe.wait_ge(s["rhs_ready"], 2 * G + 1)
                right(1)
                solve(1)
                pe.wait_ge(s["y_ready"], 2 * G + 1)
                outputs(1)

            pe.wait_ge(s["y_ready"], 8 * r + 8)
            for n in range(KT + 2):
                if n < KT:
                    if n >= 2:
                        pe.wait_ge(s["gn_c"], 8 * r + n - 1)
                    mm(B[n % 2][:, 0:S], T("head_mean"), oT[:, n, :], start=True, stop=True)\
                        .then_inc(s["gn_mu"], 1)
                if n >= 2:
                    m = n - 2
                    pe.wait_ge(s["gn_sq"], 8 * r + m + 1)
                    if m >= 2:
                        pe.wait_ge(s["gn_std"], 8 * r + m - 1)
                    mm(B[2 + m % 2][:, 0:S], T("head_mean"), sq[:, m, :], start=True, stop=True)\
                        .then_inc(s["gn_var"], 1)
            out_proj(L, 30, rw_o_split, skipped=3)

        def rwkv_act(act, L, A, evac, xm_hi, out_split):
            u, r, j = L["u"], L["rw"], L["idx"]
            for k in range(KT):
                xm_hi(L, 0, k // 4, k % 4)
            for group in range(3):
                evac(L, 8 * group, 8, mixed=group + 1)
            for k in range(2 * KT):
                xm_hi(L, 4 + k // KT, k % KT // 4, k % 4)
            act.wait_ge(s["a_used"], u + 27)
            A(work[0:64, 4, :], B[0][0:64, 0:S], ACT.Tanh)
            A(work[64:128, 4, :], B[4][64:128, 0:S], ACT.Copy)
            A(work[:, 5, :], B[1][:, 0:S], ACT.Sigmoid)
            A(work[0:32, 6, :], B[3][0:32, 0:S], ACT.Sigmoid)
            A(work[32:64, 6, :], B[2][32:64, 0:S], ACT.Copy).then_inc(s["lora1_ready"], 1)
            for n in range(KT):
                p = n % 2
                act.wait_ge(s["lora2_mm"], 8 * r + n + 1)
                if j:
                    A(bonus[:, n, :], B[2 + p][:, 0:S], ACT.Sigmoid, bias=V("v0_", n))
                A(kb[:, n, :], B[4 + 2 * p][:, 0:S], ACT.Sigmoid, bias=V(f"w0_{j}", n))
                A(bb[:, n, :], B[5 + 2 * p][:, 0:S], ACT.Sigmoid, bias=V(f"a0_{j}", n))
                A(gate[:, n, :], B[p][:, 0:S], ACT.Copy).then_inc(s["lora2_ready"], 1)
            for n in range(KT):
                act.wait_ge(s["kk_raw"], 8 * r + n + 1)
                A(sq[:, n, :], kk_[:, n, :], ACT.Square).then_inc(s["kk_sq"], 1)
            for n in range(KT):
                act.wait_ge(s["kk_sum"], 8 * r + n + 1)
                if n >= 2:
                    act.wait_ge(s["keys_ready"], 8 * r + n - 1)
                A(work[:, 2 + p_of(n), :], B[n % 4][:, 0:S], ACT.Sqrt).then_inc(s["kk_std"], 1)
                act.wait_ge(s["mid_ready"], r + 1)
                if n == 0:
                    A(dec[:, :, :, 0:1].rearrange("p k c o -> p (k c o)"), small[:, 0:16], ACT.Exp)
                    A(small[:, 32:40], small[:, 1:16:2], ACT.Exp, scale=-1.0)
                for c in range(CC):
                    cs = slice(c * P, (c + 1) * P)
                    A(dec[:, n, c, 1:P + 1], oT[:, n, cs], ACT.Exp, scale=-KAPPA,
                      bias=small[:, 2 * n + c:2 * n + c + 1])
                    last = A(em[:, n, cs], oT[:, n, cs], ACT.Exp, scale=KAPPA,
                             bias=small[:, 16 + 2 * n + c:17 + 2 * n + c])
                last.then_inc(s["dec_ready"], 1)
            for g in range(4):
                act.wait_ge(s["kt_mm"], 4 * r + g + 1)
                A(sqf[:, g * 512:(g + 1) * 512], B[2 + g % 2][:, :], ACT.Copy).then_inc(s["kt_ready"], 1)
            act.wait_ge(s["dec_ready"], 8 * r + 8)
            for g in range(4):
                G = 4 * r + g
                for lv in range(1, 7):
                    for c in range(CC):
                        act.wait_ge(s["xn_mm"], (6 * G + lv - 1) * 2 + c + 1)
                        if lv < 6:
                            A(inv[c][:, X, :, :].rearrange("p i n -> p (i n)"), B[2 + c][:, :], ACT.Copy)
                        A(inv[c][:, XT, :, :].rearrange("p i n -> p (i n)"), B[4 + c][:, :], ACT.Copy)\
                            .then_inc(s["xn_ready"], 1)

                def copy_rhs(c):
                    act.wait_ge(s["rhs_mm"], 2 * G + c + 1)
                    A(work[:, c, 0:P], B[6][:, c * P:(c + 1) * P], ACT.Copy)
                    A(work[:, c, P:2 * P], B[7][:, c * P:(c + 1) * P], ACT.Copy).then_inc(s["rhs_ready"], 1)

                def copy_u(c):
                    act.wait_ge(s["u_mm"], 2 * G + c + 1)
                    A(work[:, 2 + c, :], B[c][:, 0:S], ACT.Copy, scale=-1.0).then_inc(s["u_ready"], 1)

                def copy_y(c):
                    act.wait_ge(s["y_mm"], 2 * G + c + 1)
                    for p in range(2):
                        po = HD * p
                        last = A(oT[po:po + HD, 2 * g:2 * g + 2, c * P:(c + 1) * P],
                                 B[2 + p][po:po + HD, c * S:(c + 1) * S].rearrange("p (a b) -> p a b", a=2),
                                 ACT.Copy)
                    last.then_inc(s["y_ready"], 1)
                copy_rhs(0)
                copy_u(0)
                act.wait_ge(s["st_mm"], G + 1)
                act.wait_ge(s["factor_ready"], r + 1)
                for t in range(2):
                    last = A(work[:, 4, t * HD:(t + 1) * HD], B[4][:, t * HD:(t + 1) * HD], ACT.Copy,
                             scale=small[:, 40 + 2 * g + t:41 + 2 * g + t])
                last.then_inc(s["st_ready"], 1)
                copy_y(0)
                copy_rhs(1)
                copy_u(1)
                copy_y(1)
            for n in range(KT + 1):
                if n < KT:
                    act.wait_ge(s["gn_c"], 8 * r + n + 1)
                    A(sq[:, n, :], oT[:, n, :], ACT.Square).then_inc(s["gn_sq"], 1)
                if n >= 1:
                    m = n - 1
                    act.wait_ge(s["gn_var"], 8 * r + m + 1)
                    if m >= 2:
                        act.wait_ge(s["gn_ready"], 8 * r + m - 1)
                    A(work[:, m % 2, :], B[2 + m % 2][:, 0:S], ACT.Sqrt, bias=T("gn_eps")).then_inc(s["gn_std"], 1)
            out_split(L, 30, rw_o_split, lambda n: act.wait_ge(s["gn_ready"], 8 * r + n + 1))

        def p_of(n):
            return n % 2

        def rwkv_dve(dve, L, v, step, lo, tokens_v, out_split, add_out):
            r, j, j_ = L["rw"], L["idx"], L["idx"]
            dve.wait_ge(s["h_raw"], 8 * (L["part"] + 1))
            step.did(v.tensor_tensor(sq[:, :, 1:S], hT[:, :, 0:S - 1], hT[:, :, 1:S], ALU.subtract))
            step.did(v.tensor_scalar(sq[:, :, 0:1], hT[:, :, 0:1], -1.0, None, ALU.mult))
            step.settle()
            order = (0, 1, 2, 5, 3, 4)

            def mixed(group, i, j):
                k = i * 4 + j
                a = VEC[f"mix{order[group]}_{j_}"][0]
                num = isinstance(k, int)
                if r or group or not num or k >= 4:
                    dve.wait_ge(s["xm_ready"], i * 4 + (48 * r + 8 * group + j - 3))
                v.scalar_tensor_tensor(out=work[:, j, :], in0=sq[:, k, :] if num else sq[:, ds(k, 1), :],
                                       scalar=vec[:, a + k:a + k + 1] if num else vec[:, ds(k + a, 1)],
                                       in1=hT[:, k, :] if num else hT[:, ds(k, 1), :],
                                       op0=ALU.mult, op1=ALU.add).then_inc(s["xm_raw"], 1)

            def mixed_low(group, i, j):
                k = i * 4 + j
                t = x_split[group % 3]
                dve.wait_ge(s["xm_hi"], i * 4 + (48 * r + 8 * group + j + 1))
                hi_, lo_ = [t[:, q, k, :] if isinstance(k, int) else t[:, q, ds(k, 1), :] for q in range(2)]
                v.tensor_tensor(lo_, work[:, j, :], hi_.bitcast(f32), ALU.subtract).then_inc(s["xm_ready"], 1)

            for k in range(KT + 1):
                if k < KT:
                    mixed(0, k // 4, k % 4)
                if k:
                    mixed_low(0, (k - 1) // 4, (k - 1) % 4)
            for group in range(1, 4):
                with dve.Fori(0, 2) as i:
                    for q in range(4):
                        mixed(group, i, q)
                        lo(L, 8 * (group - 1) + q + AHEAD, i)
                        mixed_low(group, i, q)
            for t in range(2 * KT + 1):
                if t < 2 * KT:
                    mixed(4 + t // KT, t % KT // 4, t % 4)
                if t:
                    mixed_low(4 + (t - 1) // KT, (t - 1) % KT // 4, (t - 1) % 4)
            dve.wait_ge(s["xm_ready"], 48 * r + 48)
            dve.wait_ge(s["proj_evac"], L["proj"] + 24)
            for n in range(KT):
                K, R, Vt, t = qkv[:, 8 + n, :], qkv[:, n, :], qkv[:, 16 + n, :], work[:, n % 2, :]
                dve.wait_ge(s["lora2_ready"], 8 * r + n + 1)
                if j == 0:
                    v.tensor_copy(v_first[:, n, :], Vt).then_inc(s["v_final"], 1)
                else:
                    step.did(v.tensor_tensor(work[:, 7, :], v_first[:, n, :], Vt, ALU.subtract))
                    step.settle()
                    step.did(v.tensor_tensor(work[:, 7, :], work[:, 7, :], bonus[:, n, :], ALU.mult))
                    step.settle()
                    v.tensor_tensor(Vt, Vt, work[:, 7, :], ALU.add).then_inc(s["v_final"], 1)
                v.tensor_scalar(kk_[:, n, :], K, V(f"k_k_{j}", n), None, ALU.mult).then_inc(s["kk_raw"], 1)
                step.did(v.tensor_scalar(t, bb[:, n, :], 1.0, V(f"k_a_{j}", n), ALU.subtract, ALU.mult))
                dve.wait_ge(s["kk_raw"], 8 * r + n + 1)
                step.settle()
                step.did(v.scalar_tensor_tensor(out=K, in0=t, scalar=1.0, in1=K, op0=ALU.add, op1=ALU.mult))
                step.did(v.tensor_tensor_scan(oT[:, n, :], T("scan_keep"), kb[:, n, :], 0.0, ALU.mult, ALU.add))
                step.settle()
                v.scalar_tensor_tensor(out=hT[:, n, :], in0=R, scalar=V(f"r_k_{j}", n), in1=K,
                                       op0=ALU.mult, op1=ALU.mult).then_inc(s["rk_ready"], 1)
                dve.wait_ge(s["v_final"], 8 * r + n + 1)
            mids = oT[:, :, :].rearrange("p k (c t) -> p (k c) t", c=CC)[:, :, P // 2 - 1:P // 2]
            step.did(v.tensor_scalar(small[:, 0:16].unsqueeze(2), mids, KAPPA, None, ALU.mult))
            v.tensor_scalar(small[:, 16:32].unsqueeze(2), mids, -KAPPA, None, ALU.mult).then_inc(s["mid_ready"], 1)
            for n in range(KT):
                std = work[:, 2 + n % 2, :]
                dve.wait_ge(s["kk_std"], 8 * r + n + 1)
                step.did(v.tensor_scalar(std, std, 1e-12, None, ALU.max))
                step.settle()
                step.did(v.reciprocal(std, std))
                step.settle()
                step.did(v.tensor_tensor(kk_[:, n, :], kk_[:, n, :], std, ALU.mult))
                step.settle()
                step.did(v.tensor_tensor(bb[:, n, :], kk_[:, n, :], bb[:, n, :], ALU.mult))
                dve.wait_ge(s["dec_ready"], 8 * r + n + 1)

                def chunks(t):
                    return t.rearrange("p (c t) -> p c t", c=CC)
                step.did(v.tensor_tensor(kq[:, n, :, 0, :], chunks(kk_[:, n, :]), dec[:, n, :, 0:P], ALU.mult))
                step.did(v.tensor_tensor(kq[:, n, :, 1, :], chunks(qkv[:, n, :]), dec[:, n, :, 1:P + 1], ALU.mult))
                step.did(v.tensor_tensor(kb[:, n, :], qkv[:, 8 + n, :], em[:, n, :], ALU.mult))
                step.settle()
                v.tensor_tensor(bb[:, n, :], bb[:, n, :], em[:, n, :], ALU.mult).then_inc(s["keys_ready"], 1)
            v.tensor_tensor(small[:, 40:48].unsqueeze(2), small[:, 32:40].unsqueeze(2), dec[:, :, 0, P:P + 1],
                            ALU.mult).then_inc(s["factor_ready"], 1)
            for n in range(KT):
                dve.wait_ge(s["rk_sum"], 8 * r + n + 1)
                v.tensor_tensor(bonus[:, n, :], B[4 + n % 4][:, 0:S], qkv[:, 16 + n, :], ALU.mult)\
                    .then_inc(s["bonus_ready"], 1)
            tokens_v(L)
            dve.wait_ge(s["keys_ready"], 8 * r + 8)
            dve.wait_ge(s["bonus_ready"], 8 * r + 8)
            for g in range(4):
                G = 4 * r + g
                if g:
                    dve.wait_ge(s["y_mm"], 2 * G)
                for c in range(CC):
                    for i in range(4):
                        dve.wait_ge(s["score_mm"], 8 * G + 4 * c + i + 1)
                        v.tensor_tensor(sc[c][:, i, :], B[i][:, :], T("rw_mask"), ALU.mult)\
                            .then_inc(s["score_ready"], 1)
                    for p in range(2):
                        v.tensor_tensor(inv[c][:, X, p::2, :],
                                        B[6 - 2 * c + p][:, 0:S].rearrange("p (a b) -> p a b", a=2),
                                        two("pair_neg"), ALU.mult).then_inc(s["x_init"], 1)
                for lv in range(1, 7):
                    for c in range(CC):
                        dve.wait_ge(s["lx_mm"], (6 * G + lv - 1) * 2 + c + 1)
                        v.tensor_tensor(inv[c][:, Q, :, :], B[c][:, :].rearrange("p (i n) -> p i n", i=4),
                                        four(f"level{lv}"), ALU.mult).then_inc(s["q_ready"], 1)
            for n in range(KT + 2):
                if n < KT:
                    dve.wait_ge(s["gn_mu"], 8 * r + n + 1)
                    v.tensor_tensor(oT[:, n, :], oT[:, n, :], B[n % 2][:, 0:S], ALU.subtract)\
                        .then_inc(s["gn_c"], 1)
                if n >= 2:
                    m = n - 2
                    y, sd = oT[:, m, :], work[:, m % 2, :]
                    dve.wait_ge(s["gn_std"], 8 * r + m + 1)
                    step.did(v.reciprocal(sd, sd))
                    step.settle()
                    step.did(v.tensor_tensor(y, y, sd, ALU.mult))
                    step.settle()
                    step.did(v.tensor_scalar(y, y, V(f"ln_w_{j}", m), V(f"ln_b_{j}", m), ALU.mult, ALU.add))
                    step.settle()
                    step.did(v.tensor_tensor(y, y, bonus[:, m, :], ALU.add))
                    step.settle()
                    v.tensor_tensor(y, y, gate[:, m, :], ALU.mult).then_inc(s["gn_ready"], 1)
            out_split(L, 30, rw_o_split, skipped=3)
            add_out(L, 30, skipped=3)

        def rwkv_pool(pool, L, pstep):
            r = L["rw"]
            g_ = nc.gpsimd
            for g in range(4):
                G = 4 * r + g
                for c in range(CC):
                    m = inv[c]
                    pool.wait_ge(s["score_ready"], 8 * G + 4 * c + 4)
                    a2t = sc[c][:, :, 2 * P:3 * P]
                    pstep.did(g_.tensor_tensor(m[:, XT, :, :], a2t, four("pair_neg_t"), ALU.mult))
                    pstep.did(g_.tensor_tensor(m[:, LT, :, :], a2t, four("ident"), ALU.add))
                    pstep.settle()
                    pstep.did(g_.tensor_tensor(m[:, XT, :, :], m[:, XT, :, :], four("ident"), ALU.add))
                    pool.wait_ge(s["x_init"], 4 * G + 2 * c + 2)
                    pstep.settle()
                    g_.tensor_tensor(m[:, X, :, :], m[:, X, :, :], four("ident"), ALU.add)\
                        .then_inc(s["inv_init"], 1)

        @block.sync
        def _(sp):
            sp.dma_start(xT[:, :, :], x_in).then_inc(s["x_loaded"], 16)
            sp.dma_start(tab[:, :], tab_in).then_inc(s["const_loaded"], 16)
            sp.dma_start(vec[:, :], vec_in).then_inc(s["const_loaded"], 16)

            def load(L, n, i=0):
                u, back = L["u"] + n, n - 4
                if back >= 0 and L["kind"] == "rwkv" and back in (27, 28, 29):
                    sp.wait_ge(s["a_used"], u - 3)
                elif u >= 4 or not isinstance(i, int):
                    skipped = 3 if L["kind"] == "rwkv" and back >= 30 else 0
                    sp.wait_ge(s["w_lo"], i * 4 + (L["us"] + back - skipped + 1))
                sp.dma_start(ring_a[:, u % 4, :], wa[i * 4 + u, :, :] if not isinstance(i, int) else wa[u, :, :])\
                    .then_inc(a_loaded[u % 4], 16)

            for L in plan:
                n_units_here = UNITS[L["kind"]]
                if L["kind"] == "ffn":
                    def two_tiles(i, first):
                        for j in range(4):
                            load(L, j, i)
                        for j in range(2):
                            if not (first and L["d"] + j < 2):
                                sp.wait_ge(s["dn_lo"], i * 2 + (L["d"] + j - 1))
                            sp.dma_start(ring_d[:, j, :], wd[i * 2 + (L["d"] + j), :, :])\
                                .then_inc(d_loaded[j], 16)
                    two_tiles(0, True)
                    with sp.Fori(1, FT // 2) as i:
                        two_tiles(i, False)
                else:
                    looped = 24
                    for n in range(4):
                        load(L, n)
                    with sp.Fori(0, (looped - 4) // 4) as i:
                        for j in range(4):
                            load(L, 4 + j, i)
                    for n in range(looped, n_units_here):
                        load(L, n)
            sp.wait_ge(s["x_added"], 8 * (PARTS + 1))
            sp.dma_start(out, xT[:, :, :]).then_inc(s["stored"], 16)
            sp.wait_ge(s["stored"], 16)

        @block.tensor
        def _(pe):
            mm = nc.tensor.matmul
            pe.wait_ge(s["const_loaded"], 16 * N_CONST)

            def norm(m):
                for k in range(KT):
                    pe.wait_ge(s["sq_ready"], 8 * m + k + 1)
                    last = mm(norm_bank(m)[:, 0:S], T("ones"), sq[:, k, :], start=(k == 0), stop=(k == KT - 1))
                last.then_inc(s["ssum_ready"], 1)

            def product(dst, w, x, first=True, last_=True):
                for k in range(KT):
                    ks = slice(k * P, (k + 1) * P)
                    mm(dst, w[:, 0, ks], x[:, 0, k, :], start=(k == 0), stop=False)
                    mm(dst, w[:, 0, ks], x[:, 1, k, :], start=False, stop=False)
                    last = mm(dst, w[:, 1, ks], x[:, 0, k, :], start=False, stop=(k == KT - 1))
                return last

            def unit(L, n, i, dst, x, skipped=0):
                pe.wait_ge(s["w_lo"], i * 4 + (L["us"] + n - skipped + 1))
                product(dst, w_split[:, (L["u"] + n) % 4, :, :], x).then_inc(s["a_used"], 1)

            def ffn(L):
                f, d = L["d"] // FT, L["d"]

                def gate_up(i, q):
                    for g in range(2):
                        unit(L, 2 * q + g, i, B[4 + q][:, g * S:(g + 1) * S], h_split)

                def down(i, q, first=False, final=False):
                    pe.wait_ge(s["act_ready"], i * 2 + (FT * f + q + 1))
                    pe.wait_ge(s["dn_lo"], i * 2 + (d + q + 1))
                    for m in range(KT):
                        o, ms = B[m // 2][:, (m % 2) * S:(m % 2 + 1) * S], slice(m * P, (m + 1) * P)
                        mm(o, d_split[:, q, 0, ms], act_split[:, q, 0, :], start=(first and m % 2 == 0),
                           stop=False, skip_group_check=True)
                        mm(o, d_split[:, q, 0, ms], act_split[:, q, 1, :], start=False,
                           stop=False, skip_group_check=True)
                        last = mm(o, d_split[:, q, 1, ms], act_split[:, q, 0, :], start=False,
                                  stop=final, skip_group_check=True)
                    last.then_inc(s["d_used"], 1)

                pe.wait_ge(s["h_ready"], 8 * (L["hs"] + 1))
                gate_up(0, 0)
                gate_up(0, 1)
                down(0, 0, first=True)
                with pe.Fori(1, FT // 2) as i:
                    gate_up(i, 0)
                    down(i - 1, 1)
                    gate_up(i, 1)
                    down(i, 0)
                down(FT // 2 - 1, 1, final=True)

            def project(L, first, count, x):
                with pe.Fori(0, count // 4) as i:
                    for j in range(4):
                        pe.wait_ge(s["proj_evac"], i * 4 + (L["proj"] + first + j - 3))
                        unit(L, first + j, i, B[4 + (first + j) % 4][:, 0:S], x)

            def project_one(L, n):
                pe.wait_ge(s["proj_evac"], L["proj"] + n - 3)
                unit(L, n, 0, B[4 + n % 4][:, 0:S], h_split)

            def transpose_v(L, dst_done=True):
                for g in range(4):
                    if g >= 2:
                        pe.wait_ge(s["vtok_ready"], L["vt"] + g - 1)
                    for i in range(4):
                        last = nc.tensor.transpose(B[g % 2][:, i * P:(i + 1) * P],
                                                   qkv[:, 16 + 4 * (g % 2) + i, (g // 2) * P:(g // 2 + 1) * P],
                                                   T("ident"))
                    last.then_inc(s["vtok_done"], 1)

            def out_proj(L, first, x, skipped=0):
                pe.wait_ge(s["proj_evac"], L["proj"] + min(first, PROJ[L["kind"]]))
                pe.wait_ge(s["o_ready"], 8 * (L["mixers"] + 1))
                for n in range(KT):
                    if n >= 4:
                        pe.wait_ge(s["x_added"], 8 * (L["part"] + 1) + n - 3)
                    unit(L, first + n, 0, B[4 + n % 4][:, 0:S], x, skipped)

            def stick(L):
                pe.wait_ge(s["h_ready"], 8 * (L["hs"] + 1))
                project(L, 0, 24, h_split)
                pe.wait_ge(s["proj_evac"], L["proj"] + 24)
                transpose_v(L)
                pe.wait_ge(s["vtok_ready"], L["vt"] + 4)

                def z(h):
                    po, t = HD * (h % 2), h // 2
                    if h >= 2:
                        pe.wait_ge(s["zm_ready"], h - 1)
                    mm(B[h % 2][:, 0:S], qkv[po:po + HD, 8 + t, 0:P], qkv[po:po + HD, t, :], start=True, stop=True)
                    mm(B[h % 2][:, S:S + P], qkv[po:po + HD, 8 + t, P:S], qkv[po:po + HD, t, P:S],
                       start=True, stop=True).then_inc(s["z_done"], 1)

                def suffix(h):
                    pe.wait_ge(s["sp_ready"], h + 1)
                    if h >= 2:
                        pe.wait_ge(s["lg_ready"], h - 1)
                    b, sp_ = B[2 + h % 2], planes[:, 1, (h % 2) * 512:(h % 2) * 512 + 384]
                    mm(b[:, 0:S], T("tri"), sp_[:, 0:S], start=True, stop=False, skip_group_check=True)
                    mm(b[:, P:S], T("ones"), sp_[:, S:384], start=False, stop=True, skip_group_check=True)
                    mm(b[:, S:384], T("tri"), sp_[:, S:384], start=True, stop=True,
                       skip_group_check=True).then_inc(s["cum_done"], 1)

                def pv(h):
                    po, t = HD * (h % 2), h // 2
                    pe.wait_ge(s["p_ready"], h + 1)
                    if h % 2 == 0 and t >= 2:
                        pe.wait_ge(s["ot_evac"], L["pairs"] + t - 1)
                    p_, b = planes[:, 3, (h % 2) * 512:(h % 2) * 512 + 384], B[4 + t % 2]
                    mm(b[po:po + HD, 0:S], vtok[:, 0, h * HD:(h + 1) * HD], p_[:, 0:S], start=True, stop=False,
                       skip_group_check=True)
                    mm(b[po:po + HD, P:S], vtok[:, 1, h * HD:(h + 1) * HD], p_[:, S:384], start=False, stop=True,
                       skip_group_check=True).then_inc(s["pv_done"], 1)

                for t in range(NH + 3):
                    if t < NH:
                        z(t)
                    if 0 <= t - 2 < NH:
                        suffix(t - 2)
                    if 0 <= t - 3 < NH:
                        pv(t - 3)
                out_proj(L, 24, x_split[2])

            def norm_rope_mm(L, n, row, gained, rot):
                g = L["tiles"] + n
                if gained:
                    pe.wait_ge(s["nr_in"], L["heads"] + n + 1)
                else:
                    pe.wait_ge(s["proj_evac"], L["proj"] + 21)
                if n >= 2:
                    pe.wait_ge(s["qk_ready"], g - 1)
                b = B[2 + n % 2]
                if gained:
                    mm(b[:, 0:S], T("head_mean"), work[:, n % 2, :], start=True, stop=True)
                last = mm(b[:, S:2 * S], T(rot), work[:, 2 + n % 2, :] if gained else qkv[:, row, :],
                          start=True, stop=True)
                last.then_inc(s["nr_mm"], 1)

            def softmax_heads(L):
                H, O = L["heads"], L["pairs"]

                def scores(h):
                    po, t = HD * (h % 2), h // 2
                    if h >= 2:
                        pe.wait_ge(s["sm_ready"], H + h - 1)
                    for qt in range(NT):
                        last = mm(B[h % 2][:, qt * S:(qt + 1) * S], qkv[po:po + HD, t, qt * P:(qt + 1) * P],
                                  qkv[po:po + HD, 8 + t, :], start=True, stop=True)
                    last.then_inc(s["s_done"], 1)

                def turn(h):
                    pe.wait_ge(s["pn_ready"], H + h + 1)
                    if h >= 2:
                        pe.wait_ge(s["pt_ready"], H + h - 1)
                    p_ = planes[:, 0, (h % 4) * 512:(h % 4 + 1) * 512]
                    for st in range(NT):
                        for qt in range(NT):
                            last = nc.tensor.transpose(B[2 + h % 2][:, st * S + qt * P:st * S + (qt + 1) * P],
                                                       p_[:, qt * S + st * P:qt * S + (st + 1) * P], T("ident"))
                    last.then_inc(s["t_done"], 1)

                def pv(h):
                    po, t = HD * (h % 2), h // 2
                    pe.wait_ge(s["pt_ready"], H + h + 1)
                    if h % 2 == 0 and t >= 2:
                        pe.wait_ge(s["ot_evac"], O + t - 1)
                    for st in range(NT):
                        last = mm(B[4 + t % 2][po:po + HD, 0:S], vtok[:, st, h * HD:(h + 1) * HD],
                                  planes[:, 2, (h % 2) * 512 + st * S:(h % 2) * 512 + (st + 1) * S],
                                  start=(st == 0), stop=(st == NT - 1))
                    last.then_inc(s["pv_done"], 1)

                for t in range(NH + 3):
                    if t < NH:
                        scores(t)
                    if 0 <= t - 2 < NH:
                        turn(t - 2)
                    if 0 <= t - 3 < NH:
                        pv(t - 3)

            def dsa(L):
                pe.wait_ge(s["h_ready"], 8 * (L["hs"] + 1))
                project(L, 0, 20, h_split)
                project_one(L, 20)
                pe.wait_ge(s["proj_evac"], L["proj"] + 21 - 3)
                pe.wait_ge(s["w_lo"], L["us"] + 22)
                wi = w_split[:, (L["u"] + 21) % 4, :, :]
                for qt in range(NT):
                    o, qs = B[5][:, qt * 8:(qt + 1) * 8], slice(qt * P, (qt + 1) * P)
                    for k in range(KT):
                        mm(o, h_split[:, 0, k, qs], wi[:, 0, k * P:k * P + 8], start=(k == 0), stop=False)
                        mm(o, h_split[:, 0, k, qs], wi[:, 1, k * P:k * P + 8], start=False, stop=False)
                        last = mm(o, h_split[:, 1, k, qs], wi[:, 0, k * P:k * P + 8],
                                  start=False, stop=(k == KT - 1))
                last.then_inc(s["a_used"], 1)
                for j in range(8):
                    project_one(L, 22 + j)
                    for n in range(3 * j, min(3 * j + 3, 21)):
                        row = n if n < 16 else n + 8
                        norm_rope_mm(L, n, row, n < 16, "rot0")
                pe.wait_ge(s["qk_ready"], L["tiles"] + 21)
                for i in range(IDX_HEADS):
                    po, t = HD * (i % 2), 24 + i // 2
                    if i >= 2:
                        pe.wait_ge(s["idx_relu"], i - 1)
                    for qt in range(NT):
                        last = mm(B[i % 2][:, qt * S:(qt + 1) * S], qkv[po:po + HD, t, qt * P:(qt + 1) * P],
                                  qkv[po:po + HD, 28, :], start=True, stop=True)
                    last.then_inc(s["idx_mm"], 1)
                pe.wait_ge(s["idx_relu"], IDX_HEADS)
                pe.wait_ge(s["proj_evac"], L["proj"] + 30)
                transpose_v(L)
                pe.wait_ge(s["vtok_ready"], L["vt"] + 4)
                softmax_heads(L)
                out_proj(L, 30, x_split[2])

            ROT = [None, None, "rot1", "rot1", "rot1", "rot2", "rot2", "rot2"]

            def multi(L):
                pe.wait_ge(s["h_ready"], 8 * (L["hs"] + 1))
                project(L, 0, 16, h_split)
                for j in range(8):
                    project_one(L, 16 + j)
                    for n in (2 * j, 2 * j + 1):
                        g = L["tiles"] + n
                        pe.wait_ge(s["nr_in"], L["heads"] + n + 1)
                        if n >= 2:
                            pe.wait_ge(s["qk_ready"], g - 1)
                        b = B[2 + n % 2]
                        last = mm(b[:, 0:S], T("head_mean"), work[:, n % 2, :], start=True, stop=True)
                        if ROT[n % 8]:
                            last = mm(b[:, S:2 * S], T(ROT[n % 8]), work[:, 2 + n % 2, :], start=True, stop=True)
                        last.then_inc(s["nr_mm"], 1)
                pe.wait_ge(s["proj_evac"], L["proj"] + 24)
                pe.wait_ge(s["qk_ready"], L["tiles"] + 16)
                transpose_v(L)
                pe.wait_ge(s["vtok_ready"], L["vt"] + 4)
                softmax_heads(L)
                r = L["multis"]
                for seg, (a, b) in enumerate(SEGMENTS):
                    pe.wait_ge(s["on_sq"], 8 * r + b)
                    if seg >= 2:
                        pe.wait_ge(s["on_std"], 3 * r + seg - 1)
                    for n in range(a, b):
                        last = mm(B[6 + seg % 2][:, S:2 * S], T("ones"), sq[:, n, :], start=(n == a), stop=(n == b - 1))
                    last.then_inc(s["on_sum"], 1)
                out_proj(L, 24, x_split[2])

            for L in plan:
                norm(L["part"])
                dict(ffn=ffn, stick=stick, dsa=dsa, multi=multi, rwkv=lambda L: rwkv_pe(pe, L, product, project, transpose_v, out_proj))[L["kind"]](L)

        @block.scalar
        def _(act):
            A = nc.scalar.activation
            step = Steps(act, s["act_step"])
            act.wait_ge(s["const_loaded"], 16 * N_CONST)

            def hi(L, n, i=0, skipped=0):
                u = L["u"] + n
                act.wait_ge(a_loaded[u % 4], i * 16 + 16 * (u // 4 + 1))
                if u >= 4 or not isinstance(i, int) or i:
                    act.wait_ge(s["a_used"], i * 4 + (u - 3))
                A(w_split[:, u % 4, 0, :], ring_a[:, u % 4, :], ACT.Copy).then_inc(s["w_hi"], 1)

            def norm(L):
                m = L["part"]
                for k in range(KT):
                    act.wait_ge(s["x_added"], 8 * m + k + 1)
                    A(sq[:, k, :], xT[:, k, :], ACT.Square).then_inc(s["sq_ready"], 1)
                for n in range(2 if L["kind"] == "ffn" else AHEAD):
                    hi(L, n)
                act.wait_ge(s["ssum_ready"], m + 1)
                A(small_std, norm_bank(m)[:, 0:S], ACT.Sqrt, bias=T("eps"), scale=1.0 / D).then_inc(s["std_ready"], 1)

                if L["kind"] != "rwkv":
                    for k in range(KT):
                        act.wait_ge(s["h_raw"], 8 * m + k + 1)
                        A(h_split[:, 0, k, :], hT[:, k, :], ACT.Copy).then_inc(s["h_hi"], 1)

            small_std = work[:, 7, :]

            def ffn(L):
                f, u = L["d"] // FT, L["u"]

                def tile_pair(i, final):
                    for q in range(2):
                        if not (final and q):
                            for g in range(2):
                                n = 2 * q + g + 2
                                hi(L, n, i)
                        act.wait_ge(d_loaded[q], i * 16 + 16 * (L["d"] // 2 + 1))
                        if f or not isinstance(i, int) or i:
                            act.wait_ge(s["d_used"], i * 2 + (L["d"] + q - 1))
                        A(d_split[:, q, 0, :], ring_d[:, q, :], ACT.Copy).then_inc(s["dn_hi"], 1)
                        if L["idx"] < 4:
                            act.wait_ge(s["a_used"], i * 4 + (u + 2 * q + 2))
                            A(work[:, 2 + q, :], B[4 + q][:, 0:S], ACT.Silu).then_inc(s["silu_ready"], 1)
                        else:
                            act.wait_ge(s["conv_ready"], i * 2 + (FT * L["convs"] + q + 1))
                            A(work[:, 2 + q, :], work[:, 4 + q, :], ACT.Gelu).then_inc(s["silu_ready"], 1)
                        act.wait_ge(s["act_raw"], i * 2 + (FT * f + q + 1))
                        A(act_split[:, q, 0, :], work[:, q, :], ACT.Copy).then_inc(s["act_hi"], 1)
                tile_pair(0, False)
                with act.Fori(1, FT // 2 - 1) as i:
                    tile_pair(i, False)
                tile_pair(FT // 2 - 1, True)

            def evac(L, first, count, mixed=None):
                u, p = L["u"] + first, first

                def four_units(i):
                    for j in range(4):
                        hi(L, first + j + AHEAD, i)
                        if mixed is not None:
                            xm_hi(L, mixed, i, j)
                        act.wait_ge(s["a_used"], i * 4 + (u + j + 1))
                        A(qkv[:, ds(i * 4 + (first + j), 1), :], B[4 + j][:, 0:S], ACT.Copy)\
                            .then_inc(s["proj_evac"], 1)
                peeled = u == 0
                if peeled:
                    four_units(0)
                with act.Fori(int(peeled), count // 4) as i:
                    four_units(i)

            def xm_hi(L, group, i, j):
                act.wait_ge(s["xm_raw"], i * 4 + (48 * L["rw"] + 8 * group + j + 1))
                if group >= 3:
                    act.wait_ge(s["a_used"], L["u"] + (8, 16, 25)[group - 3])
                t = x_split[group % 3][:, 0, :, :]
                A(t[:, ds(i * 4 + j, 1), :] if not isinstance(i, int) else t[:, i * 4 + j, :], work[:, j, :],
                  ACT.Copy).then_inc(s["xm_hi"], 1)

            def o_hi(L, n, x, ready):
                ready(n)
                A(x[:, 0, n, :], oT[:, n, :], ACT.Copy).then_inc(s["o_hi"], 1)

            def out_split(L, first, x, ready):
                for n in range(KT):
                    ready(n)
                    A(x[:, 0, n, :], oT[:, n, :], ACT.Copy).then_inc(s["o_hi"], 1)
                    if n in (2, 4, 6):
                        hi(L, first + n // 2 - 1)
                for n in range(3, KT):
                    hi(L, first + n)

            def evac_one(L, n, row):
                act.wait_ge(s["a_used"], L["u"] + n + 1)
                A(qkv[:, row, :], B[4 + n % 4][:, 0:S], ACT.Copy).then_inc(s["proj_evac"], 1)

            def stick(L):
                evac(L, 0, 20)
                hi(L, 23)
                for n in range(20, 24):
                    evac_one(L, n, n)
                O = L["pairs"]

                def softplus_log(h):
                    act.wait_ge(s["zm_ready"], h + 1)
                    e = work[:, 2 * (h % 2):2 * (h % 2) + 2, :].rearrange("p a b -> p (a b)")[:, 0:384]
                    if h >= 2:
                        act.wait_ge(s["ln_ready"], h - 1)
                    step.did(A(e, zm_(h), ACT.Abs))
                    step.settle()
                    step.did(A(e, e, ACT.Exp, scale=-1.0))
                    if h >= 2:
                        act.wait_ge(s["sp_ready"], h - 1)
                    step.settle()
                    A(ln_(h), e, ACT.Ln, bias=1.0).then_inc(s["ln_ready"], 1)

                def weights(h):
                    act.wait_ge(s["lg_ready"], h + 1)
                    if h >= 2:
                        act.wait_ge(s["pv_done"], h - 1 + 2 * O)
                    A(planes[:, 3, (h % 2) * 512:(h % 2) * 512 + 384], lg_(h), ACT.Exp).then_inc(s["p_ready"], 1)

                def pair(t):
                    act.wait_ge(s["pv_done"], 2 * O + 2 * t + 2)
                    A(oT[:, t, :], B[4 + t % 2][:, 0:S], ACT.Copy).then_inc(s["ot_evac"], 1)

                for t in range(NH + 4):
                    if t < NH:
                        softplus_log(t)
                    if 0 <= t - 2 < NH:
                        weights(t - 2)
                    if t >= 4 and (t - 4) % 2 == 1:
                        pair((t - 4) // 2)
                act.wait_ge(s["ot_evac"], O + 8)
                out_split(L, 24, x_split[2], lambda n: None)

            def norm_rope_in(L, n, row, gain):
                g = L["tiles"] + n
                if gain is None:
                    return
                if n == 0:
                    act.wait_ge(s["proj_evac"], L["proj"] + 16)
                if n >= 2:
                    act.wait_ge(s["qk_ready"], g - 1)
                A(work[:, n % 2, :], qkv[:, row, :], ACT.Square)
                A(work[:, 2 + n % 2, :], qkv[:, row, :], ACT.Copy, scale=V(gain, row)).then_inc(s["nr_in"], 1)

            def norm_rope_std(L, n):
                act.wait_ge(s["nr_mm"], L["tiles"] + n + 1)
                A(work[:, 4 + n % 2, :], B[2 + n % 2][:, 0:S], ACT.Sqrt, bias=T("eps")).then_inc(s["nr_std"], 1)

            def softmax_heads(L):
                H, O = L["heads"], L["pairs"]

                def exps(h):
                    act.wait_ge(s["nmx_ready"], H + h + 1)
                    for qt in range(NT):
                        last = A(planes[:, 0, (h % 4) * 512 + qt * S:(h % 4) * 512 + (qt + 1) * S],
                                 planes[:, 1, (h % 2) * 512 + qt * S:(h % 2) * 512 + (qt + 1) * S], ACT.Exp,
                                 bias=small[:, 2 * (h % 2) + qt:2 * (h % 2) + qt + 1],
                                 accum_out=small[:, 4 + 2 * (h % 2) + qt:5 + 2 * (h % 2) + qt])
                    last.then_inc(s["e_ready"], 1)

                def copy_turned(h):
                    act.wait_ge(s["t_done"], H + h + 1)
                    if h >= 2:
                        act.wait_ge(s["pv_done"], 2 * O + h - 1)
                    A(planes[:, 2, (h % 2) * 512:(h % 2 + 1) * 512], B[2 + h % 2][:, :], ACT.Copy)\
                        .then_inc(s["pt_ready"], 1)

                def pair(t):
                    act.wait_ge(s["pv_done"], 2 * O + 2 * t + 2)
                    A(oT[:, t, :], B[4 + t % 2][:, 0:S], ACT.Copy).then_inc(s["ot_evac"], 1)

                for t in range(NH + 4):
                    if t < NH:
                        exps(t)
                    if 0 <= t - 2 < NH:
                        copy_turned(t - 2)
                    if t >= 4 and (t - 4) % 2 == 1:
                        pair((t - 4) // 2)

            def dsa(L):
                evac(L, 0, 16)
                for n in range(16, 20):
                    hi(L, n + AHEAD)
                    evac_one(L, n, n + 8)
                hi(L, 20 + AHEAD)
                evac_one(L, 20, 28)
                hi(L, 21 + AHEAD)
                act.wait_ge(s["a_used"], L["u"] + 22)
                A(small[:, 16:32], B[5][:, 0:16], ACT.Copy,
                  scale=IDX_HEADS ** -0.5 * HD ** -0.5).then_inc(s["proj_evac"], 1)
                for j in range(8):
                    if 22 + j + AHEAD < 30:
                        hi(L, 22 + j + AHEAD)
                    tiles = range(3 * j, min(3 * j + 3, 21))
                    for n in tiles:
                        norm_rope_in(L, n, n, "gain0" if n < 16 else None)
                        if n == 3 * j + 1:
                            evac_one(L, 22 + j, 16 + j)
                        if n < 16:
                            norm_rope_std(L, n)
                    if not len(tiles) > 1:
                        evac_one(L, 22 + j, 16 + j)
                for i in range(IDX_HEADS):
                    act.wait_ge(s["idx_mm"], i + 1)
                    if i >= 2:
                        act.wait_ge(s["idx_added"], i - 1)
                    A(planes[:, 1, (i % 2) * 512:(i % 2 + 1) * 512], B[i % 2][:, :], ACT.Relu)\
                        .then_inc(s["idx_relu"], 1)
                softmax_heads(L)
                act.wait_ge(s["ot_evac"], L["pairs"] + 8)
                out_split(L, 30, x_split[2], lambda n: None)

            def multi(L):
                evac(L, 0, 16)
                gain = f"gain{1 + L['idx']}"
                for j in range(8):
                    if 16 + j + AHEAD < 24:
                        hi(L, 16 + j + AHEAD)
                    norm_rope_in(L, 2 * j, 2 * j, gain)
                    norm_rope_in(L, 2 * j + 1, 2 * j + 1, gain)
                    evac_one(L, 16 + j, 16 + j)
                    norm_rope_std(L, 2 * j)
                    norm_rope_std(L, 2 * j + 1)
                softmax_heads(L)
                r = L["multis"]
                act.wait_ge(s["ot_evac"], L["pairs"] + 8)
                for n in range(KT):
                    A(sq[:, n, :], oT[:, n, :], ACT.Square).then_inc(s["on_sq"], 1)
                for seg, (a, b) in enumerate(SEGMENTS):
                    act.wait_ge(s["on_sum"], 3 * r + seg + 1)
                    A(work[:, seg, :], B[6 + seg % 2][:, S:2 * S], ACT.Sqrt, bias=T("eps"),
                      scale=1.0 / ((b - a) * P)).then_inc(s["on_std"], 1)
                out_split(L, 24, x_split[2], lambda n: act.wait_ge(s["on_ready"], 8 * r + n + 1))

            for L in plan:
                norm(L)
                dict(ffn=ffn, stick=stick, dsa=dsa, multi=multi,
                     rwkv=lambda L: rwkv_act(act, L, A, evac, xm_hi, out_split))[L["kind"]](L)

        @block.vector
        def _(dve):
            v = nc.vector
            step = Steps(dve, s["dve_step"])
            dve.wait_ge(s["const_loaded"], 16 * N_CONST)
            dve.wait_ge(s["x_loaded"], 16)
            v.memset(small[:, 48:49], 0.0).then_inc(s["x_added"], 8)
            v.memset(small[:, 41:42], 0.0).then_inc(s["proj_evac"], 4)

            def lo(L, n, i=0, skipped=0):
                u = L["u"] + n
                dve.wait_ge(s["w_hi"], i * 4 + (L["us"] + n - skipped + 1))
                v.tensor_tensor(w_split[:, u % 4, 1, :], ring_a[:, u % 4, :], w_split[:, u % 4, 0, :].bitcast(f32),
                                ALU.subtract).then_inc(s["w_lo"], 1)

            def lo_loop(L, count):
                with dve.Fori(0, count // 4) as i:
                    for j in range(4):
                        lo(L, j + AHEAD, i)

            def out_split(L, first, x, skipped=0):
                for n in range(KT):
                    dve.wait_ge(s["o_hi"], 8 * L["mixers"] + n + 1)
                    v.tensor_tensor(x[:, 1, n, :], oT[:, n, :], x[:, 0, n, :].bitcast(f32), ALU.subtract)\
                        .then_inc(s["o_ready"], 1)
                    if n in (3, 5, 7):
                        lo(L, first + (n - 3) // 2, 0, skipped)

            def norm(L, gain):
                m = L["part"]
                for n in range(2 if L["kind"] == "ffn" else AHEAD):
                    lo(L, n)
                dve.wait_ge(s["std_ready"], m + 1)
                r = work[:, 6, :]
                step.did(v.reciprocal(r, work[:, 7, :]))
                step.settle()
                for k in range(KT + 2):
                    if k < KT:
                        v.scalar_tensor_tensor(out=hT[:, k, :], in0=xT[:, k, :], scalar=V(gain, k), in1=r,
                                               op0=ALU.mult, op1=ALU.mult).then_inc(s["h_raw"], 1)
                    if k >= 2 and L["kind"] != "rwkv":
                        n = k - 2
                        dve.wait_ge(s["h_hi"], 8 * L["hs"] + n + 1)
                        v.tensor_tensor(h_split[:, 1, n, :], hT[:, n, :], h_split[:, 0, n, :].bitcast(f32),
                                        ALU.subtract).then_inc(s["h_ready"], 1)

            def ffn(L):
                f, u, conv = L["d"] // FT, L["u"], L["idx"] >= 4
                if conv:
                    a = VEC[f"conv{L['idx'] - 4}"][0]
                def tile_pair(i, final):
                    for q in range(2):
                        if not (final and q):
                            lo(L, 2 * q + 2, i)
                            lo(L, 2 * q + 3, i)
                        dve.wait_ge(s["dn_hi"], i * 2 + (L["d"] + q + 1))
                        v.tensor_tensor(d_split[:, q, 1, :], ring_d[:, q, :], d_split[:, q, 0, :].bitcast(f32),
                                        ALU.subtract).then_inc(s["dn_lo"], 1)
                        if conv:
                            g, c = B[4 + q], work[:, 4 + q, :]
                            w = [vec[:, ds(i * 8 + (a + 4 * q + j), 1)] if not isinstance(i, int) else
                                 vec[:, a + 8 * i + 4 * q + j:a + 8 * i + 4 * q + j + 1] for j in range(4)]
                            dve.wait_ge(s["a_used"], i * 4 + (u + 2 * q + 2))
                            step.did(v.tensor_scalar(c, g[:, 0:S], w[1], w[3], ALU.mult, ALU.add))
                            step.settle()
                            step.did(v.scalar_tensor_tensor(out=c[:, 1:S], in0=g[:, 0:S - 1], scalar=w[0],
                                                            in1=c[:, 1:S], op0=ALU.mult, op1=ALU.add))
                            step.settle()
                            v.scalar_tensor_tensor(out=c[:, 0:S - 1], in0=g[:, 1:S], scalar=w[2],
                                                   in1=c[:, 0:S - 1], op0=ALU.mult, op1=ALU.add)\
                                .then_inc(s["conv_ready"], 1)
                        dve.wait_ge(s["silu_ready"], i * 2 + (FT * f + q + 1))
                        v.tensor_tensor(work[:, q, :], work[:, 2 + q, :], B[4 + q][:, S:2 * S], ALU.mult)\
                            .then_inc(s["act_raw"], 1)
                        dve.wait_ge(s["act_hi"], i * 2 + (FT * f + q + 1))
                        v.tensor_tensor(act_split[:, q, 1, :], work[:, q, :], act_split[:, q, 0, :].bitcast(f32),
                                        ALU.subtract).then_inc(s["act_ready"], 1)
                tile_pair(0, False)
                with step.repeat(FT // 2 - 2, 4 if conv else 0, 1) as i:
                    tile_pair(i, False)
                tile_pair(FT // 2 - 1, True)
                dve.wait_ge(s["d_used"], L["d"] + FT)
                for b in range(4):
                    x2 = xT[:, 2 * b:2 * b + 2, :].rearrange("p a b -> p (a b)")
                    v.tensor_tensor(x2, x2, B[b][:, :], ALU.add).then_inc(s["x_added"], 2)

            def tokens_v(L):
                for g in range(4):
                    dve.wait_ge(s["vtok_done"], L["vt"] + g + 1)
                    v.tensor_copy(vtok[:, g // 2, (g % 2) * 512:(g % 2 + 1) * 512], B[g % 2][:, :])\
                        .then_inc(s["vtok_ready"], 1)

            def add_out(L, first, skipped=0):
                for n in range(KT):
                    if n + AHEAD < KT:
                        lo(L, first + n + AHEAD, 0, skipped)
                    dve.wait_ge(s["a_used"], L["u"] + first + n + 1)
                    v.tensor_tensor(xT[:, n, :], xT[:, n, :], B[4 + n % 4][:, 0:S], ALU.add)\
                        .then_inc(s["x_added"], 1)

            def stick(L):
                lo_loop(L, 20)
                lo(L, 23)
                tokens_v(L)

                def masked(h):
                    dve.wait_ge(s["z_done"], h + 1)
                    v.scalar_tensor_tensor(out=zm_(h), in0=B[h % 2][:, 0:384], scalar=HD ** -0.5,
                                           in1=T("stick_neg"), op0=ALU.mult, op1=ALU.add).then_inc(s["zm_ready"], 1)

                def softplus(h):
                    dve.wait_ge(s["ln_ready"], h + 1)
                    if h >= 2:
                        dve.wait_ge(s["cum_done"], h - 1)
                    v.scalar_tensor_tensor(out=planes[:, 1, (h % 2) * 512:(h % 2) * 512 + 384], in0=zm_(h),
                                           scalar=0.0, in1=ln_(h), op0=ALU.max, op1=ALU.add)\
                        .then_inc(s["sp_ready"], 1)

                def logit(h):
                    dve.wait_ge(s["cum_done"], h + 1)
                    if h >= 2:
                        dve.wait_ge(s["p_ready"], h - 1)
                    v.tensor_tensor(lg_(h), zm_(h), B[2 + h % 2][:, 0:384], ALU.subtract)\
                        .then_inc(s["lg_ready"], 1)

                for t in range(NH + 2):
                    if t < NH:
                        masked(t)
                    if 0 <= t - 1 < NH:
                        softplus(t - 1)
                    if 0 <= t - 2 < NH:
                        logit(t - 2)
                out_split(L, 24, x_split[2])
                add_out(L, 24)

            def norm_rope(L, n, row, gained, rope):
                g = L["tiles"] + n
                b, r, t1 = B[2 + n % 2], work[:, 4 + n % 2, :], work[:, 6, :]
                x = work[:, 2 + n % 2, :] if gained else qkv[:, row, :]
                dst = qkv[:, row, :]
                dve.wait_ge(s["nr_mm"], g + 1)
                if gained:
                    dve.wait_ge(s["nr_std"], L["heads"] + n + 1)
                    step.did(v.reciprocal(r, r))
                if rope:
                    step.did(v.tensor_tensor(t1, b[:, S:2 * S], T("sin" + rope), ALU.mult))
                    t2 = work[:, 7, :]
                    step.did(v.tensor_tensor(t2, x, T("cos" + rope), ALU.mult))
                    step.settle()
                    if gained:
                        step.did(v.tensor_tensor(t2, t2, t1, ALU.add))
                        step.settle()
                        v.tensor_tensor(dst, t2, r, ALU.mult).then_inc(s["qk_ready"], 1)
                    else:
                        v.tensor_tensor(dst, t2, t1, ALU.add).then_inc(s["qk_ready"], 1)
                else:
                    step.settle()
                    v.tensor_tensor(dst, x, r, ALU.mult).then_inc(s["qk_ready"], 1)
                dve.wait_ge(s["qk_ready"], g + 1)

            def softmax_heads(L, bias):
                H = L["heads"]

                def shifted(h):
                    dve.wait_ge(s["s_done"], H + h + 1)
                    sm = planes[:, 1, (h % 2) * 512:(h % 2 + 1) * 512]
                    if h >= 2:
                        dve.wait_ge(s["e_ready"], H + h - 1)
                    bb = bias(h)
                    if bb is None:
                        v.tensor_scalar(sm, B[h % 2][:, :], HD ** -0.5, None, ALU.mult).then_inc(s["sm_ready"], 1)
                    else:
                        v.scalar_tensor_tensor(out=sm, in0=B[h % 2][:, :], scalar=HD ** -0.5, in1=bb,
                                               op0=ALU.mult, op1=ALU.add).then_inc(s["sm_ready"], 1)
                    dve.wait_ge(s["sm_ready"], H + h + 1)
                    v.tensor_reduce(small[:, 2 * (h % 2):2 * (h % 2) + 2], sm.rearrange("p (a b) -> p a b", a=NT),
                                    AX.X, ALU.max, negate=True).then_inc(s["nmx_ready"], 1)

                def normed(h):
                    dve.wait_ge(s["e_ready"], H + h + 1)
                    r = small[:, 8 + 2 * (h % 2):10 + 2 * (h % 2)]
                    step.did(v.reciprocal(r, small[:, 4 + 2 * (h % 2):6 + 2 * (h % 2)]))
                    step.settle()
                    for qt in range(NT):
                        p_ = planes[:, 0, (h % 4) * 512 + qt * S:(h % 4) * 512 + (qt + 1) * S]
                        last = v.tensor_scalar(p_, p_, r[:, qt:qt + 1], None, ALU.mult)
                    last.then_inc(s["pn_ready"], 1)

                for t in range(NH + 1):
                    if t < NH:
                        shifted(t)
                    if 0 <= t - 1 < NH:
                        normed(t - 1)

            def dsa(L):
                lo_loop(L, 20)
                for j in range(7):
                    if 23 + j < 30:
                        lo(L, 23 + j)
                    for n in range(3 * j, 3 * j + 3):
                        norm_rope(L, n, n if n < 16 else n + 8, n < 16, "0")
                sc = planes[:, 4, 0:512]
                for i in range(IDX_HEADS):
                    dve.wait_ge(s["idx_relu"], i + 1)
                    if i:
                        dve.wait_ge(s["idx_added"], i)
                    for qt in range(NT):
                        cols = slice(qt * S, (qt + 1) * S)
                        last = v.scalar_tensor_tensor(
                            out=sc[:, cols], in0=planes[:, 1, (i % 2) * 512 + qt * S:(i % 2) * 512 + (qt + 1) * S],
                            scalar=small[:, 16 + 8 * qt + i:17 + 8 * qt + i],
                            in1=(T("visible") if i == 0 else sc)[:, cols], op0=ALU.mult, op1=ALU.add)
                    last.then_inc(s["idx_added"], 1)
                tokens_v(L)
                dve.wait_ge(s["idx_added"], IDX_HEADS)
                for _ in range(N_SEL // 8):
                    for qt in range(NT):
                        step.did(v.max(top8[:, 8 * qt:8 * qt + 8], sc[:, qt * S:(qt + 1) * S]))
                    step.settle()
                    for qt in range(NT):
                        row = sc[:, qt * S:(qt + 1) * S]
                        step.did(v.match_replace(row, top8[:, 8 * qt:8 * qt + 8], row, TAKEN))
                    step.settle()
                step.did(v.tensor_scalar(sc, sc, TAKEN / 2, NEG, ALU.is_gt, ALU.mult))
                step.settle()
                softmax_heads(L, lambda h: sc)
                out_split(L, 30, x_split[2])
                add_out(L, 30)

            top8 = planes[:, 4, 512:528]

            def multi(L):
                r = L["multis"]
                lo_loop(L, 16)
                for j in range(8):
                    if 19 + j < 24:
                        lo(L, 19 + j)
                    for n in (2 * j, 2 * j + 1):
                        norm_rope(L, n, n, True, (None, None, "1", "1", "1", "2", "2", "2")[n % 8])
                tokens_v(L)
                dve.wait_ge(s["na_loaded"], 16 * (r + 1))

                def bias(h):
                    if h < 4:
                        return planes[:, 5, h * 512:(h + 1) * 512]
                    return T("dilated") if h < 10 else None
                softmax_heads(L, bias)
                for seg, (a, b) in enumerate(SEGMENTS):
                    dve.wait_ge(s["on_std"], 3 * r + seg + 1)
                    step.did(v.reciprocal(work[:, 3 + seg, :], work[:, seg, :]))
                    step.settle()
                    for n in range(a, b):
                        v.scalar_tensor_tensor(out=oT[:, n, :], in0=oT[:, n, :], scalar=V(f"out_g{L['idx']}", n),
                                               in1=work[:, 3 + seg, :], op0=ALU.mult, op1=ALU.mult)\
                            .then_inc(s["on_ready"], 1)
                out_split(L, 24, x_split[2])
                add_out(L, 24)

            for L in plan:
                norm(L, f"ffn_g{L['idx']}" if L["kind"] == "ffn" else f"mix_g{MIXER_GAIN[L['kind'], L['idx']]}")
                dict(ffn=ffn, stick=stick, dsa=dsa, multi=multi,
                     rwkv=lambda L: rwkv_dve(dve, L, v, step, lo, tokens_v, out_split, add_out))[L["kind"]](L)

        @block.gpsimd
        def _(pool):
            pstep = Steps(pool, s["pool_step"])
            pool.wait_ge(s["const_loaded"], 16 * N_CONST)
            for L in plan:
                if L["kind"] == "rwkv":
                    rwkv_pool(pool, L, pstep)
                if L["kind"] == "multi":
                    pool.wait_ge(s["h_ready"], 8 * (L["hs"] + 1))
                    pool.dma_start(planes[:, 5, :], na_in[L["idx"], :, :]).then_inc(s["na_loaded"], 16)


SEGMENTS = [(0, 2), (2, 5), (5, 8)]
MIXER_GAIN = {("rwkv", 0): 0, ("stick", 0): 1, ("dsa", 0): 2, ("rwkv", 1): 3, ("multi", 0): 4, ("multi", 1): 5}


def constants():
    t = np.zeros((P, TAB_W), np.float32)

    def put(name, a):
        o, w = TAB[name]
        t[:, o:o + w] = a
    i = np.arange(P)
    put("ident", np.eye(P))
    put("ones", 1.0)
    put("tri", i[:, None] >= i[None, :])
    same = i[:, None] // HD == i[None, :] // HD
    put("head_ones", same)
    put("head_mean", same / HD)

    def rotation(half, base_rows):
        m = np.zeros((P, P), np.float32)
        for o in base_rows:
            for d in range(half):
                m[o + d + half, o + d] = -1.0
                m[o + d, o + d + half] = 1.0
        return m
    put("rot0", rotation(32, [0, 64]))
    put("rot1", rotation(8, [0, 64]))
    put("rot2", rotation(16, [0, 32, 64, 96]))
    pos = np.arange(S).astype(np.float32)

    def inv(theta, dim):
        f = np.float32
        return (f(theta) ** (-np.arange(0, dim, 2, dtype=f) / f(dim))).astype(f)
    half = np.arange(32, dtype=np.float32) / np.float32(32)
    ang0 = pos[None, :] * (np.float32(1.0) / (np.float32(10000.0) ** half)).astype(np.float32)[:, None]
    d = i % HD
    put("cos0", np.cos(ang0)[d % 32])
    put("sin0", np.sin(ang0)[d % 32])
    ang1 = pos[None, :] * inv(500000.0, 16)[:, None]
    put("cos1", np.where((d < 16)[:, None], np.cos(ang1)[d % 8], 1.0))
    put("sin1", np.where((d < 16)[:, None], np.sin(ang1)[d % 8], 0.0))
    fr = inv(10000.0, 32)
    ang_r = (pos // GRID_W)[None, :] * fr[:, None]
    ang_c = (pos % GRID_W)[None, :] * fr[:, None]
    put("cos2", np.where((d < 32)[:, None], np.cos(ang_r)[d % 16], np.cos(ang_c)[d % 16]))
    put("sin2", np.where((d < 32)[:, None], np.sin(ang_r)[d % 16], np.sin(ang_c)[d % 16]))
    q = np.arange(S)
    ok = np.concatenate([i[:, None] < q[None, :], i[:, None] < i[None, :]], 1)
    put("stick_neg", np.where(ok, 0.0, NEG))
    qq = (np.arange(NT)[None, :, None] * P + i[:, None, None])
    vis = q[None, None, :] < (qq // CH + 1) * CH
    put("visible", np.where(vis, 0.0, NEG).reshape(P, -1))
    delta = np.abs(q[None, None, :] - qq)
    count = sum(((delta % dd == 0) & (delta // dd <= (w // 2) // dd)).astype(np.int64)
                for w, dd in ((128, 1), (512, 4), (2048, 16)))
    put("dilated", np.where(count > 0, np.log(np.maximum(count, 1)), NEG).reshape(P, -1))
    put("scan_keep", np.where(q % P == 0, 0.0, 1.0)[None, :])
    strict, incl = i[:, None] < i[None, :], i[:, None] <= i[None, :]
    put("rw_mask", np.concatenate([strict, incl, strict, incl], 1))
    put("eps", EPS)
    put("gn_eps", GN_EPS)
    pair = (i[:, None] // 2 == i[None, :] // 2) & (i[:, None] > i[None, :])
    put("pair_neg", -1.0 * pair)
    put("pair_neg_t", -1.0 * pair.T)
    for lv in range(1, 7):
        n = 1 << lv
        blk = ((i[:, None] // (2 * n) == i[None, :] // (2 * n)) & ((i[:, None] // n) % 2 == 1)
               & ((i[None, :] // n) % 2 == 0))
        put(f"level{lv}", np.eye(P) - blk)
    return t


def cols(vv):
    return np.asarray(vv).reshape(-1, P).T


def blocks(w):
    w = np.asarray(w)
    n = w.shape[1] // P
    return w.reshape(KT, P, n, P).transpose(2, 1, 0, 3).reshape(n, P, KT * P)


def padded(w, n):
    return np.concatenate([w, np.zeros((w.shape[0], n - w.shape[1]), w.dtype)], 1)


def layout(layers, I):
    A, Dn = [], []
    for kind, idx in layers:
        if kind == "ffn":
            gu = I["ffn_w_gu"][idx] if idx < 4 else I["w_gate_up_2"][idx - 4]
            dn = I["ffn_w_down"][idx] if idx < 4 else I["w_down_2"][idx - 4]
            b = blocks(gu)
            A.append(np.stack([b[:FT], b[FT:]], 1).reshape(2 * FT, P, D))
            Dn.append(dn.reshape(FT, P, D))
        elif kind == "stick":
            A += [blocks(I["sb_w_qkv"][0]), blocks(I["sb_w_out"][0])]
        elif kind == "dsa":
            w = I["ds_w_in"][0]
            q, k, vv, qi, ki, wi = np.split(w, [D, 2 * D, 3 * D, 3 * D + 512, 3 * D + 576], 1)
            A += [blocks(q), blocks(k), blocks(qi), blocks(np.concatenate([ki, ki], 1)), blocks(padded(wi, P)),
                  blocks(vv), blocks(I["ds_w_out"][0])]
        elif kind == "multi":
            w = I["w_in_2"][idx]
            qa, ka, va, qd, kd, vd, qc, kc, vc = np.split(
                w, np.cumsum([256, 256, 256, 384, 384, 384, 384, 128]).tolist(), 1)

            def spread(t):
                return np.concatenate([t[:, HD * (h // 3):HD * (h // 3) + HD] for h in range(6)], 1)
            A += [blocks(np.concatenate([qa, qd, qc, ka, kd, spread(kc), va, vd, spread(vc)], 1)),
                  blocks(I["w_out_2"][idx])]
        elif kind == "rwkv":
            w = I["rw_w_rkv"][idx]
            v1 = I["rw_v1"][0] if idx else np.zeros((D, LORA_V), np.float32)
            v2 = I["rw_v2"][0] if idx else np.zeros((LORA_V, D), np.float32)
            g1, g2 = I["rw_g1"][idx], I["rw_g2"][idx]
            last = np.concatenate([g2[P:], v2, np.zeros((64, D), np.float32)], 0)
            A += [blocks(w[0]), blocks(w[1]), blocks(w[2]),
                  blocks(padded(np.concatenate([g1[:, P:], v1], 1), P)), blocks(g1[:, :P]),
                  blocks(np.concatenate([I["rw_w1"][idx], I["rw_a1"][idx]], 1)),
                  np.concatenate([I["rw_w2"][idx], I["rw_a2"][idx]], 0)[None], g2[None, :P], last[None],
                  blocks(I["rw_w_out"][idx])]
    wa = np.concatenate(A, 0)
    wd = np.concatenate(Dn, 0) if Dn else np.zeros((1, P, D), np.float32)
    vec = np.zeros((P, VEC_W), np.float32)

    def put(name, a):
        o, w = VEC[name]
        vec[:, o:o + w] = a
    for l in range(4):
        put(f"mix_g{l}", cols(I["norm_mix"][l]))
        put(f"ffn_g{l}", cols(I["norm_ffn"][l]))
    for l in range(2):
        put(f"mix_g{4 + l}", cols(I["norm1_g_2"][l]))
        put(f"ffn_g{4 + l}", cols(I["norm2_g_2"][l]))
        put(f"out_g{l}", cols(I["out_norm_g_2"][l]))
        cw = np.concatenate([I["conv_w_2"][l], I["conv_b_2"][l][None]], 0)
        put(f"conv{l}", cw.reshape(4, FT, P).transpose(2, 1, 0).reshape(P, 4 * FT))
        for j in range(6):
            put(f"mix{j}_{l}", cols(I["rw_mix"][l, j]))
        for n, key in (("w0", "rw_w0"), ("a0", "rw_a0"), ("k_k", "rw_k_k"), ("k_a", "rw_k_a"), ("ln_w", "rw_ln_w"),
                       ("ln_b", "rw_ln_b")):
            put(f"{n}_{l}", cols(I[key][l]))
        put(f"r_k_{l}", cols(I["rw_r_k"][l].reshape(-1)))
        qg, kg = I["q_norm_g_2"][l], I["k_norm_g_2"][l]
        fam = [0, 0, 1, 1, 1, 2, 2, 2]
        g = [np.concatenate([t[m], t[m]]) for t in (qg, kg) for m in fam] + [np.ones(P, np.float32)] * 8
        put(f"gain{1 + l}", np.stack(g, 1))
    put("v0_", cols(I["rw_v0"][0]))
    g = [np.concatenate([I[t][0]] * 2) for t in ("ds_q_norm", "ds_k_norm") for _ in range(8)]
    put("gain0", np.stack(g + [np.ones(P, np.float32)] * 8, 1))
    t = np.arange(S)
    r, c = t // GRID_W, t % GRID_W
    c0 = np.clip(c - NA_KW // 2, 0, GRID_W - NA_KW)
    inside = (c[None, :] >= c0[:, None]) & (c[None, :] < c0[:, None] + NA_KW)
    dr = r[None, :] - r[:, None] + NA_KH - 1
    dc = np.clip(c[None, :] - c[:, None] + NA_KW - 1, 0, 2 * NA_KW - 2)
    b = np.where(inside[None, None], I["rpb_2"][:, :, dr, dc], np.float32(NEG))
    na = b.reshape(2, 4, NT, P, S).transpose(0, 3, 1, 2, 4).reshape(2, P, 4 * NT * S)
    x = I["x"][0].T.reshape(KT, P, S).transpose(1, 0, 2)
    c_ = np.ascontiguousarray
    return dict(x=c_(x), wa=c_(wa), wd=c_(wd), tab=constants(), vec=vec, na=c_(na.astype(np.float32)))


def kernel(**inputs):
    import concourse.bacc as bacc
    from concourse.bass_utils import run_bass_kernel_spmd
    nc = bacc.Bacc("TRN2", target_bir_lowering=False, num_devices=1)
    arrays = layout(FULL, {k: np.asarray(a) for k, a in inputs.items()})
    args = {n: nc.dram_tensor(n, a.shape, mybir.dt.from_np(a.dtype), kind="ExternalInput").ap()
            for n, a in arrays.items()}
    out = nc.dram_tensor("out", (P, KT, S), mybir.dt.float32, kind="ExternalOutput").ap()
    build_program(nc, FULL, args["x"], args["wa"], args["wd"], args["tab"], args["vec"], args["na"], out)
    r = run_bass_kernel_spmd(nc, [arrays], core_ids=[0])
    y = r.results[0]["out"]
    return np.ascontiguousarray(y.transpose(1, 0, 2).reshape(D, S).T)[None]
```

```python
import numpy as np
import concourse.bass as bass
from concourse import mybir
from contextlib import ExitStack, contextmanager

D, S, P = 1024, 256, 128
KT = D // P
NT = S // P
NH, HD = 16, 64
F_FF = 2816
FT = F_FF // P
CH = 64
N_SEL, IDX_HEADS = 64, 8
GRID_W, NA_KW, NA_KH = 64, 16, 8
EPS, GN_EPS = 1e-6, 64e-5
KAPPA = float(np.exp(-0.5))
NEG = -1e30
TAKEN = -3e38
LORA_W, LORA_A, LORA_V, LORA_G = 64, 64, 32, 160

FULL = [("rwkv", 0), ("ffn", 0), ("stick", 0), ("ffn", 1), ("dsa", 0), ("ffn", 2), ("rwkv", 1), ("ffn", 3),
        ("multi", 0), ("ffn", 4), ("multi", 1), ("ffn", 5)]
PROJ = {"rwkv": 24, "stick": 24, "dsa": 30, "multi": 24}
UNITS = {"rwkv": 38, "stick": 32, "dsa": 38, "multi": 32, "ffn": 44}

TAB = {}
_at = 0
for _n, _w in [("ident", P), ("ones", P), ("tri", P), ("head_ones", P), ("head_mean", P),
               ("rot0", P), ("rot1", P), ("rot2", P), ("cos0", S), ("sin0", S), ("cos1", S), ("sin1", S),
               ("cos2", S), ("sin2", S), ("stick_neg", 3 * P), ("visible", 2 * S), ("dilated", 2 * S),
               ("scan_keep", S), ("rw_mask", 3 * P), ("eps", 1), ("gn_eps", 1), ("level0t", P)] \
        + [(f"level{i}", P) for i in range(7)]:
    TAB[_n] = (_at, _w)
    _at += _w
TAB_W = _at
VEC = {}
_at = 0
for _n, _w in ([(f"mix_g{i}", KT) for i in range(6)] + [(f"ffn_g{i}", KT) for i in range(6)]
               + [(f"{v}{j}", KT) for j in range(2) for v in
                  ("mix0_", "mix1_", "mix2_", "mix3_", "mix4_", "mix5_", "w0_", "a0_", "k_k_", "k_a_", "r_k_",
                   "ln_w_", "ln_b_")]
               + [("v0_", KT)] + [(f"gain{i}", 24) for i in range(3)] + [(f"out_g{i}", KT) for i in range(2)]
               + [(f"conv{i}", 4 * FT) for i in range(2)]):
    VEC[_n] = (_at, _w)
    _at += _w
VEC_W = _at


AHEAD = 3


def early(L):
    return 2 if L["kind"] == "ffn" else AHEAD


class Steps:

    def __init__(self, eng, sem):
        self.eng, self.sem, self.n, self.off = eng, sem, 0, 0

    def did(self, ins):
        ins.then_inc(self.sem, 1)
        self.n += 1

    def settle(self):
        self.eng.wait_ge(self.sem, self.off + self.n)

    @contextmanager
    def repeat(self, count, per, first=0):
        with self.eng.Fori(first, first + count) as i:
            before, self.off = self.n, i * per - first * per
            yield i
            assert self.n - before == per, (self.n - before, per)
        self.n, self.off = before + count * per, 0


def plan_layers(layers):
    out, u, dn, proj, part, vt, heads, pairs = [], 0, 0, 4, 0, 0, 0, 0
    tiles = us = 0
    for kind, idx in layers:
        out.append(dict(kind=kind, idx=idx, u=u, us=us, d=dn, proj=proj, part=part, vt=vt, heads=heads, pairs=pairs,
                        tiles=tiles, rw=sum(o["kind"] == "rwkv" for o in out),
                        mixers=sum(o["kind"] != "ffn" for o in out),
                        hs=sum(o["kind"] != "rwkv" for o in out),
                        convs=sum(o["kind"] == "ffn" and o["idx"] >= 4 for o in out),
                        multis=sum(o["kind"] == "multi" for o in out)))
        u += UNITS[kind]
        us += UNITS[kind] - (3 if kind == "rwkv" else 0)
        part += 1
        if kind == "ffn":
            dn += FT
        else:
            proj += PROJ[kind]
            vt += 4
        if kind in ("dsa", "multi"):
            heads += NH
            tiles += 21 if kind == "dsa" else 16
        if kind in ("stick", "dsa", "multi"):
            pairs += NH // 2
    return out, u, dn


def build_program(nc, layers, x_in, wa, wd, tab_in, vec_in, na_in, out):
    f32 = mybir.dt.float32
    ALU, ACT, AX = mybir.AluOpType, mybir.ActivationFunctionType, mybir.AxisListType
    ds = bass.ds
    plan, n_units, n_downs = plan_layers(layers)
    PARTS = len(plan)
    ctx = ExitStack()
    with ctx:
        def sb(name, shape):
            return ctx.enter_context(nc.sbuf_tensor(name, shape, f32))

        xT = sb("xT", [P, KT, S])
        hT = sb("hT", [P, KT, S])
        sq = sb("sq", [P, KT, S])
        qkv = sb("qkv", [P, 29, S])
        vtok = sb("vtok", [P, NT, D])
        oT = sb("oT", [P, KT, S])
        end_oT = nc.sbuf_base
        ring_a = sb("ring_a", [P, 4, D])
        ring_d = sb("ring_d", [P, 2, D])
        tab = sb("tab_sb", [P, TAB_W])
        vec = sb("vec_sb", [P, VEC_W])
        planes = sb("planes", [P, 8, KT * S])
        end_planes = nc.sbuf_base
        v_first = sb("v_first", [P, KT, S])
        dec = sb("dec", [P, KT, 2, P + 1])
        work = sb("work", [P, 8, S])
        small = sb("small", [P, 64])

        f32r = mybir.dt.float32r
        PLANE = KT * S * 4

        def split(name, shape, offset):
            return nc.alloc_sbuf_tensor_at(name, shape, f32r, offset=offset)
        at_planes, at_vtok = end_planes - 8 * PLANE, end_oT - 2 * PLANE
        w_split = split("w_split", [P, 4, 2, D], at_planes)
        d_split = split("d_split", [P, 2, 2, D], at_planes + 4 * PLANE)
        act_split = split("act_split", [P, 2, 2, S], at_planes + 6 * PLANE)
        x_split = [split("h_split", [P, 2, KT, S], at_vtok),
                   split("x_split1", [P, 2, KT, S], at_planes + 4 * PLANE),
                   split("o_split", [P, 2, KT, S], at_planes + 6 * PLANE)]
        h_split = x_split[0]
        rw_o_split = split("rw_o_split", [P, 2, KT, S], end_oT - 2 * PLANE - 29 * S * 4)

        def T(name):
            a, w = TAB[name]
            return tab[:, a:a + w]

        def V(name, k=None):
            a, w = VEC[name]
            return vec[:, a:a + w] if k is None else vec[:, ds(k + a, 1)] if not isinstance(k, int) \
                else vec[:, a + k:a + k + 1]

        B = [ctx.enter_context(nc.psum_tensor(f"bank{i}", [P, 512], f32)) for i in range(8)]

        sems = {}

        class _S:
            pass
        for n in ("const_loaded x_loaded x_added sq_ready ssum_ready std_ready h_ready a_used d_used silu_ready "
                  "act_ready conv_ready dve_step pool_step act_step proj_evac vtok_done vtok_ready stored "
                  "z_done zm_ready ln_ready sp_ready cum_done lg_ready p_ready pv_done ot_evac "
                  "s_done sm_ready nmx_ready e_ready pn_ready t_done pt_ready "
                  "nr_in nr_mm nr_std qk_ready idx_mm idx_relu idx_added wi_mm wi_ready sel_ready na_loaded "
                  "on_sq on_sum on_std on_ready "
                  "xx_ready xm_ready lora1_mm lora1_ready lora2_mm lora2_ready kk_sq kk_sum kk_std kk_done "
                  "cs_ready dec_ready rk_ready rk_sum keys_ready kt_mm kt_ready factor_ready score_mm score_ready "
                  "at_mm lt_ready padded turn_mm turned xt_ready lx_mm q_ready xn_mm xn_ready rhs_mm rhs_ready u_mm u_ready st_mm st_ready y_mm y_ready "
                  "w_hi w_lo dn_hi dn_lo h_raw h_hi act_raw act_hi xm_raw xm_hi o_raw o_hi o_ready "
                  "gn_mu gn_c gn_sq gn_var gn_std gn_ready kk_raw v_final bonus_ready mid_ready").split():
            sems[n] = ctx.enter_context(nc.semaphore(n))
        a_loaded = [ctx.enter_context(nc.semaphore(f"a_loaded{i}")) for i in range(4)]
        d_loaded = [ctx.enter_context(nc.semaphore(f"d_loaded{i}")) for i in range(2)]
        s = sems
        N_CONST = 2

        block = ctx.enter_context(nc.Block())

        def zm_(h):
            return planes[:, 0, (h % 4) * 512:(h % 4) * 512 + 384]

        def ln_(h):
            return planes[:, 2, (h % 2) * 512:(h % 2) * 512 + 384]

        def lg_(h):
            return planes[:, 2, 1024 + (h % 2) * 512:1024 + (h % 2) * 512 + 384]

        def plane(j):
            return planes[:, j, :].rearrange("p (k t) -> p k t", k=KT)

        def norm_bank(m):
            return B[2] if m and plan[m - 1]["kind"] != "ffn" else B[6]

        CC = NT
        kk_, em, kb, bb, gate, bonus = plane(0), plane(3), plane(4), plane(5), plane(6), plane(7)
        kq = planes[:, 1:3, :].rearrange("p a (k c q t) -> p (a k) c q t", k=KT // 2, c=CC, q=2)
        sc = [qkv[:, 8 * c:8 * c + 8, :].rearrange("p a b -> p (a b)").rearrange("p (i n) -> p i n", i=4)
              for c in range(CC)]
        inv = [qkv[:, 16:24, :].rearrange("p a b -> p (a b)").rearrange("p (m i n) -> p m i n", m=4, i=4),
               planes[:, 3, :].rearrange("p (m i n) -> p m i n", m=4, i=4)]
        X, XT, Q, LT = range(4)
        padded_q = [m.rearrange("p (m i n) -> p m i n", m=4, i=2)
                    for m in (hT[:, :, :].rearrange("p a b -> p (a b)"), planes[:, 0, :])]
        kq_rows = planes[:, 1:3, :].rearrange("p a (m x) -> p (a m) x", x=S)
        sqf = sq[:, :, :].rearrange("p a b -> p (a b)")

        def lane(t, n):
            return t[:, n, :] if isinstance(n, int) else t[:, ds(n, 1), :]

        def heads_of(g):
            return [(i, 4 * g + i, 2 * g + i // 2, HD * (i % 2)) for i in range(4)]

        def step_no(G, lv, c):
            return (6 * G + lv - 1) * 2 + c + 1

        def four(name):
            a, w = TAB[name]
            return tab[:, a:a + w].unsqueeze(1).broadcast_to([P, 4, P])

        def rwkv_pe(pe, L, product, project, transpose_v, out_proj):
            mm, u, r = nc.tensor.matmul, L["u"], L["rw"]
            for j in range(3):
                pe.wait_ge(s["xm_ready"], 48 * r + 8 * (j + 1))
                project(L, 8 * j, 8, x_split[j])

            def loaded(n):
                pe.wait_ge(a_loaded[(u + n) % 4], 16 * ((u + n) // 4 + 1))
                return ring_a[:, (u + n) % 4, :]

            def low(n, dst, m):
                pe.wait_ge(s["w_lo"], L["us"] + n + 1)
                return product(dst[:, 0:S], w_split[:, (u + n) % 4, :, :], x_split[m])
            low(24, B[2], 2)
            pe.wait_ge(s["xm_ready"], 48 * r + 32)
            low(24, B[3], 0).then_inc(s["a_used"], 1)
            low(25, B[1], 0).then_inc(s["a_used"], 1)
            pe.wait_ge(s["xm_ready"], 48 * r + 40)
            low(26, B[0], 1)
            pe.wait_ge(s["xm_ready"], 48 * r + 48)
            pe.wait_ge(s["proj_evac"], L["proj"] + 24)
            low(26, B[4], 2).then_inc(s["a_used"], 1)
            w2a2, g2a, g2v2 = loaded(27), loaded(28), loaded(29)
            pe.wait_ge(s["lora1_ready"], r + 1)
            for n in range(KT):
                p, c = n % 2, slice(n * P, (n + 1) * P)
                if n >= 2:
                    pe.wait_ge(s["lora2_ready"], 8 * r + n - 1)
                mm(B[4 + 2 * p][:, 0:S], w2a2[0:64, c], work[0:64, 4, :], start=True, stop=True)
                mm(B[5 + 2 * p][:, 0:S], w2a2[64:128, c], work[64:128, 4, :], start=True, stop=True)
                mm(B[p][:, 0:S], g2a[:, c], work[:, 5, :], start=True, stop=False)
                last = mm(B[p][:, 0:S], g2v2[0:32, c], work[0:32, 6, :], start=False, stop=True)
                if L["idx"]:
                    last = mm(B[2 + p][:, 0:S], g2v2[32:64, c], work[32:64, 6, :], start=True, stop=True)
                last.then_inc(s["lora2_mm"], 1)
            pe.wait_ge(s["lora2_mm"], 8 * r + 8)
            pe.sem_inc(s["a_used"], 3)
            pe.wait_ge(s["lora2_ready"], 8 * r + 8)
            for n in range(KT):
                pe.wait_ge(s["kk_sq"], 8 * r + n + 1)
                if n >= 4:
                    pe.wait_ge(s["kk_std"], 8 * r + n - 3)
                mm(B[n % 4][:, 0:S], T("head_ones"), sq[:, n, :], start=True, stop=True).then_inc(s["kk_sum"], 1)
            for n in range(KT):
                pe.wait_ge(s["rk_ready"], 8 * r + n + 1)
                if n >= 4:
                    pe.wait_ge(s["bonus_ready"], 8 * r + n - 3)
                mm(B[4 + n % 4][:, 0:S], T("head_ones"), hT[:, n, :], start=True, stop=True)\
                    .then_inc(s["rk_sum"], 1)
            pe.wait_ge(s["v_final"], 8 * r + 8)
            pe.wait_ge(s["kk_std"], 8 * r + 8)
            transpose_v(L)
            pe.wait_ge(s["keys_ready"], 8 * r + 8)
            pe.wait_ge(s["bonus_ready"], 8 * r + 8)
            for g in range(4):
                if g >= 2:
                    pe.wait_ge(s["kt_ready"], 4 * r + g - 1)
                src = kb if g < 2 else bb
                for i in range(4):
                    last = nc.tensor.transpose(B[2 + g % 2][:, i * P:(i + 1) * P], src[:, 4 * (g % 2) + i, 0:P],
                                               T("ident"))
                last.then_inc(s["kt_mm"], 1)
            pe.wait_ge(s["vtok_ready"], L["vt"] + 4)
            pe.wait_ge(s["kt_ready"], 4 * r + 4)

            def first_step(g):
                G = 4 * r + g
                pe.wait_ge(s["padded"], G + 1)
                for c in range(CC):
                    for t in range(2):
                        last = mm(B[c][:, t * S:(t + 1) * S], bb[:, 2 * g + t, c * P:(c + 1) * P],
                                  padded_q[g % 2][:, 2 * t + c, :, 0:P], start=True, stop=True)
                    last.then_inc(s["at_mm"], 1)

            def level_product(g, lv):
                G = 4 * r + g
                for c in range(CC):
                    if lv == 0:
                        pe.wait_ge(s["lt_ready"], 2 * G + c + 1)
                    elif lv == 1:
                        pe.wait_ge(s["q_ready"], 14 * G + c + 1)
                    else:
                        pe.wait_ge(s["xn_ready"], step_no(G, lv - 1, c))
                    for i in range(4):
                        last = mm(B[c][:, i * P:(i + 1) * P], inv[c][:, LT, i, :],
                                  inv[c][:, X, i, :] if lv else T("ident"), start=True, stop=True)
                    last.then_inc(s["lx_mm"], 1)
                    if lv > 1:
                        for i in range(4):
                            last = nc.tensor.transpose(B[2 + c][:, i * P:(i + 1) * P], inv[c][:, X, i, :], T("ident"))
                        last.then_inc(s["turn_mm"], 1)

            def level_update(g, lv):
                G = 4 * r + g
                for c in range(CC):
                    pe.wait_ge(s["q_ready"], 14 * G + 2 * lv + c + 1)
                    if lv == 1:
                        pe.wait_ge(s["xt_ready"], 2 * G + c + 1)
                        if g:
                            pe.wait_ge(s["xn_ready"], step_no(G - 1, 6, c))
                    else:
                        pe.wait_ge(s["turned"], 10 * G + 2 * (lv - 2) + c + 1)
                    for i in range(4):
                        a, b = (XT, Q) if lv < 6 else (Q, XT)
                        last = mm(B[2 + c][:, i * P:(i + 1) * P], inv[c][:, a, i, :], inv[c][:, b, i, :],
                                  start=True, stop=True)
                    last.then_inc(s["xn_mm"], 1)

            def scores(g, c, t):
                k = 4 * (4 * r + g) + 2 * c + t
                if c or t:
                    pe.wait_ge(s["score_ready"], k)
                q, cs = padded_q[g % 2][:, 2 * t + c, :, :], slice(c * P, (c + 1) * P)
                mm(B[6][:, :], kb[:, 2 * g + t, cs], q, start=True, stop=True)
                mm(B[7][:, 0:S], bb[:, 2 * g + t, cs], q[:, :, P:2 * P], start=True, stop=True)\
                    .then_inc(s["score_mm"], 1)

            def right(g, c):
                G = 4 * r + g
                pe.wait_ge(s["score_ready"], 4 * G + 2 * c + 2)
                if c:
                    pe.wait_ge(s["st_ready"], G + 1)
                    pe.wait_ge(s["y_ready"], 2 * G + 1)
                elif g:
                    pe.wait_ge(s["y_ready"], 2 * G)
                for i, h, n, po in heads_of(g):
                    b = B[4 + i % 2][:, c * P + (i // 2) * HD:c * P + (i // 2 + 1) * HD]
                    last = mm(b, sc[c][:, i, 0:P], vtok[:, c, h * HD:(h + 1) * HD], start=True, stop=(c == 0))
                    if c:
                        o = (i // 2) * HD
                        last = mm(b, kq[po:po + HD, n, 1, 0, :], work[po:po + HD, 4, o:o + HD],
                                  start=False, stop=True)
                last.then_inc(s["rhs_mm"], 1)

            def solve(g, c):
                G = 4 * r + g
                pe.wait_ge(s["rhs_ready"], 2 * G + c + 1)
                if c == 0:
                    pe.wait_ge(s["score_ready"], 4 * G + 4)
                for i, h, n, po in heads_of(g):
                    o = (i % 2) * P + (i // 2) * HD
                    last = mm(B[6][:, c * S + i * HD:c * S + (i + 1) * HD], sc[c][:, i, 3 * P:4 * P],
                              work[:, c, o:o + HD], start=True, stop=True)
                last.then_inc(s["u_mm"], 1)

            def state(g):
                G = 4 * r + g
                pe.wait_ge(s["u_ready"], 2 * G + 1)
                for i, h, n, po in heads_of(g):
                    b = B[7][po:po + HD, (i // 2) * HD:(i // 2 + 1) * HD]
                    mm(b, sqf[:, n * P + po:n * P + po + HD], vtok[:, 0, h * HD:(h + 1) * HD],
                       start=True, stop=False)
                    last = mm(b, sqf[:, D + n * P + po:D + n * P + po + HD],
                              work[:, 2, i * HD:(i + 1) * HD], start=False, stop=True)
                last.then_inc(s["st_mm"], 1)

            def outputs(g, c):
                G = 4 * r + g
                pe.wait_ge(s["u_ready"], 2 * G + c + 1)
                for i, h, n, po in heads_of(g):
                    b = B[4 + i % 2][po:po + HD, S + (i // 2) * P:S + (i // 2 + 1) * P]
                    mm(b, vtok[:, c, h * HD:(h + 1) * HD], sc[c][:, i, P:2 * P], start=True, stop=False)
                    last = mm(b, work[:, 2 + c, i * HD:(i + 1) * HD], sc[c][:, i, 2 * P:3 * P],
                              start=False, stop=(c == 0))
                    if c:
                        last = mm(b, work[po:po + HD, 4, (i // 2) * HD:(i // 2 + 1) * HD],
                                  kq[po:po + HD, n, 1, 1, :], start=False, stop=True)
                last.then_inc(s["y_mm"], 1)

            for g in range(5):
                if g < 4:
                    first_step(g)
                if g >= 2:
                    outputs(g - 2, 1)
                if g:
                    scores(g - 1, 0, 0)
                for lv in range(7):
                    if g < 4:
                        level_product(g, lv)
                    if g:
                        if lv in (0, 1, 2):
                            scores(g - 1, (lv + 1) // 2, (lv + 1) % 2)
                        if lv == 2:
                            right(g - 1, 0)
                        if lv == 3:
                            solve(g - 1, 0)
                        if lv == 4:
                            state(g - 1)
                            outputs(g - 1, 0)
                        if lv == 5:
                            right(g - 1, 1)
                        if lv == 6:
                            solve(g - 1, 1)
                    if g < 4 and lv:
                        level_update(g, lv)
            outputs(3, 1)

            pe.wait_ge(s["y_ready"], 8 * r + 8)
            for n in range(KT + 2):
                if n < KT:
                    if n >= 2:
                        pe.wait_ge(s["gn_c"], 8 * r + n - 1)
                    mm(B[n % 2][:, 0:S], T("head_mean"), oT[:, n, :], start=True, stop=True)\
                        .then_inc(s["gn_mu"], 1)
                if n >= 2:
                    m = n - 2
                    pe.wait_ge(s["gn_sq"], 8 * r + m + 1)
                    if m >= 2:
                        pe.wait_ge(s["gn_std"], 8 * r + m - 1)
                    mm(B[2 + m % 2][:, 0:S], T("head_mean"), sq[:, m, :], start=True, stop=True)\
                        .then_inc(s["gn_var"], 1)
            out_proj(L, 30, rw_o_split, skipped=3)

        def rwkv_act(act, L, A, evac, xm_hi, out_split):
            u, r, j = L["u"], L["rw"], L["idx"]
            for k in range(KT):
                xm_hi(L, 0, k // 4, k % 4)
            for group in range(3):
                evac(L, 8 * group, 8, mixed=group + 1)
            for k in range(2 * KT):
                xm_hi(L, 4 + k // KT, k % KT // 4, k % 4)
            act.wait_ge(s["a_used"], u + 27)
            A(work[0:64, 4, :], B[0][0:64, 0:S], ACT.Tanh)
            A(work[64:128, 4, :], B[4][64:128, 0:S], ACT.Copy)
            A(work[:, 5, :], B[1][:, 0:S], ACT.Sigmoid)
            A(work[0:32, 6, :], B[3][0:32, 0:S], ACT.Sigmoid)
            A(work[32:64, 6, :], B[2][32:64, 0:S], ACT.Copy).then_inc(s["lora1_ready"], 1)
            for n in range(KT):
                p = n % 2
                act.wait_ge(s["lora2_mm"], 8 * r + n + 1)
                if j:
                    A(bonus[:, n, :], B[2 + p][:, 0:S], ACT.Sigmoid, bias=V("v0_", n))
                A(kb[:, n, :], B[4 + 2 * p][:, 0:S], ACT.Sigmoid, bias=V(f"w0_{j}", n))
                A(bb[:, n, :], B[5 + 2 * p][:, 0:S], ACT.Sigmoid, bias=V(f"a0_{j}", n))
                A(gate[:, n, :], B[p][:, 0:S], ACT.Copy).then_inc(s["lora2_ready"], 1)
            for n in range(KT):
                act.wait_ge(s["kk_raw"], 8 * r + n + 1)
                A(sq[:, n, :], kk_[:, n, :], ACT.Square).then_inc(s["kk_sq"], 1)
            for n in range(KT):
                act.wait_ge(s["kk_sum"], 8 * r + n + 1)
                A(sq[:, n, :], B[n % 4][:, 0:S], ACT.Sqrt).then_inc(s["kk_std"], 1)
            act.wait_ge(s["mid_ready"], r + 1)
            A(dec[:, :, :, 0:1].rearrange("p k c o -> p (k c o)"), small[:, 0:16], ACT.Exp)
            A(small[:, 32:40], small[:, 1:16:2], ACT.Exp, scale=-1.0)
            for n in range(KT):
                for c in range(CC):
                    cs = slice(c * P, (c + 1) * P)
                    A(dec[:, n, c, 1:P + 1], oT[:, n, cs], ACT.Exp, scale=-KAPPA,
                      bias=small[:, 2 * n + c:2 * n + c + 1])
                    last = A(em[:, n, cs], oT[:, n, cs], ACT.Exp, scale=KAPPA,
                             bias=small[:, 16 + 2 * n + c:17 + 2 * n + c])
                last.then_inc(s["dec_ready"], 1)
            for g in range(4):
                act.wait_ge(s["kt_mm"], 4 * r + g + 1)
                A(sqf[:, g * 512:(g + 1) * 512], B[2 + g % 2][:, :], ACT.Copy).then_inc(s["kt_ready"], 1)
            act.wait_ge(s["dec_ready"], 8 * r + 8)

            def level_copy(g, lv):
                G = 4 * r + g
                for c in range(CC):
                    act.wait_ge(s["xn_mm"], step_no(G, lv, c))
                    if lv < 6:
                        A(inv[c][:, X, :, :].rearrange("p i n -> p (i n)"), B[2 + c][:, :], ACT.Copy)\
                            .then_inc(s["xn_ready"], 1)
                    else:
                        A(sc[c][:, :, 3 * P:4 * P], B[2 + c][:, :].rearrange("p (i n) -> p i n", i=4), ACT.Copy)\
                            .then_inc(s["xn_ready"], 1)
                if lv < 6:
                    for c in range(CC):
                        act.wait_ge(s["turn_mm"], 10 * G + 2 * (lv - 1) + c + 1)
                        A(inv[c][:, XT, :, :].rearrange("p i n -> p (i n)"), B[2 + c][:, :], ACT.Copy)\
                            .then_inc(s["turned"], 1)

            def copy_rhs(g, c):
                act.wait_ge(s["rhs_mm"], 8 * r + 2 * g + c + 1)
                A(work[:, c, 0:P], B[4][:, c * P:(c + 1) * P], ACT.Copy)
                A(work[:, c, P:2 * P], B[5][:, c * P:(c + 1) * P], ACT.Copy).then_inc(s["rhs_ready"], 1)

            def copy_u(g, c):
                act.wait_ge(s["u_mm"], 8 * r + 2 * g + c + 1)
                A(work[:, 2 + c, :], B[6][:, c * S:(c + 1) * S], ACT.Copy, scale=-1.0).then_inc(s["u_ready"], 1)

            def copy_y(g, c):
                act.wait_ge(s["y_mm"], 8 * r + 2 * g + c + 1)
                for p in range(2):
                    po = HD * p
                    last = A(oT[po:po + HD, 2 * g:2 * g + 2, c * P:(c + 1) * P],
                             B[4 + p][po:po + HD, S:2 * S].rearrange("p (a b) -> p a b", a=2), ACT.Copy)
                last.then_inc(s["y_ready"], 1)

            def copy_state(g):
                act.wait_ge(s["st_mm"], 4 * r + g + 1)
                if g == 0:
                    act.wait_ge(s["factor_ready"], r + 1)
                for t in range(2):
                    last = A(work[:, 4, t * HD:(t + 1) * HD], B[7][:, t * HD:(t + 1) * HD], ACT.Copy,
                             scale=small[:, 40 + 2 * g + t:41 + 2 * g + t])
                last.then_inc(s["st_ready"], 1)

            for g in range(5):
                if g >= 2:
                    copy_y(g - 2, 1)
                for lv in range(7):
                    if g:
                        if lv == 2:
                            copy_rhs(g - 1, 0)
                        if lv == 3:
                            copy_u(g - 1, 0)
                        if lv == 4:
                            copy_state(g - 1)
                            copy_y(g - 1, 0)
                        if lv == 5:
                            copy_rhs(g - 1, 1)
                        if lv == 6:
                            copy_u(g - 1, 1)
                    if g < 4 and lv:
                        level_copy(g, lv)
            copy_y(3, 1)
            for n in range(KT + 1):
                if n < KT:
                    act.wait_ge(s["gn_c"], 8 * r + n + 1)
                    A(sq[:, n, :], oT[:, n, :], ACT.Square).then_inc(s["gn_sq"], 1)
                if n >= 1:
                    m = n - 1
                    act.wait_ge(s["gn_var"], 8 * r + m + 1)
                    if m >= 2:
                        act.wait_ge(s["gn_ready"], 8 * r + m - 1)
                    A(work[:, m % 2, :], B[2 + m % 2][:, 0:S], ACT.Sqrt, bias=T("gn_eps")).then_inc(s["gn_std"], 1)
            out_split(L, 30, rw_o_split, lambda n: act.wait_ge(s["gn_ready"], 8 * r + n + 1))

        def rwkv_dve(dve, L, v, step, lo, tokens_v, out_split, add_out):
            r, j, j_ = L["rw"], L["idx"], L["idx"]
            dve.wait_ge(s["h_raw"], 8 * (L["part"] + 1))
            step.did(v.tensor_tensor(sq[:, :, 1:S], hT[:, :, 0:S - 1], hT[:, :, 1:S], ALU.subtract))
            step.did(v.tensor_scalar(sq[:, :, 0:1], hT[:, :, 0:1], -1.0, None, ALU.mult))
            step.settle()
            order = (0, 1, 2, 5, 3, 4)

            def mixed(group, i, j):
                k = i * 4 + j
                a = VEC[f"mix{order[group]}_{j_}"][0]
                num = isinstance(k, int)
                if r or group or not num or k >= 4:
                    dve.wait_ge(s["xm_ready"], i * 4 + (48 * r + 8 * group + j - 3))
                v.scalar_tensor_tensor(out=work[:, j, :], in0=sq[:, k, :] if num else sq[:, ds(k, 1), :],
                                       scalar=vec[:, a + k:a + k + 1] if num else vec[:, ds(k + a, 1)],
                                       in1=hT[:, k, :] if num else hT[:, ds(k, 1), :],
                                       op0=ALU.mult, op1=ALU.add).then_inc(s["xm_raw"], 1)

            def mixed_low(group, i, j):
                k = i * 4 + j
                t = x_split[group % 3]
                dve.wait_ge(s["xm_hi"], i * 4 + (48 * r + 8 * group + j + 1))
                hi_, lo_ = [t[:, q, k, :] if isinstance(k, int) else t[:, q, ds(k, 1), :] for q in range(2)]
                v.tensor_tensor(lo_, work[:, j, :], hi_.bitcast(f32), ALU.subtract).then_inc(s["xm_ready"], 1)

            for k in range(KT + 1):
                if k < KT:
                    mixed(0, k // 4, k % 4)
                if k:
                    mixed_low(0, (k - 1) // 4, (k - 1) % 4)
            for group in range(1, 4):
                with dve.Fori(0, 2) as i:
                    for q in range(4):
                        mixed(group, i, q)
                        lo(L, 8 * (group - 1) + q + AHEAD, i)
                        mixed_low(group, i, q)
            for t in range(2 * KT + 1):
                if t < 2 * KT:
                    mixed(4 + t // KT, t % KT // 4, t % 4)
                if t:
                    mixed_low(4 + (t - 1) // KT, (t - 1) % KT // 4, (t - 1) % 4)
            dve.wait_ge(s["xm_ready"], 48 * r + 48)
            dve.wait_ge(s["proj_evac"], L["proj"] + 24)
            for n in range(KT):
                K, R, Vt, t = qkv[:, 8 + n, :], qkv[:, n, :], qkv[:, 16 + n, :], work[:, n % 2, :]
                dve.wait_ge(s["lora2_ready"], 8 * r + n + 1)
                if j == 0:
                    v.tensor_copy(v_first[:, n, :], Vt).then_inc(s["v_final"], 1)
                else:
                    step.did(v.tensor_tensor(work[:, 7, :], v_first[:, n, :], Vt, ALU.subtract))
                    step.settle()
                    step.did(v.tensor_tensor(work[:, 7, :], work[:, 7, :], bonus[:, n, :], ALU.mult))
                    step.settle()
                    v.tensor_tensor(Vt, Vt, work[:, 7, :], ALU.add).then_inc(s["v_final"], 1)
                v.tensor_scalar(kk_[:, n, :], K, V(f"k_k_{j}", n), None, ALU.mult).then_inc(s["kk_raw"], 1)
                step.did(v.tensor_scalar(t, bb[:, n, :], 1.0, V(f"k_a_{j}", n), ALU.subtract, ALU.mult))
                dve.wait_ge(s["kk_raw"], 8 * r + n + 1)
                step.settle()
                step.did(v.scalar_tensor_tensor(out=K, in0=t, scalar=1.0, in1=K, op0=ALU.add, op1=ALU.mult))
                step.did(v.tensor_tensor_scan(oT[:, n, :], T("scan_keep"), kb[:, n, :], 0.0, ALU.mult, ALU.add))
                step.settle()
                v.scalar_tensor_tensor(out=hT[:, n, :], in0=R, scalar=V(f"r_k_{j}", n), in1=K,
                                       op0=ALU.mult, op1=ALU.mult).then_inc(s["rk_ready"], 1)
                dve.wait_ge(s["v_final"], 8 * r + n + 1)
            mids = oT[:, :, :].rearrange("p k (c t) -> p (k c) t", c=CC)[:, :, P // 2 - 1:P // 2]
            step.did(v.tensor_scalar(small[:, 0:16].unsqueeze(2), mids, KAPPA, None, ALU.mult))
            v.tensor_scalar(small[:, 16:32].unsqueeze(2), mids, -KAPPA, None, ALU.mult).then_inc(s["mid_ready"], 1)
            for n in range(KT):
                std = sq[:, n, :]
                dve.wait_ge(s["kk_std"], 8 * r + n + 1)
                step.did(v.tensor_scalar(std, std, 1e-12, None, ALU.max))
                step.settle()
                step.did(v.reciprocal(std, std))
                step.settle()
                step.did(v.tensor_tensor(kk_[:, n, :], kk_[:, n, :], std, ALU.mult))
                step.settle()
                step.did(v.tensor_tensor(bb[:, n, :], kk_[:, n, :], bb[:, n, :], ALU.mult))
                dve.wait_ge(s["dec_ready"], 8 * r + n + 1)

                def chunks(t):
                    return t.rearrange("p (c t) -> p c t", c=CC)
                step.did(v.tensor_tensor(kq[:, n, :, 0, :], chunks(kk_[:, n, :]), dec[:, n, :, 0:P], ALU.mult))
                step.did(v.tensor_tensor(kq[:, n, :, 1, :], chunks(qkv[:, n, :]), dec[:, n, :, 1:P + 1], ALU.mult))
                step.did(v.tensor_tensor(kb[:, n, :], qkv[:, 8 + n, :], em[:, n, :], ALU.mult))
                step.settle()
                v.tensor_tensor(bb[:, n, :], bb[:, n, :], em[:, n, :], ALU.mult).then_inc(s["keys_ready"], 1)
            v.tensor_tensor(small[:, 40:48].unsqueeze(2), small[:, 32:40].unsqueeze(2), dec[:, :, 0, P:P + 1],
                            ALU.mult).then_inc(s["factor_ready"], 1)
            for n in range(KT):
                dve.wait_ge(s["rk_sum"], 8 * r + n + 1)
                v.tensor_tensor(bonus[:, n, :], B[4 + n % 4][:, 0:S], qkv[:, 16 + n, :], ALU.mult)\
                    .then_inc(s["bonus_ready"], 1)
            tokens_v(L)
            dve.wait_ge(s["keys_ready"], 8 * r + 8)
            dve.wait_ge(s["bonus_ready"], 8 * r + 8)

            def first_masks(g):
                for c in range(CC):
                    G = 4 * r + g
                    dve.wait_ge(s["at_mm"], 2 * G + c + 1)
                    a = TAB["rw_mask"][0]
                    lt = inv[c][:, LT, :, :]
                    step.did(v.tensor_tensor(lt, B[c][:, :].rearrange("p (i n) -> p i n", i=4),
                                             tab[:, a:a + P].unsqueeze(1).broadcast_to([P, 4, P]), ALU.mult))
                    step.settle()
                    v.tensor_tensor(lt, lt, four("ident"), ALU.add).then_inc(s["lt_ready"], 1)

            def factor(g, lv):
                G = 4 * r + g
                for c in range(CC):
                    dve.wait_ge(s["lx_mm"], (7 * G + lv) * 2 + c + 1)
                    v.tensor_tensor(inv[c][:, Q if lv else X, :, :], B[c][:, :].rearrange("p (i n) -> p i n", i=4),
                                    four(f"level{lv}"), ALU.mult).then_inc(s["q_ready"], 1)

            def score_masks(g, c, t):
                G = 4 * r + g
                dve.wait_ge(s["score_mm"], 4 * G + 2 * c + t + 1)
                if g and t == 0:
                    dve.wait_ge(s["y_mm"], 2 * G - 1 + c)
                a, two_heads = TAB["rw_mask"][0], slice(2 * t, 2 * t + 2)
                v.tensor_tensor(sc[c][:, two_heads, 0:2 * P], B[6][:, :].rearrange("p (i n) -> p i n", i=2),
                                tab[:, a:a + 2 * P].unsqueeze(1).broadcast_to([P, 2, 2 * P]), ALU.mult)
                v.tensor_tensor(sc[c][:, two_heads, 2 * P:3 * P], B[7][:, 0:S].rearrange("p (i n) -> p i n", i=2),
                                tab[:, a + P:a + 2 * P].unsqueeze(1).broadcast_to([P, 2, P]), ALU.mult)\
                    .then_inc(s["score_ready"], 1)

            for g in range(5):
                if g < 4:
                    first_masks(g)
                if g:
                    score_masks(g - 1, 0, 0)
                for lv in range(7):
                    if g < 4:
                        factor(g, lv)
                    if g and lv < 3:
                        score_masks(g - 1, (lv + 1) // 2, (lv + 1) % 2)
            for n in range(KT + 2):
                if n < KT:
                    dve.wait_ge(s["gn_mu"], 8 * r + n + 1)
                    v.tensor_tensor(oT[:, n, :], oT[:, n, :], B[n % 2][:, 0:S], ALU.subtract)\
                        .then_inc(s["gn_c"], 1)
                if n >= 2:
                    m = n - 2
                    y, sd = oT[:, m, :], work[:, m % 2, :]
                    dve.wait_ge(s["gn_std"], 8 * r + m + 1)
                    step.did(v.reciprocal(sd, sd))
                    step.settle()
                    step.did(v.tensor_tensor(y, y, sd, ALU.mult))
                    step.settle()
                    step.did(v.tensor_scalar(y, y, V(f"ln_w_{j}", m), V(f"ln_b_{j}", m), ALU.mult, ALU.add))
                    step.settle()
                    step.did(v.tensor_tensor(y, y, bonus[:, m, :], ALU.add))
                    step.settle()
                    v.tensor_tensor(y, y, gate[:, m, :], ALU.mult).then_inc(s["gn_ready"], 1)
            out_split(L, 30, rw_o_split, skipped=3)
            add_out(L, 30, skipped=3)

        def rwkv_pool(pool, L, pstep):
            r = L["rw"]
            g_ = nc.gpsimd
            pool.wait_ge(s["keys_ready"], 8 * r + 8)
            pool.wait_ge(s["bonus_ready"], 8 * r + 8)
            for g in range(4):
                G, q = 4 * r + g, padded_q[g % 2]
                if g < 2:
                    if g:
                        pool.wait_ge(s["xt_ready"], 2 * G)
                    pstep.did(g_.memset(q[0:HD, :, 1, :], 0.0))
                    pstep.settle()
                    pstep.did(g_.memset(q[HD:P, :, 0, :], 0.0))
                    pstep.settle()
                else:
                    pool.wait_ge(s["score_mm"], 4 * G - 4)
                    pool.wait_ge(s["xt_ready"], 2 * G)
                pstep.did(g_.tensor_copy(q[0:HD, :, 0, :], kq_rows[0:HD, 4 * g:4 * g + 4, :]))
                pstep.settle()
                g_.tensor_copy(q[HD:P, :, 1, :], kq_rows[HD:P, 4 * g:4 * g + 4, :]).then_inc(s["padded"], 1)
                pool.wait_ge(s["padded"], G + 1)
                for c in range(CC):
                    pool.wait_ge(s["lt_ready"], 2 * G + c + 1)
                    g_.tensor_tensor(inv[c][:, XT, :, :], inv[c][:, LT, :, :], four("level0t"), ALU.mult)\
                        .then_inc(s["xt_ready"], 1)

        @block.sync
        def _(sp):
            sp.dma_start(xT[:, :, :], x_in).then_inc(s["x_loaded"], 16)
            sp.dma_start(tab[:, :], tab_in).then_inc(s["const_loaded"], 16)
            sp.dma_start(vec[:, :], vec_in).then_inc(s["const_loaded"], 16)

            def load(L, n, i=0):
                u, back = L["u"] + n, n - 4
                if back >= 0 and L["kind"] == "rwkv" and back in (27, 28, 29):
                    sp.wait_ge(s["a_used"], u - 3)
                elif u >= 4 or not isinstance(i, int):
                    skipped = 3 if L["kind"] == "rwkv" and back >= 30 else 0
                    sp.wait_ge(s["w_lo"], i * 4 + (L["us"] + back - skipped + 1))
                sp.dma_start(ring_a[:, u % 4, :], wa[i * 4 + u, :, :] if not isinstance(i, int) else wa[u, :, :])\
                    .then_inc(a_loaded[u % 4], 16)

            for L in plan:
                n_units_here = UNITS[L["kind"]]
                if L["kind"] == "ffn":
                    def two_tiles(i, first):
                        for j in range(4):
                            load(L, j, i)
                        for j in range(2):
                            if not (first and L["d"] + j < 2):
                                sp.wait_ge(s["dn_lo"], i * 2 + (L["d"] + j - 1))
                            sp.dma_start(ring_d[:, j, :], wd[i * 2 + (L["d"] + j), :, :])\
                                .then_inc(d_loaded[j], 16)
                    two_tiles(0, True)
                    with sp.Fori(1, FT // 2) as i:
                        two_tiles(i, False)
                else:
                    looped = 24
                    for n in range(4):
                        load(L, n)
                    with sp.Fori(0, (looped - 4) // 4) as i:
                        for j in range(4):
                            load(L, 4 + j, i)
                    for n in range(looped, n_units_here):
                        load(L, n)
            sp.wait_ge(s["x_added"], 8 * (PARTS + 1))
            sp.dma_start(out, xT[:, :, :]).then_inc(s["stored"], 16)
            sp.wait_ge(s["stored"], 16)

        @block.tensor
        def _(pe):
            mm = nc.tensor.matmul
            pe.wait_ge(s["const_loaded"], 16 * N_CONST)

            def norm(m):
                for k in range(KT):
                    pe.wait_ge(s["sq_ready"], 8 * m + k + 1)
                    last = mm(norm_bank(m)[:, 0:S], T("ones"), sq[:, k, :], start=(k == 0), stop=(k == KT - 1))
                last.then_inc(s["ssum_ready"], 1)

            def product(dst, w, x, ready=None):
                for k in range(KT):
                    if ready is not None:
                        pe.wait_ge(s["h_ready"], ready + k + 1)
                    ks = slice(k * P, (k + 1) * P)
                    mm(dst, w[:, 0, ks], x[:, 0, k, :], start=(k == 0), stop=False)
                    mm(dst, w[:, 0, ks], x[:, 1, k, :], start=False, stop=False)
                    last = mm(dst, w[:, 1, ks], x[:, 0, k, :], start=False, stop=(k == KT - 1))
                return last

            def unit(L, n, i, dst, x, skipped=0, ready=None):
                pe.wait_ge(s["w_lo"], i * 4 + (L["us"] + n - skipped + 1))
                product(dst, w_split[:, (L["u"] + n) % 4, :, :], x, ready).then_inc(s["a_used"], 1)

            def ffn(L):
                f, d = L["d"] // FT, L["d"]

                def gate_up(i, q, first=False):
                    for g in range(2):
                        unit(L, 2 * q + g, i, B[4 + q][:, g * S:(g + 1) * S], h_split,
                             ready=8 * L["hs"] if first and g == 0 else None)

                def down(i, q, first=False, final=False):
                    pe.wait_ge(s["act_ready"], i * 2 + (FT * f + q + 1))
                    pe.wait_ge(s["dn_lo"], i * 2 + (d + q + 1))
                    for m in range(KT):
                        o, ms = B[m // 2][:, (m % 2) * S:(m % 2 + 1) * S], slice(m * P, (m + 1) * P)
                        mm(o, d_split[:, q, 0, ms], act_split[:, q, 0, :], start=(first and m % 2 == 0),
                           stop=False, skip_group_check=True)
                        mm(o, d_split[:, q, 0, ms], act_split[:, q, 1, :], start=False,
                           stop=False, skip_group_check=True)
                        last = mm(o, d_split[:, q, 1, ms], act_split[:, q, 0, :], start=False,
                                  stop=final, skip_group_check=True)
                    last.then_inc(s["d_used"], 1)

                gate_up(0, 0, first=True)
                gate_up(0, 1)
                down(0, 0, first=True)
                with pe.Fori(1, FT // 2) as i:
                    gate_up(i, 0)
                    down(i - 1, 1)
                    gate_up(i, 1)
                    down(i, 0)
                down(FT // 2 - 1, 1, final=True)

            def project(L, first, count, x):
                def four_units(i, ready=None):
                    for j in range(4):
                        pe.wait_ge(s["proj_evac"], i * 4 + (L["proj"] + first + j - 3))
                        unit(L, first + j, i, B[4 + (first + j) % 4][:, 0:S], x, ready=ready if j == 0 else None)
                peeled = x is h_split and first == 0 and L["kind"] != "rwkv"
                if peeled:
                    four_units(0, 8 * L["hs"])
                with pe.Fori(int(peeled), count // 4) as i:
                    four_units(i)

            def project_one(L, n):
                pe.wait_ge(s["proj_evac"], L["proj"] + n - 3)
                unit(L, n, 0, B[4 + n % 4][:, 0:S], h_split)

            def transpose_v(L, dst_done=True):
                for g in range(4):
                    if g >= 2:
                        pe.wait_ge(s["vtok_ready"], L["vt"] + g - 1)
                    for i in range(4):
                        last = nc.tensor.transpose(B[g % 2][:, i * P:(i + 1) * P],
                                                   qkv[:, 16 + 4 * (g % 2) + i, (g // 2) * P:(g // 2 + 1) * P],
                                                   T("ident"))
                    last.then_inc(s["vtok_done"], 1)

            def out_proj(L, first, x, skipped=0):
                pe.wait_ge(s["proj_evac"], L["proj"] + min(first, PROJ[L["kind"]]))
                pe.wait_ge(s["o_ready"], 8 * (L["mixers"] + 1))
                for n in range(KT):
                    if n >= 4:
                        pe.wait_ge(s["x_added"], 8 * (L["part"] + 1) + n - 3)
                    unit(L, first + n, 0, B[4 + n % 4][:, 0:S], x, skipped)

            def stick(L):
                project(L, 0, 24, h_split)
                pe.wait_ge(s["proj_evac"], L["proj"] + 24)
                transpose_v(L)
                pe.wait_ge(s["vtok_ready"], L["vt"] + 4)

                def z(h):
                    po, t = HD * (h % 2), h // 2
                    if h >= 2:
                        pe.wait_ge(s["zm_ready"], h - 1)
                    mm(B[h % 2][:, 0:S], qkv[po:po + HD, 8 + t, 0:P], qkv[po:po + HD, t, :], start=True, stop=True)
                    mm(B[h % 2][:, S:S + P], qkv[po:po + HD, 8 + t, P:S], qkv[po:po + HD, t, P:S],
                       start=True, stop=True).then_inc(s["z_done"], 1)

                def suffix(h):
                    pe.wait_ge(s["sp_ready"], h + 1)
                    if h >= 2:
                        pe.wait_ge(s["lg_ready"], h - 1)
                    b, sp_ = B[2 + h % 2], planes[:, 1, (h % 2) * 512:(h % 2) * 512 + 384]
                    mm(b[:, 0:S], T("tri"), sp_[:, 0:S], start=True, stop=False, skip_group_check=True)
                    mm(b[:, P:S], T("ones"), sp_[:, S:384], start=False, stop=True, skip_group_check=True)
                    mm(b[:, S:384], T("tri"), sp_[:, S:384], start=True, stop=True,
                       skip_group_check=True).then_inc(s["cum_done"], 1)

                def pv(h):
                    po, t = HD * (h % 2), h // 2
                    pe.wait_ge(s["p_ready"], h + 1)
                    if h % 2 == 0 and t >= 2:
                        pe.wait_ge(s["ot_evac"], L["pairs"] + t - 1)
                    p_, b = planes[:, 3, (h % 2) * 512:(h % 2) * 512 + 384], B[4 + t % 2]
                    mm(b[po:po + HD, 0:S], vtok[:, 0, h * HD:(h + 1) * HD], p_[:, 0:S], start=True, stop=False,
                       skip_group_check=True)
                    mm(b[po:po + HD, P:S], vtok[:, 1, h * HD:(h + 1) * HD], p_[:, S:384], start=False, stop=True,
                       skip_group_check=True).then_inc(s["pv_done"], 1)

                for t in range(NH + 3):
                    if t < NH:
                        z(t)
                    if 0 <= t - 2 < NH:
                        suffix(t - 2)
                    if 0 <= t - 3 < NH:
                        pv(t - 3)
                out_proj(L, 24, x_split[2])

            def norm_rope_mm(L, n, row, gained, rot):
                g = L["tiles"] + n
                if gained:
                    pe.wait_ge(s["nr_in"], L["heads"] + n + 1)
                else:
                    pe.wait_ge(s["proj_evac"], L["proj"] + 21)
                if n >= 2:
                    pe.wait_ge(s["qk_ready"], g - 1)
                b = B[2 + n % 2]
                if gained:
                    mm(b[:, 0:S], T("head_mean"), work[:, n % 2, :], start=True, stop=True)
                last = mm(b[:, S:2 * S], T(rot), work[:, 2 + n % 2, :] if gained else qkv[:, row, :],
                          start=True, stop=True)
                last.then_inc(s["nr_mm"], 1)

            def softmax_heads(L):
                H, O = L["heads"], L["pairs"]

                def scores(h):
                    po, t = HD * (h % 2), h // 2
                    if h >= 2:
                        pe.wait_ge(s["sm_ready"], H + h - 1)
                    for qt in range(NT):
                        last = mm(B[h % 2][:, qt * S:(qt + 1) * S], qkv[po:po + HD, t, qt * P:(qt + 1) * P],
                                  qkv[po:po + HD, 8 + t, :], start=True, stop=True)
                    last.then_inc(s["s_done"], 1)

                def turn(h):
                    pe.wait_ge(s["pn_ready"], H + h + 1)
                    if h >= 2:
                        pe.wait_ge(s["pt_ready"], H + h - 1)
                    p_ = planes[:, 0, (h % 4) * 512:(h % 4 + 1) * 512]
                    for st in range(NT):
                        for qt in range(NT):
                            last = nc.tensor.transpose(B[2 + h % 2][:, st * S + qt * P:st * S + (qt + 1) * P],
                                                       p_[:, qt * S + st * P:qt * S + (st + 1) * P], T("ident"))
                    last.then_inc(s["t_done"], 1)

                def pv(h):
                    po, t = HD * (h % 2), h // 2
                    pe.wait_ge(s["pt_ready"], H + h + 1)
                    if h % 2 == 0 and t >= 2:
                        pe.wait_ge(s["ot_evac"], O + t - 1)
                    for st in range(NT):
                        last = mm(B[4 + t % 2][po:po + HD, 0:S], vtok[:, st, h * HD:(h + 1) * HD],
                                  planes[:, 2, (h % 2) * 512 + st * S:(h % 2) * 512 + (st + 1) * S],
                                  start=(st == 0), stop=(st == NT - 1))
                    last.then_inc(s["pv_done"], 1)

                for t in range(NH + 3):
                    if t < NH:
                        scores(t)
                    if 0 <= t - 2 < NH:
                        turn(t - 2)
                    if 0 <= t - 3 < NH:
                        pv(t - 3)

            def dsa(L):
                project(L, 0, 20, h_split)
                project_one(L, 20)
                pe.wait_ge(s["proj_evac"], L["proj"] + 21 - 3)
                pe.wait_ge(s["w_lo"], L["us"] + 22)
                wi = w_split[:, (L["u"] + 21) % 4, :, :]
                for qt in range(NT):
                    o, qs = B[5][:, qt * 8:(qt + 1) * 8], slice(qt * P, (qt + 1) * P)
                    for k in range(KT):
                        mm(o, h_split[:, 0, k, qs], wi[:, 0, k * P:k * P + 8], start=(k == 0), stop=False)
                        mm(o, h_split[:, 0, k, qs], wi[:, 1, k * P:k * P + 8], start=False, stop=False)
                        last = mm(o, h_split[:, 1, k, qs], wi[:, 0, k * P:k * P + 8],
                                  start=False, stop=(k == KT - 1))
                last.then_inc(s["a_used"], 1)
                for j in range(8):
                    project_one(L, 22 + j)
                    for n in range(3 * j, min(3 * j + 3, 21)):
                        row = n if n < 16 else n + 8
                        norm_rope_mm(L, n, row, n < 16, "rot0")
                pe.wait_ge(s["qk_ready"], L["tiles"] + 21)
                for i in range(IDX_HEADS):
                    po, t = HD * (i % 2), 24 + i // 2
                    if i >= 2:
                        pe.wait_ge(s["idx_relu"], i - 1)
                    for qt in range(NT):
                        last = mm(B[i % 2][:, qt * S:(qt + 1) * S], qkv[po:po + HD, t, qt * P:(qt + 1) * P],
                                  qkv[po:po + HD, 28, :], start=True, stop=True)
                    last.then_inc(s["idx_mm"], 1)
                pe.wait_ge(s["idx_relu"], IDX_HEADS)
                pe.wait_ge(s["proj_evac"], L["proj"] + 30)
                transpose_v(L)
                pe.wait_ge(s["vtok_ready"], L["vt"] + 4)
                softmax_heads(L)
                out_proj(L, 30, x_split[2])

            ROT = [None, None, "rot1", "rot1", "rot1", "rot2", "rot2", "rot2"]

            def multi(L):
                project(L, 0, 16, h_split)
                for j in range(8):
                    project_one(L, 16 + j)
                    for n in (2 * j, 2 * j + 1):
                        g = L["tiles"] + n
                        pe.wait_ge(s["nr_in"], L["heads"] + n + 1)
                        if n >= 2:
                            pe.wait_ge(s["qk_ready"], g - 1)
                        b = B[2 + n % 2]
                        last = mm(b[:, 0:S], T("head_mean"), work[:, n % 2, :], start=True, stop=True)
                        if ROT[n % 8]:
                            last = mm(b[:, S:2 * S], T(ROT[n % 8]), work[:, 2 + n % 2, :], start=True, stop=True)
                        last.then_inc(s["nr_mm"], 1)
                pe.wait_ge(s["proj_evac"], L["proj"] + 24)
                pe.wait_ge(s["qk_ready"], L["tiles"] + 16)
                transpose_v(L)
                pe.wait_ge(s["vtok_ready"], L["vt"] + 4)
                softmax_heads(L)
                r = L["multis"]
                for seg, (a, b) in enumerate(SEGMENTS):
                    pe.wait_ge(s["on_sq"], 8 * r + b)
                    if seg >= 2:
                        pe.wait_ge(s["on_std"], 3 * r + seg - 1)
                    for n in range(a, b):
                        last = mm(B[6 + seg % 2][:, S:2 * S], T("ones"), sq[:, n, :], start=(n == a), stop=(n == b - 1))
                    last.then_inc(s["on_sum"], 1)
                out_proj(L, 24, x_split[2])

            for L in plan:
                norm(L["part"])
                dict(ffn=ffn, stick=stick, dsa=dsa, multi=multi, rwkv=lambda L: rwkv_pe(pe, L, product, project, transpose_v, out_proj))[L["kind"]](L)

        @block.scalar
        def _(act):
            A = nc.scalar.activation
            step = Steps(act, s["act_step"])
            act.wait_ge(s["const_loaded"], 16 * N_CONST)

            def hi(L, n, i=0, skipped=0):
                u = L["u"] + n
                act.wait_ge(a_loaded[u % 4], i * 16 + 16 * (u // 4 + 1))
                if u >= 4 or not isinstance(i, int) or i:
                    act.wait_ge(s["a_used"], i * 4 + (u - 3))
                A(w_split[:, u % 4, 0, :], ring_a[:, u % 4, :], ACT.Copy).then_inc(s["w_hi"], 1)

            def norm(L):
                m = L["part"]
                after_mixer = m and plan[m - 1]["kind"] != "ffn"
                if m and not after_mixer:
                    for n in range(early(L)):
                        hi(L, n)
                for k in range(KT):
                    act.wait_ge(s["x_added"], 8 * m + k + 1)
                    A(sq[:, k, :], xT[:, k, :], ACT.Square).then_inc(s["sq_ready"], 1)
                    if after_mixer and 4 <= k < 4 + early(L):
                        hi(L, k - 4)
                act.wait_ge(s["ssum_ready"], m + 1)
                A(small_std, norm_bank(m)[:, 0:S], ACT.Sqrt, bias=T("eps"), scale=1.0 / D).then_inc(s["std_ready"], 1)
                if m == 0:
                    for n in range(early(L)):
                        hi(L, n)

                if L["kind"] != "rwkv":
                    for k in range(KT):
                        act.wait_ge(s["h_raw"], 8 * m + k + 1)
                        A(h_split[:, 0, k, :], hT[:, k, :], ACT.Copy).then_inc(s["h_hi"], 1)

            small_std = work[:, 7, :]

            def ffn(L):
                f, u = L["d"] // FT, L["u"]

                def tile_pair(i, final):
                    for q in range(2):
                        if not (final and q):
                            for g in range(2):
                                n = 2 * q + g + 2
                                hi(L, n, i)
                        act.wait_ge(d_loaded[q], i * 16 + 16 * (L["d"] // 2 + 1))
                        if f or not isinstance(i, int) or i:
                            act.wait_ge(s["d_used"], i * 2 + (L["d"] + q - 1))
                        A(d_split[:, q, 0, :], ring_d[:, q, :], ACT.Copy).then_inc(s["dn_hi"], 1)
                        if L["idx"] < 4:
                            act.wait_ge(s["a_used"], i * 4 + (u + 2 * q + 2))
                            A(work[:, 2 + q, :], B[4 + q][:, 0:S], ACT.Silu).then_inc(s["silu_ready"], 1)
                        else:
                            act.wait_ge(s["conv_ready"], i * 2 + (FT * L["convs"] + q + 1))
                            A(work[:, 2 + q, :], work[:, 4 + q, :], ACT.Gelu).then_inc(s["silu_ready"], 1)
                        act.wait_ge(s["act_raw"], i * 2 + (FT * f + q + 1))
                        A(act_split[:, q, 0, :], work[:, q, :], ACT.Copy).then_inc(s["act_hi"], 1)
                tile_pair(0, False)
                with act.Fori(1, FT // 2 - 1) as i:
                    tile_pair(i, False)
                tile_pair(FT // 2 - 1, True)

            def evac(L, first, count, mixed=None):
                u, p = L["u"] + first, first

                def four_units(i):
                    for j in range(4):
                        hi(L, first + j + AHEAD, i)
                        if mixed is not None:
                            xm_hi(L, mixed, i, j)
                        act.wait_ge(s["a_used"], i * 4 + (u + j + 1))
                        A(qkv[:, ds(i * 4 + (first + j), 1), :], B[4 + j][:, 0:S], ACT.Copy)\
                            .then_inc(s["proj_evac"], 1)
                peeled = u == 0
                if peeled:
                    four_units(0)
                with act.Fori(int(peeled), count // 4) as i:
                    four_units(i)

            def xm_hi(L, group, i, j):
                act.wait_ge(s["xm_raw"], i * 4 + (48 * L["rw"] + 8 * group + j + 1))
                if group >= 3:
                    act.wait_ge(s["a_used"], L["u"] + (8, 16, 25)[group - 3])
                t = x_split[group % 3][:, 0, :, :]
                A(t[:, ds(i * 4 + j, 1), :] if not isinstance(i, int) else t[:, i * 4 + j, :], work[:, j, :],
                  ACT.Copy).then_inc(s["xm_hi"], 1)

            def o_hi(L, n, x, ready):
                ready(n)
                A(x[:, 0, n, :], oT[:, n, :], ACT.Copy).then_inc(s["o_hi"], 1)

            def out_split(L, first, x, ready):
                for n in range(KT):
                    ready(n)
                    A(x[:, 0, n, :], oT[:, n, :], ACT.Copy).then_inc(s["o_hi"], 1)
                    if n in (2, 4, 6):
                        hi(L, first + n // 2 - 1)
                for n in range(3, KT):
                    hi(L, first + n)

            def evac_one(L, n, row):
                act.wait_ge(s["a_used"], L["u"] + n + 1)
                A(qkv[:, row, :], B[4 + n % 4][:, 0:S], ACT.Copy).then_inc(s["proj_evac"], 1)

            def stick(L):
                evac(L, 0, 20)
                hi(L, 23)
                for n in range(20, 24):
                    evac_one(L, n, n)
                O = L["pairs"]

                def softplus_log(h):
                    act.wait_ge(s["zm_ready"], h + 1)
                    e = work[:, 2 * (h % 2):2 * (h % 2) + 2, :].rearrange("p a b -> p (a b)")[:, 0:384]
                    if h >= 2:
                        act.wait_ge(s["ln_ready"], h - 1)
                    step.did(A(e, zm_(h), ACT.Abs))
                    step.settle()
                    step.did(A(e, e, ACT.Exp, scale=-1.0))
                    if h >= 2:
                        act.wait_ge(s["sp_ready"], h - 1)
                    step.settle()
                    A(ln_(h), e, ACT.Ln, bias=1.0).then_inc(s["ln_ready"], 1)

                def weights(h):
                    act.wait_ge(s["lg_ready"], h + 1)
                    if h >= 2:
                        act.wait_ge(s["pv_done"], h - 1 + 2 * O)
                    A(planes[:, 3, (h % 2) * 512:(h % 2) * 512 + 384], lg_(h), ACT.Exp).then_inc(s["p_ready"], 1)

                def pair(t):
                    act.wait_ge(s["pv_done"], 2 * O + 2 * t + 2)
                    A(oT[:, t, :], B[4 + t % 2][:, 0:S], ACT.Copy).then_inc(s["ot_evac"], 1)

                for t in range(NH + 4):
                    if t < NH:
                        softplus_log(t)
                    if 0 <= t - 2 < NH:
                        weights(t - 2)
                    if t >= 4 and (t - 4) % 2 == 1:
                        pair((t - 4) // 2)
                act.wait_ge(s["ot_evac"], O + 8)
                out_split(L, 24, x_split[2], lambda n: None)

            def norm_rope_in(L, n, row, gain):
                g = L["tiles"] + n
                if gain is None:
                    return
                if n == 0:
                    act.wait_ge(s["proj_evac"], L["proj"] + 16)
                if n >= 2:
                    act.wait_ge(s["qk_ready"], g - 1)
                A(work[:, n % 2, :], qkv[:, row, :], ACT.Square)
                A(work[:, 2 + n % 2, :], qkv[:, row, :], ACT.Copy, scale=V(gain, row)).then_inc(s["nr_in"], 1)

            def norm_rope_std(L, n):
                act.wait_ge(s["nr_mm"], L["tiles"] + n + 1)
                A(work[:, 4 + n % 2, :], B[2 + n % 2][:, 0:S], ACT.Sqrt, bias=T("eps")).then_inc(s["nr_std"], 1)

            def softmax_heads(L):
                H, O = L["heads"], L["pairs"]

                def exps(h):
                    act.wait_ge(s["nmx_ready"], H + h + 1)
                    for qt in range(NT):
                        last = A(planes[:, 0, (h % 4) * 512 + qt * S:(h % 4) * 512 + (qt + 1) * S],
                                 planes[:, 1, (h % 2) * 512 + qt * S:(h % 2) * 512 + (qt + 1) * S], ACT.Exp,
                                 bias=small[:, 2 * (h % 2) + qt:2 * (h % 2) + qt + 1],
                                 accum_out=small[:, 4 + 2 * (h % 2) + qt:5 + 2 * (h % 2) + qt])
                    last.then_inc(s["e_ready"], 1)

                def copy_turned(h):
                    act.wait_ge(s["t_done"], H + h + 1)
                    if h >= 2:
                        act.wait_ge(s["pv_done"], 2 * O + h - 1)
                    A(planes[:, 2, (h % 2) * 512:(h % 2 + 1) * 512], B[2 + h % 2][:, :], ACT.Copy)\
                        .then_inc(s["pt_ready"], 1)

                def pair(t):
                    act.wait_ge(s["pv_done"], 2 * O + 2 * t + 2)
                    A(oT[:, t, :], B[4 + t % 2][:, 0:S], ACT.Copy).then_inc(s["ot_evac"], 1)

                for t in range(NH + 4):
                    if t < NH:
                        exps(t)
                    if 0 <= t - 2 < NH:
                        copy_turned(t - 2)
                    if t >= 4 and (t - 4) % 2 == 1:
                        pair((t - 4) // 2)

            def dsa(L):
                evac(L, 0, 16)
                for n in range(16, 20):
                    hi(L, n + AHEAD)
                    evac_one(L, n, n + 8)
                hi(L, 20 + AHEAD)
                evac_one(L, 20, 28)
                hi(L, 21 + AHEAD)
                act.wait_ge(s["a_used"], L["u"] + 22)
                A(small[:, 16:32], B[5][:, 0:16], ACT.Copy,
                  scale=IDX_HEADS ** -0.5 * HD ** -0.5).then_inc(s["proj_evac"], 1)
                for j in range(8):
                    if 22 + j + AHEAD < 30:
                        hi(L, 22 + j + AHEAD)
                    tiles = range(3 * j, min(3 * j + 3, 21))
                    for n in tiles:
                        norm_rope_in(L, n, n, "gain0" if n < 16 else None)
                        if n == 3 * j + 1:
                            evac_one(L, 22 + j, 16 + j)
                        if n < 16:
                            norm_rope_std(L, n)
                    if not len(tiles) > 1:
                        evac_one(L, 22 + j, 16 + j)
                for i in range(IDX_HEADS):
                    act.wait_ge(s["idx_mm"], i + 1)
                    if i >= 2:
                        act.wait_ge(s["idx_added"], i - 1)
                    A(planes[:, 1, (i % 2) * 512:(i % 2 + 1) * 512], B[i % 2][:, :], ACT.Relu)\
                        .then_inc(s["idx_relu"], 1)
                softmax_heads(L)
                act.wait_ge(s["ot_evac"], L["pairs"] + 8)
                out_split(L, 30, x_split[2], lambda n: None)

            def multi(L):
                evac(L, 0, 16)
                gain = f"gain{1 + L['idx']}"
                for j in range(8):
                    if 16 + j + AHEAD < 24:
                        hi(L, 16 + j + AHEAD)
                    norm_rope_in(L, 2 * j, 2 * j, gain)
                    norm_rope_in(L, 2 * j + 1, 2 * j + 1, gain)
                    evac_one(L, 16 + j, 16 + j)
                    norm_rope_std(L, 2 * j)
                    norm_rope_std(L, 2 * j + 1)
                softmax_heads(L)
                r = L["multis"]
                act.wait_ge(s["ot_evac"], L["pairs"] + 8)
                for n in range(KT):
                    A(sq[:, n, :], oT[:, n, :], ACT.Square).then_inc(s["on_sq"], 1)
                for seg, (a, b) in enumerate(SEGMENTS):
                    act.wait_ge(s["on_sum"], 3 * r + seg + 1)
                    A(work[:, seg, :], B[6 + seg % 2][:, S:2 * S], ACT.Sqrt, bias=T("eps"),
                      scale=1.0 / ((b - a) * P)).then_inc(s["on_std"], 1)
                out_split(L, 24, x_split[2], lambda n: act.wait_ge(s["on_ready"], 8 * r + n + 1))

            for L in plan:
                norm(L)
                dict(ffn=ffn, stick=stick, dsa=dsa, multi=multi,
                     rwkv=lambda L: rwkv_act(act, L, A, evac, xm_hi, out_split))[L["kind"]](L)

        @block.vector
        def _(dve):
            v = nc.vector
            step = Steps(dve, s["dve_step"])
            dve.wait_ge(s["const_loaded"], 16 * N_CONST)
            dve.wait_ge(s["x_loaded"], 16)
            v.memset(small[:, 48:49], 0.0).then_inc(s["x_added"], 8)
            v.memset(small[:, 41:42], 0.0).then_inc(s["proj_evac"], 4)

            def lo(L, n, i=0, skipped=0):
                u = L["u"] + n
                dve.wait_ge(s["w_hi"], i * 4 + (L["us"] + n - skipped + 1))
                v.tensor_tensor(w_split[:, u % 4, 1, :], ring_a[:, u % 4, :], w_split[:, u % 4, 0, :].bitcast(f32),
                                ALU.subtract).then_inc(s["w_lo"], 1)

            def lo_loop(L, count):
                with dve.Fori(0, count // 4) as i:
                    for j in range(4):
                        lo(L, j + AHEAD, i)

            def out_split(L, first, x, skipped=0):
                for n in range(KT):
                    dve.wait_ge(s["o_hi"], 8 * L["mixers"] + n + 1)
                    v.tensor_tensor(x[:, 1, n, :], oT[:, n, :], x[:, 0, n, :].bitcast(f32), ALU.subtract)\
                        .then_inc(s["o_ready"], 1)
                    if n in (3, 5, 7):
                        lo(L, first + (n - 3) // 2, 0, skipped)

            def norm(L, gain):
                m = L["part"]
                dve.wait_ge(s["std_ready"], m + 1)
                r = work[:, 6, :]
                step.did(v.reciprocal(r, work[:, 7, :]))
                step.settle()
                if m == 0:
                    for n in range(early(L)):
                        lo(L, n)
                for k in range(KT + 2):
                    if k < KT:
                        v.scalar_tensor_tensor(out=hT[:, k, :], in0=xT[:, k, :], scalar=V(gain, k), in1=r,
                                               op0=ALU.mult, op1=ALU.mult).then_inc(s["h_raw"], 1)
                    if k >= 2 and L["kind"] != "rwkv":
                        n = k - 2
                        dve.wait_ge(s["h_hi"], 8 * L["hs"] + n + 1)
                        v.tensor_tensor(h_split[:, 1, n, :], hT[:, n, :], h_split[:, 0, n, :].bitcast(f32),
                                        ALU.subtract).then_inc(s["h_ready"], 1)

            def ffn(L):
                f, u, conv = L["d"] // FT, L["u"], L["idx"] >= 4
                if conv:
                    a = VEC[f"conv{L['idx'] - 4}"][0]
                def tile_pair(i, final):
                    for q in range(2):
                        if not (final and q):
                            lo(L, 2 * q + 2, i)
                            lo(L, 2 * q + 3, i)
                        dve.wait_ge(s["dn_hi"], i * 2 + (L["d"] + q + 1))
                        v.tensor_tensor(d_split[:, q, 1, :], ring_d[:, q, :], d_split[:, q, 0, :].bitcast(f32),
                                        ALU.subtract).then_inc(s["dn_lo"], 1)
                        if conv:
                            g, c = B[4 + q], work[:, 4 + q, :]
                            w = [vec[:, ds(i * 8 + (a + 4 * q + j), 1)] if not isinstance(i, int) else
                                 vec[:, a + 8 * i + 4 * q + j:a + 8 * i + 4 * q + j + 1] for j in range(4)]
                            dve.wait_ge(s["a_used"], i * 4 + (u + 2 * q + 2))
                            step.did(v.tensor_scalar(c, g[:, 0:S], w[1], w[3], ALU.mult, ALU.add))
                            step.settle()
                            step.did(v.scalar_tensor_tensor(out=c[:, 1:S], in0=g[:, 0:S - 1], scalar=w[0],
                                                            in1=c[:, 1:S], op0=ALU.mult, op1=ALU.add))
                            step.settle()
                            v.scalar_tensor_tensor(out=c[:, 0:S - 1], in0=g[:, 1:S], scalar=w[2],
                                                   in1=c[:, 0:S - 1], op0=ALU.mult, op1=ALU.add)\
                                .then_inc(s["conv_ready"], 1)
                        dve.wait_ge(s["silu_ready"], i * 2 + (FT * f + q + 1))
                        v.tensor_tensor(work[:, q, :], work[:, 2 + q, :], B[4 + q][:, S:2 * S], ALU.mult)\
                            .then_inc(s["act_raw"], 1)
                        dve.wait_ge(s["act_hi"], i * 2 + (FT * f + q + 1))
                        v.tensor_tensor(act_split[:, q, 1, :], work[:, q, :], act_split[:, q, 0, :].bitcast(f32),
                                        ALU.subtract).then_inc(s["act_ready"], 1)
                tile_pair(0, False)
                with step.repeat(FT // 2 - 2, 4 if conv else 0, 1) as i:
                    tile_pair(i, False)
                tile_pair(FT // 2 - 1, True)
                for n in range(KT):
                    next_lo(L, n)
                dve.wait_ge(s["d_used"], L["d"] + FT)
                for b in range(4):
                    x2 = xT[:, 2 * b:2 * b + 2, :].rearrange("p a b -> p (a b)")
                    v.tensor_tensor(x2, x2, B[b][:, :], ALU.add).then_inc(s["x_added"], 2)

            def tokens_v(L):
                for g in range(4):
                    dve.wait_ge(s["vtok_done"], L["vt"] + g + 1)
                    v.tensor_copy(vtok[:, g // 2, (g % 2) * 512:(g % 2 + 1) * 512], B[g % 2][:, :])\
                        .then_inc(s["vtok_ready"], 1)

            def add_out(L, first, skipped=0):
                for n in range(KT):
                    if n + AHEAD < KT:
                        lo(L, first + n + AHEAD, 0, skipped)
                    dve.wait_ge(s["a_used"], L["u"] + first + n + 1)
                    v.tensor_tensor(xT[:, n, :], xT[:, n, :], B[4 + n % 4][:, 0:S], ALU.add)\
                        .then_inc(s["x_added"], 1)
                    if n >= 4:
                        next_lo(L, n - 4)

            def next_lo(L, n):
                if L["part"] + 1 < PARTS and n < early(plan[L["part"] + 1]):
                    lo(plan[L["part"] + 1], n)

            def stick(L):
                lo_loop(L, 20)
                lo(L, 23)
                tokens_v(L)

                def masked(h):
                    dve.wait_ge(s["z_done"], h + 1)
                    v.scalar_tensor_tensor(out=zm_(h), in0=B[h % 2][:, 0:384], scalar=HD ** -0.5,
                                           in1=T("stick_neg"), op0=ALU.mult, op1=ALU.add).then_inc(s["zm_ready"], 1)

                def softplus(h):
                    dve.wait_ge(s["ln_ready"], h + 1)
                    if h >= 2:
                        dve.wait_ge(s["cum_done"], h - 1)
                    v.scalar_tensor_tensor(out=planes[:, 1, (h % 2) * 512:(h % 2) * 512 + 384], in0=zm_(h),
                                           scalar=0.0, in1=ln_(h), op0=ALU.max, op1=ALU.add)\
                        .then_inc(s["sp_ready"], 1)

                def logit(h):
                    dve.wait_ge(s["cum_done"], h + 1)
                    if h >= 2:
                        dve.wait_ge(s["p_ready"], h - 1)
                    v.tensor_tensor(lg_(h), zm_(h), B[2 + h % 2][:, 0:384], ALU.subtract)\
                        .then_inc(s["lg_ready"], 1)

                for t in range(NH + 2):
                    if t < NH:
                        masked(t)
                    if 0 <= t - 1 < NH:
                        softplus(t - 1)
                    if 0 <= t - 2 < NH:
                        logit(t - 2)
                out_split(L, 24, x_split[2])
                add_out(L, 24)

            def norm_rope(L, n, row, gained, rope):
                g = L["tiles"] + n
                b, r, t1 = B[2 + n % 2], work[:, 4 + n % 2, :], work[:, 6, :]
                x = work[:, 2 + n % 2, :] if gained else qkv[:, row, :]
                dst = qkv[:, row, :]
                dve.wait_ge(s["nr_mm"], g + 1)
                if gained:
                    dve.wait_ge(s["nr_std"], L["heads"] + n + 1)
                    step.did(v.reciprocal(r, r))
                if rope:
                    step.did(v.tensor_tensor(t1, b[:, S:2 * S], T("sin" + rope), ALU.mult))
                    t2 = work[:, 7, :]
                    step.did(v.tensor_tensor(t2, x, T("cos" + rope), ALU.mult))
                    step.settle()
                    if gained:
                        step.did(v.tensor_tensor(t2, t2, t1, ALU.add))
                        step.settle()
                        v.tensor_tensor(dst, t2, r, ALU.mult).then_inc(s["qk_ready"], 1)
                    else:
                        v.tensor_tensor(dst, t2, t1, ALU.add).then_inc(s["qk_ready"], 1)
                else:
                    step.settle()
                    v.tensor_tensor(dst, x, r, ALU.mult).then_inc(s["qk_ready"], 1)
                dve.wait_ge(s["qk_ready"], g + 1)

            def softmax_heads(L, bias):
                H = L["heads"]

                def shifted(h):
                    dve.wait_ge(s["s_done"], H + h + 1)
                    sm = planes[:, 1, (h % 2) * 512:(h % 2 + 1) * 512]
                    if h >= 2:
                        dve.wait_ge(s["e_ready"], H + h - 1)
                    bb = bias(h)
                    if bb is None:
                        v.tensor_scalar(sm, B[h % 2][:, :], HD ** -0.5, None, ALU.mult).then_inc(s["sm_ready"], 1)
                    else:
                        v.scalar_tensor_tensor(out=sm, in0=B[h % 2][:, :], scalar=HD ** -0.5, in1=bb,
                                               op0=ALU.mult, op1=ALU.add).then_inc(s["sm_ready"], 1)
                    dve.wait_ge(s["sm_ready"], H + h + 1)
                    v.tensor_reduce(small[:, 2 * (h % 2):2 * (h % 2) + 2], sm.rearrange("p (a b) -> p a b", a=NT),
                                    AX.X, ALU.max, negate=True).then_inc(s["nmx_ready"], 1)

                def normed(h):
                    dve.wait_ge(s["e_ready"], H + h + 1)
                    r = small[:, 8 + 2 * (h % 2):10 + 2 * (h % 2)]
                    step.did(v.reciprocal(r, small[:, 4 + 2 * (h % 2):6 + 2 * (h % 2)]))
                    step.settle()
                    for qt in range(NT):
                        p_ = planes[:, 0, (h % 4) * 512 + qt * S:(h % 4) * 512 + (qt + 1) * S]
                        last = v.tensor_scalar(p_, p_, r[:, qt:qt + 1], None, ALU.mult)
                    last.then_inc(s["pn_ready"], 1)

                for t in range(NH + 1):
                    if t < NH:
                        shifted(t)
                    if 0 <= t - 1 < NH:
                        normed(t - 1)

            def dsa(L):
                lo_loop(L, 20)
                for j in range(7):
                    if 23 + j < 30:
                        lo(L, 23 + j)
                    for n in range(3 * j, 3 * j + 3):
                        norm_rope(L, n, n if n < 16 else n + 8, n < 16, "0")
                sc = planes[:, 4, 0:512]
                for i in range(IDX_HEADS):
                    dve.wait_ge(s["idx_relu"], i + 1)
                    if i:
                        dve.wait_ge(s["idx_added"], i)
                    for qt in range(NT):
                        cols = slice(qt * S, (qt + 1) * S)
                        last = v.scalar_tensor_tensor(
                            out=sc[:, cols], in0=planes[:, 1, (i % 2) * 512 + qt * S:(i % 2) * 512 + (qt + 1) * S],
                            scalar=small[:, 16 + 8 * qt + i:17 + 8 * qt + i],
                            in1=(T("visible") if i == 0 else sc)[:, cols], op0=ALU.mult, op1=ALU.add)
                    last.then_inc(s["idx_added"], 1)
                tokens_v(L)
                dve.wait_ge(s["idx_added"], IDX_HEADS)
                for _ in range(N_SEL // 8):
                    for qt in range(NT):
                        step.did(v.max(top8[:, 8 * qt:8 * qt + 8], sc[:, qt * S:(qt + 1) * S]))
                    step.settle()
                    for qt in range(NT):
                        row = sc[:, qt * S:(qt + 1) * S]
                        step.did(v.match_replace(row, top8[:, 8 * qt:8 * qt + 8], row, TAKEN))
                    step.settle()
                step.did(v.tensor_scalar(sc, sc, TAKEN / 2, NEG, ALU.is_gt, ALU.mult))
                step.settle()
                softmax_heads(L, lambda h: sc)
                out_split(L, 30, x_split[2])
                add_out(L, 30)

            top8 = planes[:, 4, 512:528]

            def multi(L):
                r = L["multis"]
                lo_loop(L, 16)
                for j in range(8):
                    if 19 + j < 24:
                        lo(L, 19 + j)
                    for n in (2 * j, 2 * j + 1):
                        norm_rope(L, n, n, True, (None, None, "1", "1", "1", "2", "2", "2")[n % 8])
                tokens_v(L)
                dve.wait_ge(s["na_loaded"], 16 * (r + 1))

                def bias(h):
                    if h < 4:
                        return planes[:, 5, h * 512:(h + 1) * 512]
                    return T("dilated") if h < 10 else None
                softmax_heads(L, bias)
                for seg, (a, b) in enumerate(SEGMENTS):
                    dve.wait_ge(s["on_std"], 3 * r + seg + 1)
                    step.did(v.reciprocal(work[:, 3 + seg, :], work[:, seg, :]))
                    step.settle()
                    for n in range(a, b):
                        v.scalar_tensor_tensor(out=oT[:, n, :], in0=oT[:, n, :], scalar=V(f"out_g{L['idx']}", n),
                                               in1=work[:, 3 + seg, :], op0=ALU.mult, op1=ALU.mult)\
                            .then_inc(s["on_ready"], 1)
                out_split(L, 24, x_split[2])
                add_out(L, 24)

            for L in plan:
                norm(L, f"ffn_g{L['idx']}" if L["kind"] == "ffn" else f"mix_g{MIXER_GAIN[L['kind'], L['idx']]}")
                dict(ffn=ffn, stick=stick, dsa=dsa, multi=multi,
                     rwkv=lambda L: rwkv_dve(dve, L, v, step, lo, tokens_v, out_split, add_out))[L["kind"]](L)

        @block.gpsimd
        def _(pool):
            pstep = Steps(pool, s["pool_step"])
            pool.wait_ge(s["const_loaded"], 16 * N_CONST)
            for L in plan:
                if L["kind"] == "rwkv":
                    rwkv_pool(pool, L, pstep)
                if L["kind"] == "multi":
                    pool.wait_ge(s["h_ready"], 8 * (L["hs"] + 1))
                    pool.dma_start(planes[:, 5, :], na_in[L["idx"], :, :]).then_inc(s["na_loaded"], 16)


SEGMENTS = [(0, 2), (2, 5), (5, 8)]
MIXER_GAIN = {("rwkv", 0): 0, ("stick", 0): 1, ("dsa", 0): 2, ("rwkv", 1): 3, ("multi", 0): 4, ("multi", 1): 5}


def constants():
    t = np.zeros((P, TAB_W), np.float32)

    def put(name, a):
        o, w = TAB[name]
        t[:, o:o + w] = a
    i = np.arange(P)
    put("ident", np.eye(P))
    put("ones", 1.0)
    put("tri", i[:, None] >= i[None, :])
    same = i[:, None] // HD == i[None, :] // HD
    put("head_ones", same)
    put("head_mean", same / HD)

    def rotation(half, base_rows):
        m = np.zeros((P, P), np.float32)
        for o in base_rows:
            for d in range(half):
                m[o + d + half, o + d] = -1.0
                m[o + d, o + d + half] = 1.0
        return m
    put("rot0", rotation(32, [0, 64]))
    put("rot1", rotation(8, [0, 64]))
    put("rot2", rotation(16, [0, 32, 64, 96]))
    pos = np.arange(S).astype(np.float32)

    def inv(theta, dim):
        f = np.float32
        return (f(theta) ** (-np.arange(0, dim, 2, dtype=f) / f(dim))).astype(f)
    half = np.arange(32, dtype=np.float32) / np.float32(32)
    ang0 = pos[None, :] * (np.float32(1.0) / (np.float32(10000.0) ** half)).astype(np.float32)[:, None]
    d = i % HD
    put("cos0", np.cos(ang0)[d % 32])
    put("sin0", np.sin(ang0)[d % 32])
    ang1 = pos[None, :] * inv(500000.0, 16)[:, None]
    put("cos1", np.where((d < 16)[:, None], np.cos(ang1)[d % 8], 1.0))
    put("sin1", np.where((d < 16)[:, None], np.sin(ang1)[d % 8], 0.0))
    fr = inv(10000.0, 32)
    ang_r = (pos // GRID_W)[None, :] * fr[:, None]
    ang_c = (pos % GRID_W)[None, :] * fr[:, None]
    put("cos2", np.where((d < 32)[:, None], np.cos(ang_r)[d % 16], np.cos(ang_c)[d % 16]))
    put("sin2", np.where((d < 32)[:, None], np.sin(ang_r)[d % 16], np.sin(ang_c)[d % 16]))
    q = np.arange(S)
    ok = np.concatenate([i[:, None] < q[None, :], i[:, None] < i[None, :]], 1)
    put("stick_neg", np.where(ok, 0.0, NEG))
    qq = (np.arange(NT)[None, :, None] * P + i[:, None, None])
    vis = q[None, None, :] < (qq // CH + 1) * CH
    put("visible", np.where(vis, 0.0, NEG).reshape(P, -1))
    delta = np.abs(q[None, None, :] - qq)
    count = sum(((delta % dd == 0) & (delta // dd <= (w // 2) // dd)).astype(np.int64)
                for w, dd in ((128, 1), (512, 4), (2048, 16)))
    put("dilated", np.where(count > 0, np.log(np.maximum(count, 1)), NEG).reshape(P, -1))
    put("scan_keep", np.where(q % P == 0, 0.0, 1.0)[None, :])
    strict, incl = i[:, None] < i[None, :], i[:, None] <= i[None, :]
    put("rw_mask", np.concatenate([strict, incl, incl], 1))
    put("eps", EPS)
    put("gn_eps", GN_EPS)
    for lv in range(7):
        n = 1 << lv
        blk = ((i[:, None] // (2 * n) == i[None, :] // (2 * n)) & ((i[:, None] // n) % 2 == 1)
               & ((i[None, :] // n) % 2 == 0))
        put(f"level{lv}", np.eye(P) - blk)
        if lv == 0:
            put("level0t", np.eye(P) - blk.T)
    return t


def cols(vv):
    return np.asarray(vv).reshape(-1, P).T


def blocks(w):
    w = np.asarray(w)
    n = w.shape[1] // P
    return w.reshape(KT, P, n, P).transpose(2, 1, 0, 3).reshape(n, P, KT * P)


def padded(w, n):
    return np.concatenate([w, np.zeros((w.shape[0], n - w.shape[1]), w.dtype)], 1)


def layout(layers, I):
    A, Dn = [], []
    for kind, idx in layers:
        if kind == "ffn":
            gu = I["ffn_w_gu"][idx] if idx < 4 else I["w_gate_up_2"][idx - 4]
            dn = I["ffn_w_down"][idx] if idx < 4 else I["w_down_2"][idx - 4]
            b = blocks(gu)
            A.append(np.stack([b[:FT], b[FT:]], 1).reshape(2 * FT, P, D))
            Dn.append(dn.reshape(FT, P, D))
        elif kind == "stick":
            A += [blocks(I["sb_w_qkv"][0]), blocks(I["sb_w_out"][0])]
        elif kind == "dsa":
            w = I["ds_w_in"][0]
            q, k, vv, qi, ki, wi = np.split(w, [D, 2 * D, 3 * D, 3 * D + 512, 3 * D + 576], 1)
            A += [blocks(q), blocks(k), blocks(qi), blocks(np.concatenate([ki, ki], 1)), blocks(padded(wi, P)),
                  blocks(vv), blocks(I["ds_w_out"][0])]
        elif kind == "multi":
            w = I["w_in_2"][idx]
            qa, ka, va, qd, kd, vd, qc, kc, vc = np.split(
                w, np.cumsum([256, 256, 256, 384, 384, 384, 384, 128]).tolist(), 1)

            def spread(t):
                return np.concatenate([t[:, HD * (h // 3):HD * (h // 3) + HD] for h in range(6)], 1)
            A += [blocks(np.concatenate([qa, qd, qc, ka, kd, spread(kc), va, vd, spread(vc)], 1)),
                  blocks(I["w_out_2"][idx])]
        elif kind == "rwkv":
            w = I["rw_w_rkv"][idx]
            v1 = I["rw_v1"][0] if idx else np.zeros((D, LORA_V), np.float32)
            v2 = I["rw_v2"][0] if idx else np.zeros((LORA_V, D), np.float32)
            g1, g2 = I["rw_g1"][idx], I["rw_g2"][idx]
            last = np.concatenate([g2[P:], v2, np.zeros((64, D), np.float32)], 0)
            A += [blocks(w[0]), blocks(w[1]), blocks(w[2]),
                  blocks(padded(np.concatenate([g1[:, P:], v1], 1), P)), blocks(g1[:, :P]),
                  blocks(np.concatenate([I["rw_w1"][idx], I["rw_a1"][idx]], 1)),
                  np.concatenate([I["rw_w2"][idx], I["rw_a2"][idx]], 0)[None], g2[None, :P], last[None],
                  blocks(I["rw_w_out"][idx])]
    wa = np.concatenate(A, 0)
    wd = np.concatenate(Dn, 0) if Dn else np.zeros((1, P, D), np.float32)
    vec = np.zeros((P, VEC_W), np.float32)

    def put(name, a):
        o, w = VEC[name]
        vec[:, o:o + w] = a
    for l in range(4):
        put(f"mix_g{l}", cols(I["norm_mix"][l]))
        put(f"ffn_g{l}", cols(I["norm_ffn"][l]))
    for l in range(2):
        put(f"mix_g{4 + l}", cols(I["norm1_g_2"][l]))
        put(f"ffn_g{4 + l}", cols(I["norm2_g_2"][l]))
        put(f"out_g{l}", cols(I["out_norm_g_2"][l]))
        cw = np.concatenate([I["conv_w_2"][l], I["conv_b_2"][l][None]], 0)
        put(f"conv{l}", cw.reshape(4, FT, P).transpose(2, 1, 0).reshape(P, 4 * FT))
        for j in range(6):
            put(f"mix{j}_{l}", cols(I["rw_mix"][l, j]))
        for n, key in (("w0", "rw_w0"), ("a0", "rw_a0"), ("k_k", "rw_k_k"), ("k_a", "rw_k_a"), ("ln_w", "rw_ln_w"),
                       ("ln_b", "rw_ln_b")):
            put(f"{n}_{l}", cols(I[key][l]))
        put(f"r_k_{l}", cols(I["rw_r_k"][l].reshape(-1)))
        qg, kg = I["q_norm_g_2"][l], I["k_norm_g_2"][l]
        fam = [0, 0, 1, 1, 1, 2, 2, 2]
        g = [np.concatenate([t[m], t[m]]) for t in (qg, kg) for m in fam] + [np.ones(P, np.float32)] * 8
        put(f"gain{1 + l}", np.stack(g, 1))
    put("v0_", cols(I["rw_v0"][0]))
    g = [np.concatenate([I[t][0]] * 2) for t in ("ds_q_norm", "ds_k_norm") for _ in range(8)]
    put("gain0", np.stack(g + [np.ones(P, np.float32)] * 8, 1))
    t = np.arange(S)
    r, c = t // GRID_W, t % GRID_W
    c0 = np.clip(c - NA_KW // 2, 0, GRID_W - NA_KW)
    inside = (c[None, :] >= c0[:, None]) & (c[None, :] < c0[:, None] + NA_KW)
    dr = r[None, :] - r[:, None] + NA_KH - 1
    dc = np.clip(c[None, :] - c[:, None] + NA_KW - 1, 0, 2 * NA_KW - 2)
    b = np.where(inside[None, None], I["rpb_2"][:, :, dr, dc], np.float32(NEG))
    na = b.reshape(2, 4, NT, P, S).transpose(0, 3, 1, 2, 4).reshape(2, P, 4 * NT * S)
    x = I["x"][0].T.reshape(KT, P, S).transpose(1, 0, 2)
    c_ = np.ascontiguousarray
    return dict(x=c_(x), wa=c_(wa), wd=c_(wd), tab=constants(), vec=vec, na=c_(na.astype(np.float32)))


def kernel(**inputs):
    import concourse.bacc as bacc
    from concourse.bass_utils import run_bass_kernel_spmd
    nc = bacc.Bacc("TRN2", target_bir_lowering=False, num_devices=1)
    arrays = layout(FULL, {k: np.asarray(a) for k, a in inputs.items()})
    args = {n: nc.dram_tensor(n, a.shape, mybir.dt.from_np(a.dtype), kind="ExternalInput").ap()
            for n, a in arrays.items()}
    out = nc.dram_tensor("out", (P, KT, S), mybir.dt.float32, kind="ExternalOutput").ap()
    build_program(nc, FULL, args["x"], args["wa"], args["wd"], args["tab"], args["vec"], args["na"], out)
    r = run_bass_kernel_spmd(nc, [arrays], core_ids=[0])
    y = r.results[0]["out"]
    return np.ascontiguousarray(y.transpose(1, 0, 2).reshape(D, S).T)[None]
```

```python
import numpy as np
import concourse.bass as bass
from concourse import mybir
from contextlib import ExitStack, contextmanager

D, S, P = 1024, 256, 128
KT = D // P
NT = S // P
NH, HD = 16, 64
F_FF = 2816
FT = F_FF // P
CH = 64
N_SEL, IDX_HEADS = 64, 8
GRID_W, NA_KW, NA_KH = 64, 16, 8
EPS, GN_EPS = 1e-6, 64e-5
KAPPA = float(np.exp(-0.5))
NEG = -1e30
TAKEN = -3e38
LORA_W, LORA_A, LORA_V, LORA_G = 64, 64, 32, 160

FULL = [("rwkv", 0), ("ffn", 0), ("stick", 0), ("ffn", 1), ("dsa", 0), ("ffn", 2), ("rwkv", 1), ("ffn", 3),
        ("multi", 0), ("ffn", 4), ("multi", 1), ("ffn", 5)]
PROJ = {"rwkv": 24, "stick": 24, "dsa": 30, "multi": 24}
UNITS = {"rwkv": 38, "stick": 32, "dsa": 38, "multi": 32, "ffn": 44}

TAB = {}
_at = 0
for _n, _w in [("ones", P), ("eps", 1), ("gn_eps", 1), ("ident", P), ("tri", P), ("head_ones", P), ("head_mean", P),
               ("rot0", P), ("rot1", P), ("rot2", P), ("cos0", S), ("sin0", S), ("cos1", S), ("sin1", S),
               ("cos2", S), ("sin2", S), ("stick_neg", 3 * P), ("visible", 2 * S), ("dilated", 2 * S),
               ("scan_keep", S), ("rw_mask", 3 * P), ("head_sum", 32), ("head_avg", 32), ("head_back", P),
               ("level0t", P)] \
        + [(f"level{i}", P) for i in range(7)]:
    TAB[_n] = (_at, _w)
    _at += _w
TAB_W = _at
FIRST_W = TAB["ident"][0]
VEC = {}
_at = 0
for _n, _w in ([(f"mix_g{i}", KT) for i in range(6)] + [(f"ffn_g{i}", KT) for i in range(6)]
               + [(f"{v}{j}", KT) for j in range(2) for v in
                  ("mix0_", "mix1_", "mix2_", "mix3_", "mix4_", "mix5_", "w0_", "a0_", "k_k_", "k_a_", "r_k_",
                   "ln_w_", "ln_b_")]
               + [("v0_", KT)] + [(f"gain{i}", 24) for i in range(3)] + [(f"out_g{i}", KT) for i in range(2)]
               + [(f"conv{i}", 4 * FT) for i in range(2)]):
    VEC[_n] = (_at, _w)
    _at += _w
VEC_W = _at


AHEAD = 3


def early(L):
    return 2 if L["kind"] == "ffn" else AHEAD


class Steps:

    def __init__(self, eng, sem):
        self.eng, self.sem, self.n, self.off = eng, sem, 0, 0

    def did(self, ins):
        ins.then_inc(self.sem, 1)
        self.n += 1

    def settle(self):
        self.eng.wait_ge(self.sem, self.off + self.n)

    @contextmanager
    def repeat(self, count, per, first=0):
        with self.eng.Fori(first, first + count) as i:
            before, self.off = self.n, i * per - first * per
            yield i
            assert self.n - before == per, (self.n - before, per)
        self.n, self.off = before + count * per, 0


def rope_of(kind, n):
    return "0" if kind == "dsa" else (None, None, "1", "1", "1", "2", "2", "2")[n % 8]


def ropes_until(kind, n):
    return sum(rope_of(kind, m) is not None for m in range(n + 1))


def tiles_after(kind, n):
    tiles, units = (21, PROJ[kind]) if kind == "dsa" else (16, PROJ[kind])
    return range(*(min(tiles, tiles * max(0, m - 3) // (units - 4)) for m in (n, n + 1)))


def row_of(kind, n):
    if kind != "dsa" or n < 16:
        return n
    return n + 8 if n < 21 else n - 6


def plan_layers(layers):
    out, u, dn, proj, part, vt, heads, pairs = [], 0, 0, 4, 0, 0, 0, 0
    tiles = us = ropes = 0
    for kind, idx in layers:
        out.append(dict(kind=kind, idx=idx, u=u, us=us, d=dn, proj=proj, part=part, vt=vt, heads=heads, pairs=pairs,
                        tiles=tiles, ropes=ropes, rw=sum(o["kind"] == "rwkv" for o in out),
                        mixers=sum(o["kind"] != "ffn" for o in out),
                        hs=sum(o["kind"] != "rwkv" for o in out),
                        convs=sum(o["kind"] == "ffn" and o["idx"] >= 4 for o in out),
                        multis=sum(o["kind"] == "multi" for o in out)))
        u += UNITS[kind]
        us += UNITS[kind] - (3 if kind == "rwkv" else 0)
        part += 1
        if kind == "ffn":
            dn += FT
        else:
            proj += PROJ[kind]
            vt += 4
        if kind in ("dsa", "multi"):
            heads += NH
            tiles += 21 if kind == "dsa" else 16
            ropes += 21 if kind == "dsa" else 12
        if kind in ("stick", "dsa", "multi"):
            pairs += NH // 2
    return out, u, dn


def build_program(nc, layers, x_in, wa, wd, tab_in, vec_in, na_in, out):
    f32 = mybir.dt.float32
    ALU, ACT, AX = mybir.AluOpType, mybir.ActivationFunctionType, mybir.AxisListType
    ds = bass.ds
    plan, n_units, n_downs = plan_layers(layers)
    PARTS = len(plan)
    ctx = ExitStack()
    with ctx:
        def sb(name, shape):
            return ctx.enter_context(nc.sbuf_tensor(name, shape, f32))

        xT = sb("xT", [P, KT, S])
        hT = sb("hT", [P, KT, S])
        sq = sb("sq", [P, KT, S])
        qkv = sb("qkv", [P, 29, S])
        vtok = sb("vtok", [P, NT, D])
        oT = sb("oT", [P, KT, S])
        end_oT = nc.sbuf_base
        ring_a = sb("ring_a", [P, 4, D])
        ring_d = sb("ring_d", [P, 2, D])
        tab = sb("tab_sb", [P, TAB_W])
        vec = sb("vec_sb", [P, VEC_W])
        planes = sb("planes", [P, 8, KT * S])
        end_planes = nc.sbuf_base
        v_first = sb("v_first", [P, KT, S])
        dec = sb("dec", [P, KT, 2, P + 1])
        work = sb("work", [P, 8, S])
        small = sb("small", [P, 64])

        f32r = mybir.dt.float32r
        PLANE = KT * S * 4

        def split(name, shape, offset):
            return nc.alloc_sbuf_tensor_at(name, shape, f32r, offset=offset)
        at_planes, at_vtok = end_planes - 8 * PLANE, end_oT - 2 * PLANE
        w_split = split("w_split", [P, 4, 2, D], at_planes)
        d_split = split("d_split", [P, 2, 2, D], at_planes + 4 * PLANE)
        act_split = split("act_split", [P, 2, 2, S], at_planes + 6 * PLANE)
        x_split = [split("h_split", [P, 2, KT, S], at_vtok),
                   split("x_split1", [P, 2, KT, S], at_planes + 4 * PLANE),
                   split("o_split", [P, 2, KT, S], at_planes + 6 * PLANE)]
        h_split = x_split[0]
        rw_o_split = split("rw_o_split", [P, 2, KT, S], end_oT - 2 * PLANE - 29 * S * 4)

        def T(name):
            a, w = TAB[name]
            return tab[:, a:a + w]

        def V(name, k=None):
            a, w = VEC[name]
            return vec[:, a:a + w] if k is None else vec[:, ds(k + a, 1)] if not isinstance(k, int) \
                else vec[:, a + k:a + k + 1]

        B = [ctx.enter_context(nc.psum_tensor(f"bank{i}", [P, 512], f32)) for i in range(8)]

        sems = {}

        for n in ("const_loaded tab_loaded x_loaded x_added sq_ready ssum_ready std_ready h_ready a_used d_used "
                  "silu_ready "
                  "act_ready conv_ready dve_step pool_step act_step proj_evac vtok_done vtok_ready stored "
                  "z_done zm_ready ln_ready sp_ready cum_done lg_ready p_ready pv_done ot_evac "
                  "e_done cos_ready k_padded s_done sm_ready nmx_ready e_ready pn_ready t_done pt_ready "
                  "nr_in nr_mm nr_std qk_ready idx_mm idx_relu idx_added na_loaded "
                  "on_sq on_sum on_std on_ready "
                  "xx_ready xm_ready lora1_ready lora2_mm lora2_ready kk_sq kk_sum kk_std kk_done "
                  "dec_ready rk_ready rk_sum keys_ready kt_mm kt_ready factor_ready score_mm score_ready "
                  "at_mm lt_ready padded turn_mm turned xt_ready lx_mm q_ready xn_mm "
                  "xn_ready rhs_mm rhs_ready u_mm u_ready st_mm st_ready y_mm y_ready "
                  "w_hi w_lo dn_hi dn_lo h_raw h_hi act_raw act_hi xm_raw xm_hi  o_hi o_ready "
                  "kk_inv kk_spread gn_inv gn_scaled gn_spread gn_affine gn_mu gn_c gn_sq gn_var gn_std gn_ready "
                  "ka_ready r_k_ready v_final bonus_ready mid_ready").split():
            sems[n] = ctx.enter_context(nc.semaphore(n))
        a_loaded = [ctx.enter_context(nc.semaphore(f"a_loaded{i}")) for i in range(4)]
        d_loaded = [ctx.enter_context(nc.semaphore(f"d_loaded{i}")) for i in range(2)]
        s = sems

        block = ctx.enter_context(nc.Block())

        def squared(n):
            return planes[:, 6, (n % 4) * S:(n % 4 + 1) * S]

        def gained_(n):
            return planes[:, 7, (n % 4) * S:(n % 4 + 1) * S]

        def root_(n):
            return work[:, n % 4, :]

        def padded_k(L, t):
            m = hT[:, :, :].rearrange("p a b -> p (a b)") if t < 4 else planes[:, 5 if L["kind"] == "dsa" else 4, :]
            return m.rearrange("p (m i n) -> p m i n", m=4, i=2)[:, t % 4, :, :]

        def v_bank(L, g):
            return B[4 + g % 2] if L["kind"] == "multi" else B[g % 2]

        def score_banks(t):
            return (B[0], B[1]) if t % 2 == 0 else (B[6], B[7])

        def slot(p, h):
            return planes[:, p, (h % 4) * 512:(h % 4) * 512 + 384]

        def zm_(h):
            return slot((0, 5)[h // 4 % 2], h)

        def sp_(h):
            return slot(1, h)

        def ln_(h):
            return slot(2, h)

        def p_(h):
            return slot(3, h)

        def lg_(h):
            return slot(4, h)

        def four_heads(g):
            return range(4 * g, 4 * g + 4) if 0 <= g < NH // 4 else ()

        def plane(j):
            return planes[:, j, :].rearrange("p (k t) -> p k t", k=KT)

        def norm_bank(m):
            return B[2] if m and plan[m - 1]["kind"] != "ffn" else B[6]

        CC = NT
        kk_, em, kb, bb, gate, bonus = plane(0), plane(3), plane(4), plane(5), plane(6), plane(7)
        kq = planes[:, 1:3, :].rearrange("p a (k c q t) -> p (a k) c q t", k=KT // 2, c=CC, q=2)
        sc = [qkv[:, 8 * c:8 * c + 8, :].rearrange("p a b -> p (a b)").rearrange("p (i n) -> p i n", i=4)
              for c in range(CC)]
        inv = [qkv[:, 16:24, :].rearrange("p a b -> p (a b)").rearrange("p (m i n) -> p m i n", m=4, i=4),
               planes[:, 3, :].rearrange("p (m i n) -> p m i n", m=4, i=4)]
        X, XT, Q, LT = range(4)
        padded_q = [m.rearrange("p (m i n) -> p m i n", m=4, i=2)
                    for m in (hT[:, :, :].rearrange("p a b -> p (a b)"), planes[:, 0, :])]
        norms = work[:, 2:4, :].rearrange("p a b -> p (a b)")
        kq_rows = planes[:, 1:3, :].rearrange("p a (m x) -> p (a m) x", x=S)
        sqf = sq[:, :, :].rearrange("p a b -> p (a b)")

        def heads_of(g):
            return [(i, 4 * g + i, 2 * g + i // 2, HD * (i % 2)) for i in range(4)]

        def step_no(G, lv, c):
            return (6 * G + lv - 1) * 2 + c + 1

        def chunks(t):
            return t.rearrange("p (c t) -> p c t", c=CC)

        def four(name):
            a, w = TAB[name]
            return tab[:, a:a + w].unsqueeze(1).broadcast_to([P, 4, P])

        def rwkv_pe(pe, L, product, project, transpose_v, out_proj):
            mm, u, r = nc.tensor.matmul, L["u"], L["rw"]
            for j in range(3):
                if j:
                    pe.wait_ge(s["xm_ready"], 48 * r + 8 * (j + 1))
                project(L, 8 * j, 8, x_split[j])

            def loaded(n):
                pe.wait_ge(a_loaded[(u + n) % 4], 16 * ((u + n) // 4 + 1))
                return ring_a[:, (u + n) % 4, :]

            def low(n, dst, m):
                pe.wait_ge(s["w_lo"], L["us"] + n + 1)
                return product(dst[:, 0:S], w_split[:, (u + n) % 4, :, :], x_split[m])
            low(24, B[2], 2)
            pe.wait_ge(s["xm_ready"], 48 * r + 32)
            low(24, B[3], 0).then_inc(s["a_used"], 1)
            low(25, B[1], 0).then_inc(s["a_used"], 1)
            pe.wait_ge(s["xm_ready"], 48 * r + 40)
            low(26, B[0], 1)
            pe.wait_ge(s["xm_ready"], 48 * r + 48)
            pe.wait_ge(s["proj_evac"], L["proj"] + 24)
            low(26, B[4], 2).then_inc(s["a_used"], 1)
            w2a2, g2a, g2v2 = loaded(27), loaded(28), loaded(29)
            pe.wait_ge(s["lora1_ready"], r + 1)
            for n in range(KT):
                p, c = n % 2, slice(n * P, (n + 1) * P)
                if n >= 2:
                    pe.wait_ge(s["lora2_ready"], 8 * r + n - 1)
                mm(B[4 + 2 * p][:, 0:S], w2a2[0:64, c], work[0:64, 4, :], start=True, stop=True)
                mm(B[5 + 2 * p][:, 0:S], w2a2[64:128, c], work[64:128, 4, :], start=True, stop=True)
                mm(B[p][:, 0:S], g2a[:, c], work[:, 5, :], start=True, stop=False)
                last = mm(B[p][:, 0:S], g2v2[0:32, c], work[0:32, 6, :], start=False, stop=True)
                if L["idx"]:
                    last = mm(B[2 + p][:, 0:S], g2v2[32:64, c], work[32:64, 6, :], start=True, stop=True)
                last.then_inc(s["lora2_mm"], 1)
            pe.wait_ge(s["lora2_mm"], 8 * r + 8)
            pe.sem_inc(s["a_used"], 3)
            pe.wait_ge(s["lora2_ready"], 8 * r + 8)
            def gather(n, b, which):
                q = 32 * (n % 4)
                return mm(b[q:q + 32, n // 4 * S:(n // 4 + 1) * S], T(which), sq[:, n, :], start=True, stop=True)

            def spread(n, src):
                q = 32 * (n % 4)
                a = TAB["head_back"][0]
                return mm(B[n % 4][:, 0:S], tab[q:q + 32, a:a + P], src[q:q + 32, n // 4 * S:(n // 4 + 1) * S],
                          start=True, stop=True)
            for n in range(KT):
                pe.wait_ge(s["kk_sq"], 8 * r + n + 1)
                last = gather(n, B[7], "head_sum")
            last.then_inc(s["kk_sum"], 1)
            for n in range(KT):
                pe.wait_ge(s["rk_ready"], 8 * r + n + 1)
                if n >= 3:
                    pe.wait_ge(s["bonus_ready"], 8 * r + n - 2)
                mm(B[4 + n % 3][:, 0:S], T("head_ones"), hT[:, n, :], start=True, stop=True)\
                    .then_inc(s["rk_sum"], 1)
            pe.wait_ge(s["kk_inv"], r + 1)
            for n in range(KT):
                if n >= 4:
                    pe.wait_ge(s["kk_done"], 8 * r + n - 3)
                spread(n, norms).then_inc(s["kk_spread"], 1)
            pe.wait_ge(s["v_final"], 8 * r + 8)
            pe.wait_ge(s["kk_done"], 8 * r + 8)
            transpose_v(L)
            pe.wait_ge(s["keys_ready"], 8 * r + 8)
            pe.wait_ge(s["r_k_ready"], 8 * r + 8)
            pe.wait_ge(s["bonus_ready"], 8 * r + 8)
            for g in range(4):
                if g >= 2:
                    pe.wait_ge(s["kt_ready"], 4 * r + g - 1)
                src = kb if g < 2 else bb
                for i in range(4):
                    last = nc.tensor.transpose(B[2 + g % 2][:, i * P:(i + 1) * P], src[:, 4 * (g % 2) + i, 0:P],
                                               T("ident"))
                last.then_inc(s["kt_mm"], 1)
            pe.wait_ge(s["vtok_ready"], L["vt"] + 4)
            pe.wait_ge(s["kt_ready"], 4 * r + 4)

            def first_step(g):
                G = 4 * r + g
                pe.wait_ge(s["padded"], G + 1)
                for c in range(CC):
                    for t in range(2):
                        last = mm(B[c][:, t * S:(t + 1) * S], bb[:, 2 * g + t, c * P:(c + 1) * P],
                                  padded_q[g % 2][:, 2 * t + c, :, 0:P], start=True, stop=True)
                    last.then_inc(s["at_mm"], 1)

            def level_product(g, lv):
                G = 4 * r + g
                for c in range(CC):
                    if lv == 0:
                        pe.wait_ge(s["lt_ready"], 2 * G + c + 1)
                    elif lv == 1:
                        pe.wait_ge(s["q_ready"], 14 * G + c + 1)
                    else:
                        pe.wait_ge(s["xn_ready"], step_no(G, lv - 1, c))
                    for i in range(4):
                        o = B[c][:, i * P:(i + 1) * P]
                        if lv:
                            last = mm(o, inv[c][:, LT, i, :], inv[c][:, X, i, :], start=True, stop=True)
                        else:
                            last = nc.tensor.transpose(o, inv[c][:, LT, i, :], T("ident"))
                    last.then_inc(s["lx_mm"], 1)
                    if lv > 1:
                        for i in range(4):
                            last = nc.tensor.transpose(B[2 + c][:, i * P:(i + 1) * P], inv[c][:, X, i, :], T("ident"))
                        last.then_inc(s["turn_mm"], 1)

            def level_update(g, lv):
                G = 4 * r + g
                for c in range(CC):
                    pe.wait_ge(s["q_ready"], 14 * G + 2 * lv + c + 1)
                    if lv == 1:
                        pe.wait_ge(s["xt_ready"], 2 * G + c + 1)
                        if g:
                            pe.wait_ge(s["xn_ready"], step_no(G - 1, 6, c))
                    else:
                        pe.wait_ge(s["turned"], 10 * G + 2 * (lv - 2) + c + 1)
                    for i in range(4):
                        a, b = (XT, Q) if lv < 6 else (Q, XT)
                        last = mm(B[2 + c][:, i * P:(i + 1) * P], inv[c][:, a, i, :], inv[c][:, b, i, :],
                                  start=True, stop=True)
                    last.then_inc(s["xn_mm"], 1)

            def scores(g, c, t):
                k = 4 * (4 * r + g) + 2 * c + t
                if c or t:
                    pe.wait_ge(s["score_ready"], k)
                q, cs = padded_q[g % 2][:, 2 * t + c, :, :], slice(c * P, (c + 1) * P)
                mm(B[6][:, :], kb[:, 2 * g + t, cs], q, start=True, stop=True)
                mm(B[7][:, 0:S], bb[:, 2 * g + t, cs], q[:, :, P:2 * P], start=True, stop=True)\
                    .then_inc(s["score_mm"], 1)

            def right(g, c):
                G = 4 * r + g
                pe.wait_ge(s["score_ready"], 4 * G + 2 * c + 2)
                if c:
                    pe.wait_ge(s["st_ready"], G + 1)
                    pe.wait_ge(s["y_ready"], 2 * G + 1)
                elif g:
                    pe.wait_ge(s["y_ready"], 2 * G)
                for i, h, n, po in heads_of(g):
                    b = B[4 + i % 2][:, c * P + (i // 2) * HD:c * P + (i // 2 + 1) * HD]
                    last = mm(b, sc[c][:, i, 0:P], vtok[:, c, h * HD:(h + 1) * HD], start=True, stop=(c == 0))
                    if c:
                        o = (i // 2) * HD
                        last = mm(b, kq[po:po + HD, n, 1, 0, :], work[po:po + HD, 4, o:o + HD],
                                  start=False, stop=True)
                last.then_inc(s["rhs_mm"], 1)

            def solve(g, c):
                G = 4 * r + g
                pe.wait_ge(s["rhs_ready"], 2 * G + c + 1)
                if c == 0:
                    pe.wait_ge(s["score_ready"], 4 * G + 4)
                for i, h, n, po in heads_of(g):
                    o = (i % 2) * P + (i // 2) * HD
                    last = mm(B[6][:, c * S + i * HD:c * S + (i + 1) * HD], sc[c][:, i, 3 * P:4 * P],
                              work[:, c, o:o + HD], start=True, stop=True)
                last.then_inc(s["u_mm"], 1)

            def state(g):
                G = 4 * r + g
                pe.wait_ge(s["u_ready"], 2 * G + 1)
                for i, h, n, po in heads_of(g):
                    b = B[7][po:po + HD, (i // 2) * HD:(i // 2 + 1) * HD]
                    mm(b, sqf[:, n * P + po:n * P + po + HD], vtok[:, 0, h * HD:(h + 1) * HD],
                       start=True, stop=False)
                    last = mm(b, sqf[:, D + n * P + po:D + n * P + po + HD],
                              work[:, 2, i * HD:(i + 1) * HD], start=False, stop=True)
                last.then_inc(s["st_mm"], 1)

            def outputs(g, c):
                G = 4 * r + g
                pe.wait_ge(s["u_ready"], 2 * G + c + 1)
                for i, h, n, po in heads_of(g):
                    b = B[4 + i % 2][po:po + HD, S + (i // 2) * P:S + (i // 2 + 1) * P]
                    mm(b, vtok[:, c, h * HD:(h + 1) * HD], sc[c][:, i, P:2 * P], start=True, stop=False)
                    last = mm(b, work[:, 2 + c, i * HD:(i + 1) * HD], sc[c][:, i, 2 * P:3 * P],
                              start=False, stop=(c == 0))
                    if c:
                        last = mm(b, work[po:po + HD, 4, (i // 2) * HD:(i // 2 + 1) * HD],
                                  kq[po:po + HD, n, 1, 1, :], start=False, stop=True)
                last.then_inc(s["y_mm"], 1)

            def head_moments(n):
                if n < KT:
                    pe.wait_ge(s["y_ready"], 8 * r + 2 * (n // 2) + 2)
                    if n >= 2:
                        pe.wait_ge(s["gn_c"], 8 * r + n - 1)
                    mm(B[n % 2][:, 0:S], T("head_mean"), oT[:, n, :], start=True, stop=True).then_inc(s["gn_mu"], 1)
                if n >= 2:
                    pe.wait_ge(s["gn_sq"], 8 * r + n - 1)
                    last = gather(n - 2, B[3], "head_avg")
                    if n == KT + 1:
                        last.then_inc(s["gn_var"], 1)

            for g in range(5):
                if g < 4:
                    first_step(g)
                if g >= 2:
                    outputs(g - 2, 1)
                if g:
                    scores(g - 1, 0, 0)
                for lv in range(7):
                    if g < 4:
                        level_product(g, lv)
                    if g:
                        if lv in (0, 1, 2):
                            scores(g - 1, (lv + 1) // 2, (lv + 1) % 2)
                        if lv == 2:
                            right(g - 1, 0)
                        if lv == 3:
                            solve(g - 1, 0)
                        if lv == 4:
                            state(g - 1)
                            outputs(g - 1, 0)
                        if lv == 5:
                            right(g - 1, 1)
                        if lv == 6:
                            solve(g - 1, 1)
                    if g == 4 and lv:
                        if lv == 1:
                            pe.wait_ge(s["xn_ready"], step_no(4 * r + 3, 6, 1))
                        head_moments(lv - 1)
                    if g < 4 and lv:
                        level_update(g, lv)
            outputs(3, 1)

            for n in range(6, KT + 2):
                head_moments(n)
            pe.wait_ge(s["gn_inv"], r + 1)
            for n in range(KT):
                if n >= 4:
                    pe.wait_ge(s["gn_scaled"], 8 * r + n - 3)
                spread(n, norms).then_inc(s["gn_spread"], 1)
            out_proj(L, 30, rw_o_split, skipped=3)

        def rwkv_act(act, L, A, evac, xm_hi, tokens_v, out_split):
            u, r, j = L["u"], L["rw"], L["idx"]
            for k in range(KT):
                xm_hi(L, 0, k // 4, k % 4)
            for group in range(3):
                evac(L, 8 * group, 8, mixed=group + 1)
            for k in range(2 * KT):
                xm_hi(L, 4 + k // KT, k % KT // 4, k % 4)
            act.wait_ge(s["a_used"], u + 27)
            A(work[0:64, 4, :], B[0][0:64, 0:S], ACT.Tanh)
            A(work[64:128, 4, :], B[4][64:128, 0:S], ACT.Copy)
            A(work[:, 5, :], B[1][:, 0:S], ACT.Sigmoid)
            A(work[0:32, 6, :], B[3][0:32, 0:S], ACT.Sigmoid)
            A(work[32:64, 6, :], B[2][32:64, 0:S], ACT.Copy).then_inc(s["lora1_ready"], 1)
            for n in range(KT):
                p = n % 2
                act.wait_ge(s["lora2_mm"], 8 * r + n + 1)
                if j:
                    A(bonus[:, n, :], B[2 + p][:, 0:S], ACT.Sigmoid, bias=V("v0_", n))
                A(kb[:, n, :], B[4 + 2 * p][:, 0:S], ACT.Sigmoid, bias=V(f"w0_{j}", n))
                A(bb[:, n, :], B[5 + 2 * p][:, 0:S], ACT.Sigmoid, bias=V(f"a0_{j}", n))
                A(gate[:, n, :], B[p][:, 0:S], ACT.Copy).then_inc(s["lora2_ready"], 1)
                A(kk_[:, n, :], qkv[:, 8 + n, :], ACT.Copy, scale=V(f"k_k_{j}", n))
                A(sq[:, n, :], qkv[:, 8 + n, :], ACT.Square, scale=V(f"k_k_{j}", n)).then_inc(s["kk_sq"], 1)
            act.wait_ge(s["kk_sum"], r + 1)
            A(norms, B[7][:, :], ACT.Sqrt).then_inc(s["kk_std"], 1)
            act.wait_ge(s["mid_ready"], r + 1)
            A(dec[:, :, :, 0:1].rearrange("p k c o -> p (k c o)"), small[:, 0:16], ACT.Exp)
            A(small[:, 32:40], small[:, 1:16:2], ACT.Exp, scale=-1.0)
            for n in range(KT):
                for c in range(CC):
                    cs = slice(c * P, (c + 1) * P)
                    A(dec[:, n, c, 1:P + 1], oT[:, n, cs], ACT.Exp, scale=-KAPPA,
                      bias=small[:, 2 * n + c:2 * n + c + 1])
                    last = A(em[:, n, cs], oT[:, n, cs], ACT.Exp, scale=KAPPA,
                             bias=small[:, 16 + 2 * n + c:17 + 2 * n + c])
                last.then_inc(s["dec_ready"], 1)
            tokens_v(L)
            for g in range(4):
                act.wait_ge(s["kt_mm"], 4 * r + g + 1)
                A(sqf[:, g * 512:(g + 1) * 512], B[2 + g % 2][:, :], ACT.Copy).then_inc(s["kt_ready"], 1)
            act.wait_ge(s["dec_ready"], 8 * r + 8)

            def level_copy(g, lv):
                G = 4 * r + g
                for c in range(CC):
                    act.wait_ge(s["xn_mm"], step_no(G, lv, c))
                    if lv < 6:
                        A(inv[c][:, X, :, :].rearrange("p i n -> p (i n)"), B[2 + c][:, :], ACT.Copy)\
                            .then_inc(s["xn_ready"], 1)
                    else:
                        A(sc[c][:, :, 3 * P:4 * P], B[2 + c][:, :].rearrange("p (i n) -> p i n", i=4), ACT.Copy)\
                            .then_inc(s["xn_ready"], 1)
                if lv < 6:
                    for c in range(CC):
                        act.wait_ge(s["turn_mm"], 10 * G + 2 * (lv - 1) + c + 1)
                        A(inv[c][:, XT, :, :].rearrange("p i n -> p (i n)"), B[2 + c][:, :], ACT.Copy)\
                            .then_inc(s["turned"], 1)

            def copy_rhs(g, c):
                act.wait_ge(s["rhs_mm"], 8 * r + 2 * g + c + 1)
                A(work[:, c, 0:P], B[4][:, c * P:(c + 1) * P], ACT.Copy)
                A(work[:, c, P:2 * P], B[5][:, c * P:(c + 1) * P], ACT.Copy).then_inc(s["rhs_ready"], 1)

            def copy_u(g, c):
                act.wait_ge(s["u_mm"], 8 * r + 2 * g + c + 1)
                A(work[:, 2 + c, :], B[6][:, c * S:(c + 1) * S], ACT.Copy, scale=-1.0).then_inc(s["u_ready"], 1)

            def copy_y(g, c):
                act.wait_ge(s["y_mm"], 8 * r + 2 * g + c + 1)
                for p in range(2):
                    po = HD * p
                    last = A(oT[po:po + HD, 2 * g:2 * g + 2, c * P:(c + 1) * P],
                             B[4 + p][po:po + HD, S:2 * S].rearrange("p (a b) -> p a b", a=2), ACT.Copy)
                last.then_inc(s["y_ready"], 1)

            def copy_state(g):
                act.wait_ge(s["st_mm"], 4 * r + g + 1)
                if g == 0:
                    act.wait_ge(s["factor_ready"], r + 1)
                for t in range(2):
                    last = A(work[:, 4, t * HD:(t + 1) * HD], B[7][:, t * HD:(t + 1) * HD], ACT.Copy,
                             scale=small[:, 40 + 2 * g + t:41 + 2 * g + t])
                last.then_inc(s["st_ready"], 1)

            def centred_square(n):
                act.wait_ge(s["gn_c"], 8 * r + n + 1)
                A(sq[:, n, :], oT[:, n, :], ACT.Square).then_inc(s["gn_sq"], 1)

            for g in range(5):
                if g >= 2:
                    copy_y(g - 2, 1)
                for lv in range(7):
                    if g:
                        if lv == 2:
                            copy_rhs(g - 1, 0)
                        if lv == 3:
                            copy_u(g - 1, 0)
                        if lv == 4:
                            copy_state(g - 1)
                            copy_y(g - 1, 0)
                        if lv == 5:
                            copy_rhs(g - 1, 1)
                        if lv == 6:
                            copy_u(g - 1, 1)
                    if g == 4 and lv:
                        centred_square(lv - 1)
                    if g < 4 and lv:
                        level_copy(g, lv)
            A(small[:, 63:64], T("eps"), ACT.Sqrt)
            copy_y(3, 1)
            for n in range(6, KT):
                centred_square(n)
            act.wait_ge(s["gn_var"], r + 1)
            A(norms, B[3][:, :], ACT.Sqrt, bias=T("gn_eps")).then_inc(s["gn_std"], 1)
            out_split(L, 30, rw_o_split, lambda n: act.wait_ge(s["gn_ready"], 8 * r + n + 1))

        def rwkv_dve(dve, L, v, step, lo, out_split, add_out):
            r, j, j_ = L["rw"], L["idx"], L["idx"]
            dve.wait_ge(s["h_raw"], 8 * (L["part"] + 1))
            order = (0, 1, 2, 5, 3, 4)

            def mixed(group, i, j):
                k = i * 4 + j
                a = VEC[f"mix{order[group]}_{j_}"][0]
                num = isinstance(k, int)
                if r or group or not num or k >= 4:
                    dve.wait_ge(s["xm_ready"], i * 4 + (48 * r + 8 * group + j - 3))
                v.scalar_tensor_tensor(out=work[:, j, :], in0=sq[:, k, :] if num else sq[:, ds(k, 1), :],
                                       scalar=vec[:, a + k:a + k + 1] if num else vec[:, ds(k + a, 1)],
                                       in1=hT[:, k, :] if num else hT[:, ds(k, 1), :],
                                       op0=ALU.mult, op1=ALU.add).then_inc(s["xm_raw"], 1)

            def mixed_low(group, i, j):
                k = i * 4 + j
                t = x_split[group % 3]
                dve.wait_ge(s["xm_hi"], i * 4 + (48 * r + 8 * group + j + 1))
                hi_, lo_ = [t[:, q, k, :] if isinstance(k, int) else t[:, q, ds(k, 1), :] for q in range(2)]
                v.tensor_tensor(lo_, work[:, j, :], hi_.bitcast(f32), ALU.subtract).then_inc(s["xm_ready"], 1)

            for k in range(KT + 1):
                if k < KT:
                    dve.wait_ge(s["xx_ready"], 8 * r + k + 1)
                    mixed(0, k // 4, k % 4)
                if k:
                    mixed_low(0, (k - 1) // 4, (k - 1) % 4)
            for group in range(1, 4):
                with dve.Fori(0, 2) as i:
                    for q in range(4):
                        mixed(group, i, q)
                        lo(L, 8 * (group - 1) + q + AHEAD, i)
                        mixed_low(group, i, q)
            for t in range(2 * KT + 1):
                if t < 2 * KT:
                    mixed(4 + t // KT, t % KT // 4, t % 4)
                if t:
                    mixed_low(4 + (t - 1) // KT, (t - 1) % KT // 4, (t - 1) % 4)
            dve.wait_ge(s["xm_ready"], 48 * r + 48)
            dve.wait_ge(s["proj_evac"], L["proj"] + 24)
            for n in range(KT):
                K, R, t = qkv[:, 8 + n, :], qkv[:, n, :], work[:, n % 2, :]
                dve.wait_ge(s["lora2_ready"], 8 * r + n + 1)
                step.did(v.tensor_tensor_scan(oT[:, n, :], T("scan_keep"), kb[:, n, :], 0.0, ALU.mult, ALU.add))
                dve.wait_ge(s["kk_sq"], 8 * r + n + 1)
                dve.wait_ge(s["ka_ready"], 8 * r + n + 1)
                step.did(v.scalar_tensor_tensor(out=K, in0=t, scalar=1.0, in1=K, op0=ALU.add, op1=ALU.mult))
                step.settle()
                v.scalar_tensor_tensor(out=hT[:, n, :], in0=R, scalar=V(f"r_k_{j}", n), in1=K,
                                       op0=ALU.mult, op1=ALU.mult).then_inc(s["rk_ready"], 1)
            mids = oT[:, :, :].rearrange("p k (c t) -> p (k c) t", c=CC)[:, :, P // 2 - 1:P // 2]
            step.did(v.tensor_scalar(small[:, 0:16].unsqueeze(2), mids, KAPPA, None, ALU.mult))
            v.tensor_scalar(small[:, 16:32].unsqueeze(2), mids, -KAPPA, None, ALU.mult).then_inc(s["mid_ready"], 1)
            dve.wait_ge(s["kk_std"], r + 1)
            step.did(v.tensor_scalar(norms, norms, 1e-12, None, ALU.max))
            step.settle()
            v.reciprocal(norms, norms).then_inc(s["kk_inv"], 1)
            for n in range(KT):
                dve.wait_ge(s["rk_sum"], 8 * r + n + 1)
                dve.wait_ge(s["v_final"], 8 * r + n + 1)
                v.tensor_tensor(bonus[:, n, :], B[4 + n % 3][:, 0:S], qkv[:, 16 + n, :], ALU.mult)\
                    .then_inc(s["bonus_ready"], 1)
            for n in range(KT):
                dve.wait_ge(s["kk_spread"], 8 * r + n + 1)
                v.tensor_tensor(kk_[:, n, :], kk_[:, n, :], B[n % 4][:, 0:S], ALU.mult).then_inc(s["kk_done"], 1)
                dve.wait_ge(s["kk_done"], 8 * r + n + 1)
                step.did(v.tensor_tensor(bb[:, n, :], kk_[:, n, :], bb[:, n, :], ALU.mult))
                dve.wait_ge(s["dec_ready"], 8 * r + n + 1)
                step.did(v.tensor_tensor(kq[:, n, :, 0, :], chunks(kk_[:, n, :]), dec[:, n, :, 0:P], ALU.mult))
                step.settle()
                v.tensor_tensor(bb[:, n, :], bb[:, n, :], em[:, n, :], ALU.mult).then_inc(s["keys_ready"], 1)
            v.tensor_tensor(small[:, 40:48].unsqueeze(2), small[:, 32:40].unsqueeze(2), dec[:, :, 0, P:P + 1],
                            ALU.mult).then_inc(s["factor_ready"], 1)
            dve.wait_ge(s["keys_ready"], 8 * r + 8)
            dve.wait_ge(s["bonus_ready"], 8 * r + 8)

            def first_masks(g):
                for c in range(CC):
                    G = 4 * r + g
                    dve.wait_ge(s["at_mm"], 2 * G + c + 1)
                    a = TAB["rw_mask"][0]
                    lt = inv[c][:, LT, :, :]
                    step.did(v.tensor_tensor(lt, B[c][:, :].rearrange("p (i n) -> p i n", i=4),
                                             tab[:, a:a + P].unsqueeze(1).broadcast_to([P, 4, P]), ALU.mult))
                    step.settle()
                    v.tensor_tensor(lt, lt, four("ident"), ALU.add).then_inc(s["lt_ready"], 1)

            def factor(g, lv):
                G = 4 * r + g
                for c in range(CC):
                    dve.wait_ge(s["lx_mm"], (7 * G + lv) * 2 + c + 1)
                    v.tensor_tensor(inv[c][:, Q if lv else X, :, :], B[c][:, :].rearrange("p (i n) -> p i n", i=4),
                                    four(f"level{lv}"), ALU.mult).then_inc(s["q_ready"], 1)

            def score_masks(g, c, t):
                G = 4 * r + g
                dve.wait_ge(s["score_mm"], 4 * G + 2 * c + t + 1)
                if g and t == 0:
                    dve.wait_ge(s["y_mm"], 2 * G - 1 + c)
                a, two_heads = TAB["rw_mask"][0], slice(2 * t, 2 * t + 2)
                v.tensor_tensor(sc[c][:, two_heads, 0:2 * P], B[6][:, :].rearrange("p (i n) -> p i n", i=2),
                                tab[:, a:a + 2 * P].unsqueeze(1).broadcast_to([P, 2, 2 * P]), ALU.mult)
                v.tensor_tensor(sc[c][:, two_heads, 2 * P:3 * P], B[7][:, 0:S].rearrange("p (i n) -> p i n", i=2),
                                tab[:, a + P:a + 2 * P].unsqueeze(1).broadcast_to([P, 2, P]), ALU.mult)\
                    .then_inc(s["score_ready"], 1)

            def centre(n):
                dve.wait_ge(s["gn_mu"], 8 * r + n + 1)
                v.tensor_tensor(oT[:, n, :], oT[:, n, :], B[n % 2][:, 0:S], ALU.subtract).then_inc(s["gn_c"], 1)

            for g in range(5):
                if g < 4:
                    first_masks(g)
                if g:
                    score_masks(g - 1, 0, 0)
                for lv in range(7):
                    if g < 4:
                        factor(g, lv)
                    if g and lv < 3:
                        score_masks(g - 1, (lv + 1) // 2, (lv + 1) % 2)
                    if g == 4 and lv:
                        centre(lv - 1)
            for n in range(6, KT):
                centre(n)
            dve.wait_ge(s["gn_std"], r + 1)
            dve.wait_ge(s["gn_c"], 8 * r + 8)
            v.reciprocal(norms, norms).then_inc(s["gn_inv"], 1)
            for n in range(KT):
                dve.wait_ge(s["gn_spread"], 8 * r + n + 1)
                v.tensor_tensor(oT[:, n, :], oT[:, n, :], B[n % 4][:, 0:S], ALU.mult).then_inc(s["gn_scaled"], 1)
                dve.wait_ge(s["gn_scaled"], 8 * r + n + 1)
                v.tensor_scalar(oT[:, n, :], oT[:, n, :], V(f"ln_w_{j}", n), V(f"ln_b_{j}", n), ALU.mult, ALU.add)\
                    .then_inc(s["gn_affine"], 1)
            out_split(L, 30, rw_o_split, skipped=3)
            add_out(L, 30, skipped=3)

        def rwkv_pool(pool, L, pstep):
            r = L["rw"]
            g_, j = nc.gpsimd, L["idx"]
            for k in range(KT):
                pool.wait_ge(s["h_raw"], 8 * L["part"] + k + 1)
                g_.tensor_tensor(sq[:, k, 1:S], hT[:, k, 0:S - 1], hT[:, k, 1:S], ALU.subtract)
                g_.tensor_scalar(sq[:, k, 0:1], hT[:, k, 0:1], -1.0, None, ALU.mult).then_inc(s["xx_ready"], 1)
            for n in range(KT):
                Vt = qkv[:, 16 + n, :]
                pool.wait_ge(s["lora2_ready"], 8 * r + n + 1)
                if n >= 2:
                    pool.wait_ge(s["rk_ready"], 8 * r + n - 1)
                g_.tensor_scalar(work[:, n % 2, :], bb[:, n, :], 1.0, V(f"k_a_{j}", n), ALU.subtract, ALU.mult)\
                    .then_inc(s["ka_ready"], 1)
                if j == 0:
                    g_.tensor_copy(v_first[:, n, :], Vt).then_inc(s["v_final"], 1)
                else:
                    if n == 0:
                        pool.wait_ge(s["proj_evac"], L["proj"] + 24)
                    mix = work[:, 7, :]
                    pstep.did(g_.tensor_tensor(mix, v_first[:, n, :], Vt, ALU.subtract))
                    pstep.settle()
                    pstep.did(g_.tensor_tensor(mix, mix, bonus[:, n, :], ALU.mult))
                    pstep.settle()
                    g_.tensor_tensor(Vt, Vt, mix, ALU.add).then_inc(s["v_final"], 1)
                    pool.wait_ge(s["v_final"], 8 * r + n + 1)
            for n in range(KT):
                pool.wait_ge(s["dec_ready"], 8 * r + n + 1)
                g_.tensor_tensor(kq[:, n, :, 1, :], chunks(qkv[:, n, :]), dec[:, n, :, 1:P + 1], ALU.mult)
                g_.tensor_tensor(kb[:, n, :], qkv[:, 8 + n, :], em[:, n, :], ALU.mult).then_inc(s["r_k_ready"], 1)
            pool.wait_ge(s["r_k_ready"], 8 * r + 8)
            pool.wait_ge(s["keys_ready"], 8 * r + 8)
            pool.wait_ge(s["bonus_ready"], 8 * r + 8)
            for g in range(4):
                G, q = 4 * r + g, padded_q[g % 2]
                if g < 2:
                    if g:
                        pool.wait_ge(s["xt_ready"], 2 * G)
                    pstep.did(g_.memset(q[0:HD, :, 1, :], 0.0))
                    pstep.settle()
                    pstep.did(g_.memset(q[HD:P, :, 0, :], 0.0))
                    pstep.settle()
                else:
                    pool.wait_ge(s["score_mm"], 4 * G - 4)
                    pool.wait_ge(s["xt_ready"], 2 * G)
                pstep.did(g_.tensor_copy(q[0:HD, :, 0, :], kq_rows[0:HD, 4 * g:4 * g + 4, :]))
                pstep.settle()
                g_.tensor_copy(q[HD:P, :, 1, :], kq_rows[HD:P, 4 * g:4 * g + 4, :]).then_inc(s["padded"], 1)
                pool.wait_ge(s["padded"], G + 1)
                for c in range(CC):
                    pool.wait_ge(s["lt_ready"], 2 * G + c + 1)
                    g_.tensor_tensor(inv[c][:, XT, :, :], inv[c][:, LT, :, :], four("level0t"), ALU.mult)\
                        .then_inc(s["xt_ready"], 1)
            for n in range(KT):
                pool.wait_ge(s["gn_affine"], 8 * r + n + 1)
                pstep.did(g_.tensor_tensor(oT[:, n, :], oT[:, n, :], bonus[:, n, :], ALU.add))
                pstep.settle()
                g_.tensor_tensor(oT[:, n, :], oT[:, n, :], gate[:, n, :], ALU.mult).then_inc(s["gn_ready"], 1)

        @block.sync
        def _(sp):
            sp.dma_start(xT[:, :, :], x_in).then_inc(s["x_loaded"], 16)
            sp.dma_start(tab[:, 0:FIRST_W], tab_in[:, 0:FIRST_W]).then_inc(s["const_loaded"], 16)
            sp.dma_start(vec[:, :], vec_in).then_inc(s["const_loaded"], 16)

            def load(L, n, i=0):
                u, back = L["u"] + n, n - 4
                if back >= 0 and L["kind"] == "rwkv" and back in (27, 28, 29):
                    sp.wait_ge(s["a_used"], u - 3)
                elif u >= 4 or not isinstance(i, int):
                    skipped = 3 if L["kind"] == "rwkv" and back >= 30 else 0
                    sp.wait_ge(s["w_lo"], i * 4 + (L["us"] + back - skipped + 1))
                sp.dma_start(ring_a[:, u % 4, :], wa[i * 4 + u, :, :] if not isinstance(i, int) else wa[u, :, :])\
                    .then_inc(a_loaded[u % 4], 16)

            for L in plan:
                n_units_here = UNITS[L["kind"]]
                if L["kind"] == "ffn":
                    def two_tiles(i, first):
                        for j in range(4):
                            load(L, j, i)
                        if first and L["part"] == 0:
                            sp.dma_start(tab[:, FIRST_W:TAB_W], tab_in[:, FIRST_W:TAB_W])\
                                .then_inc(s["tab_loaded"], 16)
                        for j in range(2):
                            if not (first and L["d"] + j < 2):
                                sp.wait_ge(s["dn_lo"], i * 2 + (L["d"] + j - 1))
                            sp.dma_start(ring_d[:, j, :], wd[i * 2 + (L["d"] + j), :, :])\
                                .then_inc(d_loaded[j], 16)
                    two_tiles(0, True)
                    with sp.Fori(1, FT // 2) as i:
                        two_tiles(i, False)
                else:
                    looped = 24
                    for n in range(4):
                        load(L, n)
                    if L["part"] == 0:
                        sp.dma_start(tab[:, FIRST_W:TAB_W], tab_in[:, FIRST_W:TAB_W]).then_inc(s["tab_loaded"], 16)
                    with sp.Fori(0, (looped - 4) // 4) as i:
                        for j in range(4):
                            load(L, 4 + j, i)
                    for n in range(looped, n_units_here):
                        load(L, n)
            sp.wait_ge(s["x_added"], 8 * (PARTS + 1))
            sp.dma_start(out, xT[:, :, :]).then_inc(s["stored"], 16)
            sp.wait_ge(s["stored"], 16)

        @block.tensor
        def _(pe):
            mm = nc.tensor.matmul
            pe.wait_ge(s["const_loaded"], 32)

            def norm(m):
                for k in range(KT):
                    pe.wait_ge(s["sq_ready"], 8 * m + k + 1)
                    last = mm(norm_bank(m)[:, 0:S], T("ones"), sq[:, k, :], start=(k == 0), stop=(k == KT - 1))
                last.then_inc(s["ssum_ready"], 1)

            def product(dst, w, x, ready=None):
                for k in range(KT):
                    if ready:
                        pe.wait_ge(s[ready[0]], ready[1] + k + 1)
                    ks = slice(k * P, (k + 1) * P)
                    mm(dst, w[:, 0, ks], x[:, 0, k, :], start=(k == 0), stop=False)
                    mm(dst, w[:, 0, ks], x[:, 1, k, :], start=False, stop=False)
                    last = mm(dst, w[:, 1, ks], x[:, 0, k, :], start=False, stop=(k == KT - 1))
                return last

            def unit(L, n, i, dst, x, skipped=0, ready=None):
                pe.wait_ge(s["w_lo"], i * 4 + (L["us"] + n - skipped + 1))
                product(dst, w_split[:, (L["u"] + n) % 4, :, :], x, ready).then_inc(s["a_used"], 1)

            def ffn(L):
                f, d = L["d"] // FT, L["d"]

                def gate_up(i, q, first=False):
                    for g in range(2):
                        unit(L, 2 * q + g, i, B[4 + q][:, g * S:(g + 1) * S], h_split,
                             ready=("h_ready", 8 * L["hs"]) if first and g == 0 else None)

                def down(i, q, first=False, final=False):
                    pe.wait_ge(s["act_ready"], i * 2 + (FT * f + q + 1))
                    pe.wait_ge(s["dn_lo"], i * 2 + (d + q + 1))
                    for m in range(KT):
                        o, ms = B[m // 2][:, (m % 2) * S:(m % 2 + 1) * S], slice(m * P, (m + 1) * P)
                        mm(o, d_split[:, q, 0, ms], act_split[:, q, 0, :], start=(first and m % 2 == 0),
                           stop=False, skip_group_check=True)
                        mm(o, d_split[:, q, 0, ms], act_split[:, q, 1, :], start=False,
                           stop=False, skip_group_check=True)
                        last = mm(o, d_split[:, q, 1, ms], act_split[:, q, 0, :], start=False,
                                  stop=final, skip_group_check=True)
                    last.then_inc(s["d_used"], 1)

                gate_up(0, 0, first=True)
                gate_up(0, 1)
                down(0, 0, first=True)
                with pe.Fori(1, FT // 2) as i:
                    gate_up(i, 0)
                    down(i - 1, 1)
                    gate_up(i, 1)
                    down(i, 0)
                down(FT // 2 - 1, 1, final=True)

            def project(L, first, count, x):
                def four_units(i, ready=None):
                    for j in range(4):
                        pe.wait_ge(s["proj_evac"], i * 4 + (L["proj"] + first + j - 3))
                        unit(L, first + j, i, B[4 + (first + j) % 4][:, 0:S], x, ready=ready if j == 0 else None)
                peeled = first == 0
                if peeled:
                    four_units(0, ("xm_ready", 48 * L["rw"]) if L["kind"] == "rwkv" else ("h_ready", 8 * L["hs"]))
                with pe.Fori(int(peeled), count // 4) as i:
                    four_units(i)

            def project_one(L, n):
                pe.wait_ge(s["proj_evac"], L["proj"] + n - 3)
                unit(L, n, 0, B[4 + n % 4][:, 0:S], h_split, ready=("h_ready", 8 * L["hs"]) if n == 0 else None)

            def transpose_v(L):
                for g in range(4):
                    if g >= 2:
                        pe.wait_ge(s["vtok_ready"], L["vt"] + g - 1)
                    for i in range(4):
                        last = nc.tensor.transpose(v_bank(L, g)[:, i * P:(i + 1) * P],
                                                   qkv[:, 16 + 4 * (g % 2) + i, (g // 2) * P:(g // 2 + 1) * P],
                                                   T("ident"))
                    last.then_inc(s["vtok_done"], 1)

            def out_proj(L, first, x, skipped=0):
                pe.wait_ge(s["proj_evac"], L["proj"] + min(first, PROJ[L["kind"]]))
                for n in range(KT):
                    if n >= 4:
                        pe.wait_ge(s["x_added"], 8 * (L["part"] + 1) + n - 3)
                    unit(L, first + n, 0, B[4 + n % 4][:, 0:S], x, skipped,
                         ready=("o_ready", 8 * L["mixers"]) if n == 0 else None)

            def stick(L):
                project(L, 0, 24, h_split)
                pe.wait_ge(s["proj_evac"], L["proj"] + 24)
                transpose_v(L)
                pe.wait_ge(s["vtok_ready"], L["vt"] + 4)

                def z(h):
                    po, t = HD * (h % 2), h // 2
                    if h >= 2:
                        pe.wait_ge(s["zm_ready"], h - 1)
                    mm(B[h % 2][:, 0:S], qkv[po:po + HD, 8 + t, 0:P], qkv[po:po + HD, t, :], start=True, stop=True)
                    mm(B[h % 2][:, S:S + P], qkv[po:po + HD, 8 + t, P:S], qkv[po:po + HD, t, P:S],
                       start=True, stop=True).then_inc(s["z_done"], 1)

                def suffix(h):
                    pe.wait_ge(s["sp_ready"], h + 1)
                    if h >= 2:
                        pe.wait_ge(s["lg_ready"], h - 1)
                    b = B[2 + h % 2]
                    mm(b[:, 0:S], T("tri"), sp_(h)[:, 0:S], start=True, stop=False, skip_group_check=True)
                    mm(b[:, P:S], T("ones"), sp_(h)[:, S:384], start=False, stop=True, skip_group_check=True)
                    mm(b[:, S:384], T("tri"), sp_(h)[:, S:384], start=True, stop=True,
                       skip_group_check=True).then_inc(s["cum_done"], 1)

                def pv(h):
                    po, t = HD * (h % 2), h // 2
                    pe.wait_ge(s["p_ready"], h + 1)
                    if h % 2 == 0 and t >= 2:
                        pe.wait_ge(s["ot_evac"], L["pairs"] + t - 1)
                    b = B[4 + t % 2]
                    mm(b[po:po + HD, 0:S], vtok[:, 0, h * HD:(h + 1) * HD], p_(h)[:, 0:S], start=True, stop=False,
                       skip_group_check=True)
                    mm(b[po:po + HD, P:S], vtok[:, 1, h * HD:(h + 1) * HD], p_(h)[:, S:384], start=False, stop=True,
                       skip_group_check=True).then_inc(s["pv_done"], 1)

                for g in range(NH // 4 + 1):
                    for h in four_heads(g):
                        z(h)
                    for h in four_heads(g - 1):
                        suffix(h)
                    for h in four_heads(g - 1):
                        pv(h)
                out_proj(L, 24, x_split[2])

            def norm_rope_mm(L, n):
                gained, rope, b = n < 16, rope_of(L["kind"], n), B[n % 4]
                if gained:
                    pe.wait_ge(s["nr_in"], L["heads"] + n + 1)
                else:
                    pe.wait_ge(s["proj_evac"], L["proj"] + n + 1)
                if n >= 4:
                    pe.wait_ge(s["qk_ready"], L["tiles"] + n - 3)
                if gained:
                    last = mm(b[:, 0:S], T("head_mean"), squared(n), start=True, stop=True)
                if rope:
                    last = mm(b[:, S:2 * S], T("rot" + rope), gained_(n) if gained else qkv[:, row_of("dsa", n), :],
                              start=True, stop=True)
                last.then_inc(s["nr_mm"], 1)

            def softmax_heads(L):
                H, O = L["heads"], L["pairs"]

                def scores(t):
                    pe.wait_ge(s["k_padded"], H // 2 + t + 1)
                    if t >= 2:
                        pe.wait_ge(s["sm_ready"], H + 2 * t - 2)
                    for qt in range(NT):
                        last = mm(score_banks(t)[qt][:, :], qkv[:, t, qt * P:(qt + 1) * P], padded_k(L, t),
                                  start=True, stop=True)
                    last.then_inc(s["s_done"], 2)

                def turn(h):
                    pe.wait_ge(s["pn_ready"], H + h + 1)
                    if h >= 2:
                        pe.wait_ge(s["pt_ready"], H + h - 1)
                    p_ = planes[:, 0, (h % 4) * 512:(h % 4 + 1) * 512]
                    for st in range(NT):
                        for qt in range(NT):
                            last = nc.tensor.transpose(B[2 + h % 2][:, st * S + qt * P:st * S + (qt + 1) * P],
                                                       p_[:, qt * S + st * P:qt * S + (st + 1) * P], T("ident"))
                    last.then_inc(s["t_done"], 1)

                def pv(h):
                    po, t = HD * (h % 2), h // 2
                    pe.wait_ge(s["pt_ready"], H + h + 1)
                    if h % 2 == 0 and t >= 2:
                        pe.wait_ge(s["ot_evac"], O + t - 1)
                    for st in range(NT):
                        last = mm(B[4 + t % 2][po:po + HD, 0:S], vtok[:, st, h * HD:(h + 1) * HD],
                                  planes[:, 2, (h % 2) * 512 + st * S:(h % 2) * 512 + (st + 1) * S],
                                  start=(st == 0), stop=(st == NT - 1))
                    last.then_inc(s["pv_done"], 1)

                scores(0)
                for t in range(NH + 3):
                    if t + 2 < NH and t % 2 == 0:
                        scores(t // 2 + 1)
                    if 0 <= t - 2 < NH:
                        turn(t - 2)
                    if L["kind"] == "multi" and t == NH:
                        pe.wait_ge(s["sm_ready"], H + NH)
                        out_sum(L, 0)
                        out_sum(L, 1)
                    if 0 <= t - 3 < NH:
                        pv(t - 3)

            def out_sum(L, seg):
                a, b = SEGMENTS[seg]
                pe.wait_ge(s["on_sq"], 8 * L["multis"] + b)
                if seg >= 2:
                    pe.wait_ge(s["on_std"], 3 * L["multis"] + seg - 1)
                for n in range(a, b):
                    last = mm(B[6 + seg % 2][:, S:2 * S], T("ones"), sq[:, n, :], start=(n == a), stop=(n == b - 1))
                last.then_inc(s["on_sum"], 1)

            def index_weights(L):
                pe.wait_ge(s["proj_evac"], L["proj"] + 21 - 3)
                pe.wait_ge(s["w_lo"], L["us"] + 22)
                wi = w_split[:, (L["u"] + 21) % 4, :, :]
                for qt in range(NT):
                    o, qs = B[5][:, qt * 8:(qt + 1) * 8], slice(qt * P, (qt + 1) * P)
                    for k in range(KT):
                        mm(o, h_split[:, 0, k, qs], wi[:, 0, k * P:k * P + 8], start=(k == 0), stop=False)
                        mm(o, h_split[:, 0, k, qs], wi[:, 1, k * P:k * P + 8], start=False, stop=False)
                        last = mm(o, h_split[:, 1, k, qs], wi[:, 0, k * P:k * P + 8],
                                  start=False, stop=(k == KT - 1))
                last.then_inc(s["a_used"], 1)

            def dsa(L):
                for n in range(PROJ["dsa"]):
                    if n == 21:
                        index_weights(L)
                    else:
                        project_one(L, n)
                    for t in tiles_after("dsa", n):
                        norm_rope_mm(L, t)
                pe.wait_ge(s["qk_ready"], L["tiles"] + 21)
                for i in range(IDX_HEADS):
                    po, t = HD * (i % 2), 24 + i // 2
                    if i >= 2:
                        pe.wait_ge(s["idx_relu"], i - 1)
                    for qt in range(NT):
                        last = mm(B[i % 2][:, qt * S:(qt + 1) * S], qkv[po:po + HD, t, qt * P:(qt + 1) * P],
                                  qkv[po:po + HD, 28, :], start=True, stop=True)
                    last.then_inc(s["idx_mm"], 1)
                pe.wait_ge(s["idx_relu"], IDX_HEADS)
                pe.wait_ge(s["proj_evac"], L["proj"] + 30)
                transpose_v(L)
                pe.wait_ge(s["vtok_ready"], L["vt"] + 4)
                softmax_heads(L)
                out_proj(L, 30, x_split[2])

            def multi(L):
                for n in range(PROJ["multi"]):
                    project_one(L, n)
                    for t in tiles_after("multi", n):
                        norm_rope_mm(L, t)
                pe.wait_ge(s["proj_evac"], L["proj"] + 24)
                transpose_v(L)
                pe.wait_ge(s["qk_ready"], L["tiles"] + 16)
                pe.wait_ge(s["vtok_ready"], L["vt"] + 4)
                softmax_heads(L)
                out_sum(L, 2)
                out_proj(L, 24, x_split[2])

            for L in plan:
                norm(L["part"])
                if L["part"] == 0:
                    pe.wait_ge(s["tab_loaded"], 16)
                dict(ffn=ffn, stick=stick, dsa=dsa, multi=multi,
                     rwkv=lambda L: rwkv_pe(pe, L, product, project, transpose_v, out_proj))[L["kind"]](L)

        @block.scalar
        def _(act):
            A = nc.scalar.activation
            step = Steps(act, s["act_step"])
            act.wait_ge(s["const_loaded"], 32)

            def hi(L, n, i=0, skipped=0):
                u = L["u"] + n
                act.wait_ge(a_loaded[u % 4], i * 16 + 16 * (u // 4 + 1))
                if u >= 4 or not isinstance(i, int) or i:
                    act.wait_ge(s["a_used"], i * 4 + (u - 3))
                A(w_split[:, u % 4, 0, :], ring_a[:, u % 4, :], ACT.Copy).then_inc(s["w_hi"], 1)

            def root_table():
                A(small[:, 63:64], T("eps"), ACT.Sqrt)

            def norm(L):
                m = L["part"]
                after_mixer = m and plan[m - 1]["kind"] != "ffn"
                root_table()
                if m and not after_mixer:
                    for n in range(early(L)):
                        hi(L, n)
                for k in range(KT):
                    act.wait_ge(s["x_added"], 8 * m + k + 1)
                    A(sq[:, k, :], xT[:, k, :], ACT.Square).then_inc(s["sq_ready"], 1)
                    if after_mixer and 4 <= k < 4 + early(L):
                        hi(L, k - 4)
                act.wait_ge(s["ssum_ready"], m + 1)
                A(small_std, norm_bank(m)[:, 0:S], ACT.Sqrt, bias=T("eps"), scale=1.0 / D).then_inc(s["std_ready"], 1)
                if m == 0:
                    for n in range(early(L)):
                        hi(L, n)

                if L["kind"] != "rwkv":
                    for k in range(KT):
                        act.wait_ge(s["h_raw"], 8 * m + k + 1)
                        A(h_split[:, 0, k, :], hT[:, k, :], ACT.Copy).then_inc(s["h_hi"], 1)

            small_std = work[:, 7, :]

            def ffn(L):
                f, u = L["d"] // FT, L["u"]

                def tile_pair(i, final):
                    for q in range(2):
                        if not (final and q):
                            for g in range(2):
                                n = 2 * q + g + 2
                                hi(L, n, i)
                        act.wait_ge(d_loaded[q], i * 16 + 16 * (L["d"] // 2 + 1))
                        if f or not isinstance(i, int) or i:
                            act.wait_ge(s["d_used"], i * 2 + (L["d"] + q - 1))
                        A(d_split[:, q, 0, :], ring_d[:, q, :], ACT.Copy).then_inc(s["dn_hi"], 1)
                        if L["idx"] < 4:
                            act.wait_ge(s["a_used"], i * 4 + (u + 2 * q + 2))
                            A(work[:, 2 + q, :], B[4 + q][:, 0:S], ACT.Silu).then_inc(s["silu_ready"], 1)
                        else:
                            act.wait_ge(s["conv_ready"], i * 2 + (FT * L["convs"] + q + 1))
                            A(work[:, 2 + q, :], work[:, 4 + q, :], ACT.Gelu).then_inc(s["silu_ready"], 1)
                        act.wait_ge(s["act_raw"], i * 2 + (FT * f + q + 1))
                        A(act_split[:, q, 0, :], work[:, q, :], ACT.Copy).then_inc(s["act_hi"], 1)
                tile_pair(0, False)
                with act.Fori(1, FT // 2 - 1) as i:
                    tile_pair(i, False)
                tile_pair(FT // 2 - 1, True)

            def evac(L, first, count, mixed=None):
                u = L["u"] + first

                def four_units(i):
                    for j in range(4):
                        hi(L, first + j + AHEAD, i)
                        if mixed is not None:
                            xm_hi(L, mixed, i, j)
                        act.wait_ge(s["a_used"], i * 4 + (u + j + 1))
                        A(qkv[:, ds(i * 4 + (first + j), 1), :], B[4 + j][:, 0:S], ACT.Copy)\
                            .then_inc(s["proj_evac"], 1)
                peeled = u == 0
                if peeled:
                    four_units(0)
                with act.Fori(int(peeled), count // 4) as i:
                    four_units(i)

            def xm_hi(L, group, i, j):
                act.wait_ge(s["xm_raw"], i * 4 + (48 * L["rw"] + 8 * group + j + 1))
                if group >= 3:
                    act.wait_ge(s["a_used"], L["u"] + (8, 16, 25)[group - 3])
                t = x_split[group % 3][:, 0, :, :]
                A(t[:, ds(i * 4 + j, 1), :] if not isinstance(i, int) else t[:, i * 4 + j, :], work[:, j, :],
                  ACT.Copy).then_inc(s["xm_hi"], 1)

            def out_split(L, first, x, ready):
                for n in range(KT):
                    ready(n)
                    A(x[:, 0, n, :], oT[:, n, :], ACT.Copy).then_inc(s["o_hi"], 1)
                    if n in (2, 4, 6):
                        hi(L, first + n // 2 - 1)
                for n in range(3, KT):
                    hi(L, first + n)

            def tokens_v(L):
                for g in range(4):
                    act.wait_ge(s["vtok_done"], L["vt"] + g + 1)
                    A(vtok[:, g // 2, (g % 2) * 512:(g % 2 + 1) * 512], v_bank(L, g)[:, :], ACT.Copy)\
                        .then_inc(s["vtok_ready"], 1)

            def evac_one(L, n, row):
                act.wait_ge(s["a_used"], L["u"] + n + 1)
                A(qkv[:, row, :], B[4 + n % 4][:, 0:S], ACT.Copy).then_inc(s["proj_evac"], 1)

            def stick(L):
                evac(L, 0, 20)
                hi(L, 23)
                for n in range(20, 24):
                    evac_one(L, n, n)
                tokens_v(L)
                O = L["pairs"]

                def e_(h):
                    q = (h % 4) * 384
                    return work[:, 0:6, :].rearrange("p a b -> p (a b)")[:, q:q + 384]

                def exp_abs(h):
                    act.wait_ge(s["zm_ready"], h + 1)
                    if h >= 4:
                        act.wait_ge(s["ln_ready"], h - 3)
                    step.did(A(e_(h), zm_(h), ACT.Abs))
                    step.settle()
                    A(e_(h), e_(h), ACT.Exp, scale=-1.0).then_inc(s["e_done"], 1)

                def log(h):
                    act.wait_ge(s["e_done"], h + 1)
                    if h >= 4:
                        act.wait_ge(s["sp_ready"], h - 3)
                    A(ln_(h), e_(h), ACT.Ln, bias=1.0).then_inc(s["ln_ready"], 1)

                def weights(h):
                    act.wait_ge(s["lg_ready"], h + 1)
                    if h >= 4:
                        act.wait_ge(s["pv_done"], h - 3 + 2 * O)
                    A(p_(h), lg_(h), ACT.Exp).then_inc(s["p_ready"], 1)

                for g in range(NH // 4 + 2):
                    for h in four_heads(g):
                        exp_abs(h)
                    for h in four_heads(g - 2)[::2]:
                        o_pair(L, h // 2)
                    for h in four_heads(g - 1):
                        weights(h)
                    for h in four_heads(g):
                        log(h)
                out_weights(L, 24)

            def o_pair(L, t):
                act.wait_ge(s["pv_done"], 2 * L["pairs"] + 2 * t + 2)
                A(x_split[2][:, 0, t, :], B[4 + t % 2][:, 0:S], ACT.Copy).then_inc(s["o_hi"], 1)
                A(oT[:, t, :], B[4 + t % 2][:, 0:S], ACT.Copy).then_inc(s["ot_evac"], 1)

            def out_weights(L, first):
                for n in range(KT):
                    hi(L, first + n)

            def norm_rope_in(L, n, row, gain):
                g = L["tiles"] + n
                act.wait_ge(s["proj_evac"], L["proj"] + n + 1)
                if n >= 4:
                    act.wait_ge(s["qk_ready"], g - 3)
                A(squared(n), qkv[:, row, :], ACT.Square)
                A(gained_(n), qkv[:, row, :], ACT.Copy, scale=V(gain, row)).then_inc(s["nr_in"], 1)

            def projections(L, gain):
                count = PROJ[L["kind"]]
                for n in range(count):
                    if n + AHEAD < count:
                        hi(L, n + AHEAD)
                    if L["kind"] == "dsa" and n == 21:
                        act.wait_ge(s["a_used"], L["u"] + 22)
                        A(small[:, 16:32], B[5][:, 0:16], ACT.Copy,
                          scale=IDX_HEADS ** -0.5 * HD ** -0.5).then_inc(s["proj_evac"], 1)
                    else:
                        evac_one(L, n, row_of(L["kind"], n))
                    if n == 3:
                        norm_rope_in(L, 0, 0, gain)
                        norm_rope_in(L, 1, 1, gain)
                    for t in tiles_after(L["kind"], n):
                        if t + 2 < 16:
                            norm_rope_in(L, t + 2, t + 2, gain)
                        if t < 16:
                            norm_rope_std(L, t)

            def norm_rope_std(L, n):
                act.wait_ge(s["nr_mm"], L["tiles"] + n + 1)
                A(root_(n), B[n % 4][:, 0:S], ACT.Sqrt, bias=T("eps")).then_inc(s["nr_std"], 1)

            def softmax_heads(L):
                H, O = L["heads"], L["pairs"]

                def exps(h):
                    act.wait_ge(s["nmx_ready"], H + h + 1)
                    for qt in range(NT):
                        k = 4 * (h // 2 % 2) + 2 * qt + h % 2
                        last = A(planes[:, 0, (h % 4) * 512 + qt * S:(h % 4) * 512 + (qt + 1) * S],
                                 planes[:, 1, k * S:(k + 1) * S], ACT.Exp, bias=small[:, 48 + k:49 + k],
                                 accum_out=small[:, 32 + 2 * (h % 4) + qt:33 + 2 * (h % 4) + qt])
                    last.then_inc(s["e_ready"], 1)

                def copy_turned(h):
                    act.wait_ge(s["t_done"], H + h + 1)
                    if h >= 2:
                        act.wait_ge(s["pv_done"], 2 * O + h - 1)
                    A(planes[:, 2, (h % 2) * 512:(h % 2 + 1) * 512], B[2 + h % 2][:, :], ACT.Copy)\
                        .then_inc(s["pt_ready"], 1)

                def pair(t):
                    if L["kind"] == "dsa":
                        o_pair(L, t)
                    else:
                        act.wait_ge(s["pv_done"], 2 * O + 2 * t + 2)
                        A(sq[:, t, :], B[4 + t % 2][:, 0:S], ACT.Square).then_inc(s["on_sq"], 1)
                        A(oT[:, t, :], B[4 + t % 2][:, 0:S], ACT.Copy).then_inc(s["ot_evac"], 1)

                for t in range(NH + 4):
                    if t < NH:
                        exps(t)
                    if 0 <= t - 2 < NH:
                        copy_turned(t - 2)
                    if L["kind"] == "multi" and t == NH + 1:
                        out_root(L, 0)
                        out_root(L, 1)
                    if t >= 4 and (t - 4) % 2 == 1:
                        pair((t - 4) // 2)

            def dsa(L):
                projections(L, "gain0")
                for i in range(IDX_HEADS):
                    act.wait_ge(s["idx_mm"], i + 1)
                    if i >= 2:
                        act.wait_ge(s["idx_added"], i - 1)
                    A(planes[:, 1, (i % 2) * 512:(i % 2 + 1) * 512], B[i % 2][:, :], ACT.Relu)\
                        .then_inc(s["idx_relu"], 1)
                tokens_v(L)
                softmax_heads(L)
                out_weights(L, 30)

            def multi(L):
                projections(L, f"gain{1 + L['idx']}")
                tokens_v(L)
                softmax_heads(L)
                r = L["multis"]
                def o_high(n):
                    act.wait_ge(s["on_ready"], 8 * r + n + 1)
                    A(x_split[2][:, 0, n, :], oT[:, n, :], ACT.Copy).then_inc(s["o_hi"], 1)
                last = SEGMENTS[-1][0]
                for n in range(last):
                    o_high(n)
                for n in range(AHEAD):
                    hi(L, 24 + n)
                out_root(L, 2)
                for n in range(last, KT):
                    o_high(n)
                for n in range(AHEAD, KT):
                    hi(L, 24 + n)

            def out_root(L, seg):
                a, b = SEGMENTS[seg]
                act.wait_ge(s["on_sum"], 3 * L["multis"] + seg + 1)
                A(work[:, seg, :], B[6 + seg % 2][:, S:2 * S], ACT.Sqrt, bias=T("eps"),
                  scale=1.0 / ((b - a) * P)).then_inc(s["on_std"], 1)

            for L in plan:
                norm(L)
                if L["part"] == 0:
                    act.wait_ge(s["tab_loaded"], 16)
                dict(ffn=ffn, stick=stick, dsa=dsa, multi=multi,
                     rwkv=lambda L: rwkv_act(act, L, A, evac, xm_hi, tokens_v, out_split))[L["kind"]](L)

        @block.vector
        def _(dve):
            v = nc.vector
            step = Steps(dve, s["dve_step"])
            dve.wait_ge(s["const_loaded"], 32)
            dve.wait_ge(s["x_loaded"], 16)
            v.memset(small[:, 48:49], 0.0).then_inc(s["x_added"], 8)
            v.memset(small[:, 41:42], 0.0).then_inc(s["proj_evac"], 4)

            def lo(L, n, i=0, skipped=0):
                u = L["u"] + n
                dve.wait_ge(s["w_hi"], i * 4 + (L["us"] + n - skipped + 1))
                v.tensor_tensor(w_split[:, u % 4, 1, :], ring_a[:, u % 4, :], w_split[:, u % 4, 0, :].bitcast(f32),
                                ALU.subtract).then_inc(s["w_lo"], 1)

            def lo_loop(L, count):
                with dve.Fori(0, count // 4) as i:
                    for j in range(4):
                        lo(L, j + AHEAD, i)

            def o_low(L, n):
                dve.wait_ge(s["o_hi"], 8 * L["mixers"] + n + 1)
                dve.wait_ge(s["ot_evac"], L["pairs"] + n + 1)
                v.tensor_tensor(x_split[2][:, 1, n, :], oT[:, n, :], x_split[2][:, 0, n, :].bitcast(f32),
                                ALU.subtract).then_inc(s["o_ready"], 1)

            def out_split(L, first, x, skipped=0):
                for n in range(KT):
                    dve.wait_ge(s["o_hi"], 8 * L["mixers"] + n + 1)
                    v.tensor_tensor(x[:, 1, n, :], oT[:, n, :], x[:, 0, n, :].bitcast(f32), ALU.subtract)\
                        .then_inc(s["o_ready"], 1)
                    if n in (3, 5, 7):
                        lo(L, first + (n - 3) // 2, 0, skipped)

            def norm(L, gain):
                m = L["part"]
                dve.wait_ge(s["std_ready"], m + 1)
                r = work[:, 6, :]
                step.did(v.reciprocal(r, work[:, 7, :]))
                step.settle()
                if m == 0:
                    lo(L, 0)
                for k in range(KT + 2):
                    if k < KT:
                        v.scalar_tensor_tensor(out=hT[:, k, :], in0=xT[:, k, :], scalar=V(gain, k), in1=r,
                                               op0=ALU.mult, op1=ALU.mult).then_inc(s["h_raw"], 1)
                    if k >= 2 and L["kind"] != "rwkv":
                        n = k - 2
                        dve.wait_ge(s["h_hi"], 8 * L["hs"] + n + 1)
                        v.tensor_tensor(h_split[:, 1, n, :], hT[:, n, :], h_split[:, 0, n, :].bitcast(f32),
                                        ALU.subtract).then_inc(s["h_ready"], 1)
                if m == 0:
                    for n in range(1, early(L)):
                        lo(L, n)

            def ffn(L):
                f, u, conv = L["d"] // FT, L["u"], L["idx"] >= 4
                if conv:
                    a = VEC[f"conv{L['idx'] - 4}"][0]
                def tile_pair(i, final):
                    for q in range(2):
                        if not (final and q):
                            lo(L, 2 * q + 2, i)
                            lo(L, 2 * q + 3, i)
                        dve.wait_ge(s["dn_hi"], i * 2 + (L["d"] + q + 1))
                        v.tensor_tensor(d_split[:, q, 1, :], ring_d[:, q, :], d_split[:, q, 0, :].bitcast(f32),
                                        ALU.subtract).then_inc(s["dn_lo"], 1)
                        if conv:
                            g, c = B[4 + q], work[:, 4 + q, :]
                            w = [vec[:, ds(i * 8 + (a + 4 * q + j), 1)] if not isinstance(i, int) else
                                 vec[:, a + 8 * i + 4 * q + j:a + 8 * i + 4 * q + j + 1] for j in range(4)]
                            dve.wait_ge(s["a_used"], i * 4 + (u + 2 * q + 2))
                            step.did(v.tensor_scalar(c, g[:, 0:S], w[1], w[3], ALU.mult, ALU.add))
                            step.settle()
                            step.did(v.scalar_tensor_tensor(out=c[:, 1:S], in0=g[:, 0:S - 1], scalar=w[0],
                                                            in1=c[:, 1:S], op0=ALU.mult, op1=ALU.add))
                            step.settle()
                            v.scalar_tensor_tensor(out=c[:, 0:S - 1], in0=g[:, 1:S], scalar=w[2],
                                                   in1=c[:, 0:S - 1], op0=ALU.mult, op1=ALU.add)\
                                .then_inc(s["conv_ready"], 1)
                        dve.wait_ge(s["silu_ready"], i * 2 + (FT * f + q + 1))
                        v.tensor_tensor(work[:, q, :], work[:, 2 + q, :], B[4 + q][:, S:2 * S], ALU.mult)\
                            .then_inc(s["act_raw"], 1)
                        dve.wait_ge(s["act_hi"], i * 2 + (FT * f + q + 1))
                        v.tensor_tensor(act_split[:, q, 1, :], work[:, q, :], act_split[:, q, 0, :].bitcast(f32),
                                        ALU.subtract).then_inc(s["act_ready"], 1)
                tile_pair(0, False)
                with step.repeat(FT // 2 - 2, 4 if conv else 0, 1) as i:
                    tile_pair(i, False)
                tile_pair(FT // 2 - 1, True)
                for n in range(KT):
                    next_lo(L, n)
                dve.wait_ge(s["d_used"], L["d"] + FT)
                for b in range(4):
                    x2 = xT[:, 2 * b:2 * b + 2, :].rearrange("p a b -> p (a b)")
                    v.tensor_tensor(x2, x2, B[b][:, :], ALU.add).then_inc(s["x_added"], 2)

            def add_out(L, first, skipped=0):
                for n in range(KT):
                    if n + AHEAD < KT:
                        lo(L, first + n + AHEAD, 0, skipped)
                    dve.wait_ge(s["a_used"], L["u"] + first + n + 1)
                    v.tensor_tensor(xT[:, n, :], xT[:, n, :], B[4 + n % 4][:, 0:S], ALU.add)\
                        .then_inc(s["x_added"], 1)
                    if n >= 4:
                        next_lo(L, n - 4)

            def next_lo(L, n):
                if L["part"] + 1 < PARTS and n < early(plan[L["part"] + 1]):
                    lo(plan[L["part"] + 1], n)

            def stick(L):
                lo_loop(L, 20)
                lo(L, 23)

                def masked(h):
                    dve.wait_ge(s["z_done"], h + 1)
                    v.scalar_tensor_tensor(out=zm_(h), in0=B[h % 2][:, 0:384], scalar=HD ** -0.5,
                                           in1=T("stick_neg"), op0=ALU.mult, op1=ALU.add).then_inc(s["zm_ready"], 1)

                def softplus(h):
                    dve.wait_ge(s["ln_ready"], h + 1)
                    if h >= 4:
                        dve.wait_ge(s["cum_done"], h - 3)
                    v.scalar_tensor_tensor(out=sp_(h), in0=zm_(h),
                                           scalar=0.0, in1=ln_(h), op0=ALU.max, op1=ALU.add)\
                        .then_inc(s["sp_ready"], 1)

                def logit(h):
                    dve.wait_ge(s["cum_done"], h + 1)
                    if h >= 4:
                        dve.wait_ge(s["p_ready"], h - 3)
                    v.tensor_tensor(lg_(h), zm_(h), B[2 + h % 2][:, 0:384], ALU.subtract)\
                        .then_inc(s["lg_ready"], 1)

                for g in range(NH // 4 + 2):
                    for h in four_heads(g):
                        masked(h)
                    for h in four_heads(g - 1):
                        softplus(h)
                    for h in four_heads(g - 1):
                        logit(h)
                    for h in four_heads(g - 2)[::2]:
                        o_low(L, h // 2)
                for n in range(AHEAD):
                    lo(L, 24 + n)
                add_out(L, 24)

            def projections(L):
                count = PROJ[L["kind"]]
                for n in range(count):
                    if n + AHEAD < count:
                        lo(L, n + AHEAD)
                    for t in tiles_after(L["kind"], n):
                        norm_rope(L, t, row_of(L["kind"], t), t < 16, rope_of(L["kind"], t))

            def norm_rope(L, n, row, gained, rope):
                g = L["tiles"] + n
                b, r, t1 = B[n % 4], root_(n), work[:, 6, :]
                x = gained_(n) if gained else qkv[:, row, :]
                dst = qkv[:, row, :]
                dve.wait_ge(s["nr_mm"], g + 1)
                if gained:
                    dve.wait_ge(s["nr_std"], L["heads"] + n + 1)
                    step.did(v.reciprocal(r, r))
                if rope:
                    step.did(v.tensor_tensor(t1, b[:, S:2 * S], T("sin" + rope), ALU.mult))
                    dve.wait_ge(s["cos_ready"], L["ropes"] + ropes_until(L["kind"], n))
                    step.settle()
                    if gained:
                        step.did(v.tensor_tensor(t1, x, t1, ALU.add))
                        step.settle()
                        v.tensor_tensor(dst, t1, r, ALU.mult).then_inc(s["qk_ready"], 1)
                    else:
                        v.tensor_tensor(dst, x, t1, ALU.add).then_inc(s["qk_ready"], 1)
                else:
                    step.settle()
                    v.tensor_tensor(dst, x, r, ALU.mult).then_inc(s["qk_ready"], 1)
                dve.wait_ge(s["qk_ready"], g + 1)

            def softmax_heads(L, bias):
                H = L["heads"]

                def shifted(t):
                    dve.wait_ge(s["s_done"], H + 2 * t + 2)
                    if t >= 2:
                        dve.wait_ge(s["e_ready"], H + 2 * t - 2)
                    k = 4 * (t % 2)
                    for qt in range(NT):
                        sm = planes[:, 1, (k + 2 * qt) * S:(k + 2 * qt + 2) * S].rearrange("p (a b) -> p a b", a=2)
                        src = score_banks(t)[qt][:, :].rearrange("p (a b) -> p a b", a=2)
                        bb = bias(t, qt)
                        if bb is None:
                            last = v.tensor_scalar(sm, src, HD ** -0.5, None, ALU.mult)
                        else:
                            last = v.scalar_tensor_tensor(out=sm, in0=src, scalar=HD ** -0.5, in1=bb,
                                                          op0=ALU.mult, op1=ALU.add)
                    last.then_inc(s["sm_ready"], 2)
                    dve.wait_ge(s["sm_ready"], H + 2 * t + 2)
                    v.tensor_reduce(small[:, 48 + k:52 + k],
                                    planes[:, 1, k * S:(k + 4) * S].rearrange("p (a b) -> p a b", a=4),
                                    AX.X, ALU.max, negate=True).then_inc(s["nmx_ready"], 2)

                def normed(h):
                    dve.wait_ge(s["e_ready"], H + h + 1)
                    r = small[:, 8 + 2 * (h % 2):10 + 2 * (h % 2)]
                    step.did(v.reciprocal(r, small[:, 32 + 2 * (h % 4):34 + 2 * (h % 4)]))
                    step.settle()
                    for qt in range(NT):
                        p_ = planes[:, 0, (h % 4) * 512 + qt * S:(h % 4) * 512 + (qt + 1) * S]
                        last = v.tensor_scalar(p_, p_, r[:, qt:qt + 1], None, ALU.mult)
                    last.then_inc(s["pn_ready"], 1)

                shifted(0)
                for t in range(NH + 1):
                    if 0 <= t - 1 < NH:
                        normed(t - 1)
                    if t + 2 < NH and t % 2 == 0:
                        shifted(t // 2 + 1)
                    if L["kind"] == "dsa" and t >= 7 and t % 2:
                        o_low(L, (t - 7) // 2)

            def dsa(L):
                projections(L)
                sc = planes[:, 4, 0:512]
                for i in range(IDX_HEADS):
                    dve.wait_ge(s["idx_relu"], i + 1)
                    if i:
                        dve.wait_ge(s["idx_added"], i)
                    for qt in range(NT):
                        cols = slice(qt * S, (qt + 1) * S)
                        last = v.scalar_tensor_tensor(
                            out=sc[:, cols], in0=planes[:, 1, (i % 2) * 512 + qt * S:(i % 2) * 512 + (qt + 1) * S],
                            scalar=small[:, 16 + 8 * qt + i:17 + 8 * qt + i],
                            in1=(T("visible") if i == 0 else sc)[:, cols], op0=ALU.mult, op1=ALU.add)
                    last.then_inc(s["idx_added"], 1)
                dve.wait_ge(s["idx_added"], IDX_HEADS)
                for _ in range(N_SEL // 8):
                    for qt in range(NT):
                        step.did(v.max(top8[:, 8 * qt:8 * qt + 8], sc[:, qt * S:(qt + 1) * S]))
                    step.settle()
                    for qt in range(NT):
                        row = sc[:, qt * S:(qt + 1) * S]
                        step.did(v.match_replace(row, top8[:, 8 * qt:8 * qt + 8], row, TAKEN))
                    step.settle()
                step.did(v.tensor_scalar(sc, sc, TAKEN / 2, NEG, ALU.is_gt, ALU.mult))
                step.settle()
                softmax_heads(L, lambda t, qt: both(sc, qt))
                for n in range(AHEAD):
                    lo(L, 30 + n)
                for n in range(5, KT):
                    o_low(L, n)
                add_out(L, 30)

            def both(m, qt):
                return m[:, qt * S:(qt + 1) * S].unsqueeze(1).broadcast_to([P, 2, S])

            top8 = planes[:, 4, 512:528]

            def multi(L):
                r = L["multis"]
                projections(L)
                dve.wait_ge(s["na_loaded"], 16 * (r + 1))

                def bias(t, qt):
                    if t < 2:
                        return planes[:, 5, :].rearrange("p (h q n) -> p h q n", h=4, q=NT)[:, 2 * t:2 * t + 2, qt, :]
                    return both(T("dilated"), qt) if t < 5 else None
                softmax_heads(L, bias)
                def normed_segment(seg):
                    dve.wait_ge(s["on_std"], 3 * r + seg + 1)
                    step.did(v.reciprocal(work[:, 3 + seg, :], work[:, seg, :]))
                    for n in range(*SEGMENTS[seg]):
                        dve.wait_ge(s["ot_evac"], L["pairs"] + n + 1)
                        step.settle()
                        v.scalar_tensor_tensor(out=oT[:, n, :], in0=oT[:, n, :], scalar=V(f"out_g{L['idx']}", n),
                                               in1=work[:, 3 + seg, :], op0=ALU.mult, op1=ALU.mult)\
                            .then_inc(s["on_ready"], 1)

                last = SEGMENTS[-1][0]
                normed_segment(0)
                normed_segment(1)
                for n in range(last):
                    o_low(L, n)
                for n in range(AHEAD):
                    lo(L, 24 + n)
                normed_segment(2)
                for n in range(last, KT):
                    o_low(L, n)
                add_out(L, 24)

            for L in plan:
                norm(L, f"ffn_g{L['idx']}" if L["kind"] == "ffn" else f"mix_g{MIXER_GAIN[L['kind'], L['idx']]}")
                if L["part"] == 0:
                    dve.wait_ge(s["tab_loaded"], 16)
                dict(ffn=ffn, stick=stick, dsa=dsa, multi=multi,
                     rwkv=lambda L: rwkv_dve(dve, L, v, step, lo, out_split, add_out))[L["kind"]](L)

        @block.gpsimd
        def _(pool):
            pstep = Steps(pool, s["pool_step"])
            pool.wait_ge(s["tab_loaded"], 16)
            pool.wait_ge(s["const_loaded"], 32)
            for L in plan:
                if L["kind"] == "rwkv":
                    rwkv_pool(pool, L, pstep)
                if L["kind"] == "multi":
                    pool.wait_ge(s["h_ready"], 8 * (L["hs"] + 1))
                    pool.dma_start(planes[:, 5, :], na_in[L["idx"], :, :]).then_inc(s["na_loaded"], 16)
                if L["kind"] in ("dsa", "multi"):
                    pool.wait_ge(s["h_ready"], 8 * (L["hs"] + 1))
                    for t in range(0, KT, 4):
                        for i in range(2):
                            other = slice(HD * (1 - i), HD * (1 - i) + HD)
                            for n in range(t, t + 4):
                                last = nc.gpsimd.memset(padded_k(L, n)[other, i, :], 0.0)
                            pstep.did(last)
                            pstep.settle()

                    def times_cos(n):
                        rope = rope_of(L["kind"], n)
                        if rope:
                            x = gained_(n) if n < 16 else qkv[:, 8 + n, :]
                            pool.wait_ge(s["nr_mm"], L["tiles"] + n + 1)
                            nc.gpsimd.tensor_tensor(x, x, T("cos" + rope), ALU.mult).then_inc(s["cos_ready"], 1)

                    def pad(n):
                        pool.wait_ge(s["qk_ready"], L["tiles"] + KT + n + 1)
                        pool.wait_ge(s["cos_ready"], L["ropes"] + ropes_until(L["kind"], min(KT + n + 1, tiles - 1)))
                        pstep.did(nc.gpsimd.tensor_copy(padded_k(L, n)[0:HD, 0, :], qkv[0:HD, 8 + n, :]))
                        pstep.settle()
                        nc.gpsimd.tensor_copy(padded_k(L, n)[HD:P, 1, :], qkv[HD:P, 8 + n, :])\
                            .then_inc(s["k_padded"], 1)
                        pool.wait_ge(s["k_padded"], L["heads"] // 2 + n + 1)

                    tiles = 21 if L["kind"] == "dsa" else 16
                    for n in range(tiles + 1):
                        if n < tiles:
                            times_cos(n)
                        if 0 <= n - 1 - KT < KT:
                            pad(n - 1 - KT)


SEGMENTS = [(0, 2), (2, 5), (5, 8)]
MIXER_GAIN = {("rwkv", 0): 0, ("stick", 0): 1, ("dsa", 0): 2, ("rwkv", 1): 3, ("multi", 0): 4, ("multi", 1): 5}


def constants():
    t = np.zeros((P, TAB_W), np.float32)

    def put(name, a):
        o, w = TAB[name]
        t[:, o:o + w] = a
    i = np.arange(P)
    put("ident", np.eye(P))
    put("ones", 1.0)
    put("tri", i[:, None] >= i[None, :])
    same = i[:, None] // HD == i[None, :] // HD
    put("head_ones", same)
    put("head_mean", same / HD)
    own = np.arange(32)[None, :] == i[:, None] // HD
    put("head_sum", own)
    put("head_avg", own / HD)
    put("head_back", i[:, None] % 32 == i[None, :] // HD)

    def rotation(half, base_rows):
        m = np.zeros((P, P), np.float32)
        for o in base_rows:
            for d in range(half):
                m[o + d + half, o + d] = -1.0
                m[o + d, o + d + half] = 1.0
        return m
    put("rot0", rotation(32, [0, 64]))
    put("rot1", rotation(8, [0, 64]))
    put("rot2", rotation(16, [0, 32, 64, 96]))
    pos = np.arange(S).astype(np.float32)

    def inv(theta, dim):
        f = np.float32
        return (f(theta) ** (-np.arange(0, dim, 2, dtype=f) / f(dim))).astype(f)
    half = np.arange(32, dtype=np.float32) / np.float32(32)
    ang0 = pos[None, :] * (np.float32(1.0) / (np.float32(10000.0) ** half)).astype(np.float32)[:, None]
    d = i % HD
    put("cos0", np.cos(ang0)[d % 32])
    put("sin0", np.sin(ang0)[d % 32])
    ang1 = pos[None, :] * inv(500000.0, 16)[:, None]
    put("cos1", np.where((d < 16)[:, None], np.cos(ang1)[d % 8], 1.0))
    put("sin1", np.where((d < 16)[:, None], np.sin(ang1)[d % 8], 0.0))
    fr = inv(10000.0, 32)
    ang_r = (pos // GRID_W)[None, :] * fr[:, None]
    ang_c = (pos % GRID_W)[None, :] * fr[:, None]
    put("cos2", np.where((d < 32)[:, None], np.cos(ang_r)[d % 16], np.cos(ang_c)[d % 16]))
    put("sin2", np.where((d < 32)[:, None], np.sin(ang_r)[d % 16], np.sin(ang_c)[d % 16]))
    q = np.arange(S)
    ok = np.concatenate([i[:, None] < q[None, :], i[:, None] < i[None, :]], 1)
    put("stick_neg", np.where(ok, 0.0, NEG))
    qq = (np.arange(NT)[None, :, None] * P + i[:, None, None])
    vis = q[None, None, :] < (qq // CH + 1) * CH
    put("visible", np.where(vis, 0.0, NEG).reshape(P, -1))
    delta = np.abs(q[None, None, :] - qq)
    count = sum(((delta % dd == 0) & (delta // dd <= (w // 2) // dd)).astype(np.int64)
                for w, dd in ((128, 1), (512, 4), (2048, 16)))
    put("dilated", np.where(count > 0, np.log(np.maximum(count, 1)), NEG).reshape(P, -1))
    put("scan_keep", np.where(q % P == 0, 0.0, 1.0)[None, :])
    strict, incl = i[:, None] < i[None, :], i[:, None] <= i[None, :]
    put("rw_mask", np.concatenate([strict, incl, incl], 1))
    put("eps", EPS)
    put("gn_eps", GN_EPS)
    for lv in range(7):
        n = 1 << lv
        blk = ((i[:, None] // (2 * n) == i[None, :] // (2 * n)) & ((i[:, None] // n) % 2 == 1)
               & ((i[None, :] // n) % 2 == 0))
        put(f"level{lv}", np.eye(P) - blk)
        if lv == 0:
            put("level0t", np.eye(P) - blk.T)
    return t


def cols(vv):
    return np.asarray(vv).reshape(-1, P).T


def blocks(w):
    w = np.asarray(w)
    n = w.shape[1] // P
    return w.reshape(KT, P, n, P).transpose(2, 1, 0, 3).reshape(n, P, KT * P)


def padded(w, n):
    return np.concatenate([w, np.zeros((w.shape[0], n - w.shape[1]), w.dtype)], 1)


def layout(layers, I):
    A, Dn = [], []
    for kind, idx in layers:
        if kind == "ffn":
            gu = I["ffn_w_gu"][idx] if idx < 4 else I["w_gate_up_2"][idx - 4]
            dn = I["ffn_w_down"][idx] if idx < 4 else I["w_down_2"][idx - 4]
            b = blocks(gu)
            A.append(np.stack([b[:FT], b[FT:]], 1).reshape(2 * FT, P, D))
            Dn.append(dn.reshape(FT, P, D))
        elif kind == "stick":
            A += [blocks(I["sb_w_qkv"][0]), blocks(I["sb_w_out"][0])]
        elif kind == "dsa":
            w = I["ds_w_in"][0]
            q, k, vv, qi, ki, wi = np.split(w, [D, 2 * D, 3 * D, 3 * D + 512, 3 * D + 576], 1)
            A += [blocks(q), blocks(k), blocks(qi), blocks(np.concatenate([ki, ki], 1)), blocks(padded(wi, P)),
                  blocks(vv), blocks(I["ds_w_out"][0])]
        elif kind == "multi":
            w = I["w_in_2"][idx]
            qa, ka, va, qd, kd, vd, qc, kc, vc = np.split(
                w, np.cumsum([256, 256, 256, 384, 384, 384, 384, 128]).tolist(), 1)

            def spread(t):
                return np.concatenate([t[:, HD * (h // 3):HD * (h // 3) + HD] for h in range(6)], 1)
            A += [blocks(np.concatenate([qa, qd, qc, ka, kd, spread(kc), va, vd, spread(vc)], 1)),
                  blocks(I["w_out_2"][idx])]
        elif kind == "rwkv":
            w = I["rw_w_rkv"][idx]
            v1 = I["rw_v1"][0] if idx else np.zeros((D, LORA_V), np.float32)
            v2 = I["rw_v2"][0] if idx else np.zeros((LORA_V, D), np.float32)
            g1, g2 = I["rw_g1"][idx], I["rw_g2"][idx]
            last = np.concatenate([g2[P:], v2, np.zeros((64, D), np.float32)], 0)
            A += [blocks(w[0]), blocks(w[1]), blocks(w[2]),
                  blocks(padded(np.concatenate([g1[:, P:], v1], 1), P)), blocks(g1[:, :P]),
                  blocks(np.concatenate([I["rw_w1"][idx], I["rw_a1"][idx]], 1)),
                  np.concatenate([I["rw_w2"][idx], I["rw_a2"][idx]], 0)[None], g2[None, :P], last[None],
                  blocks(I["rw_w_out"][idx])]
    wa = np.concatenate(A, 0)
    wd = np.concatenate(Dn, 0) if Dn else np.zeros((1, P, D), np.float32)
    vec = np.zeros((P, VEC_W), np.float32)

    def put(name, a):
        o, w = VEC[name]
        vec[:, o:o + w] = a
    for l in range(4):
        put(f"mix_g{l}", cols(I["norm_mix"][l]))
        put(f"ffn_g{l}", cols(I["norm_ffn"][l]))
    for l in range(2):
        put(f"mix_g{4 + l}", cols(I["norm1_g_2"][l]))
        put(f"ffn_g{4 + l}", cols(I["norm2_g_2"][l]))
        put(f"out_g{l}", cols(I["out_norm_g_2"][l]))
        cw = np.concatenate([I["conv_w_2"][l], I["conv_b_2"][l][None]], 0)
        put(f"conv{l}", cw.reshape(4, FT, P).transpose(2, 1, 0).reshape(P, 4 * FT))
        for j in range(6):
            put(f"mix{j}_{l}", cols(I["rw_mix"][l, j]))
        for n, key in (("w0", "rw_w0"), ("a0", "rw_a0"), ("k_k", "rw_k_k"), ("k_a", "rw_k_a"), ("ln_w", "rw_ln_w"),
                       ("ln_b", "rw_ln_b")):
            put(f"{n}_{l}", cols(I[key][l]))
        put(f"r_k_{l}", cols(I["rw_r_k"][l].reshape(-1)))
        qg, kg = I["q_norm_g_2"][l], I["k_norm_g_2"][l]
        fam = [0, 0, 1, 1, 1, 2, 2, 2]
        g = [np.concatenate([t[m], t[m]]) for t in (qg, kg) for m in fam] + [np.ones(P, np.float32)] * 8
        put(f"gain{1 + l}", np.stack(g, 1))
    put("v0_", cols(I["rw_v0"][0]))
    g = [np.concatenate([I[t][0]] * 2) for t in ("ds_q_norm", "ds_k_norm") for _ in range(8)]
    put("gain0", np.stack(g + [np.ones(P, np.float32)] * 8, 1))
    t = np.arange(S)
    r, c = t // GRID_W, t % GRID_W
    c0 = np.clip(c - NA_KW // 2, 0, GRID_W - NA_KW)
    inside = (c[None, :] >= c0[:, None]) & (c[None, :] < c0[:, None] + NA_KW)
    dr = r[None, :] - r[:, None] + NA_KH - 1
    dc = np.clip(c[None, :] - c[:, None] + NA_KW - 1, 0, 2 * NA_KW - 2)
    b = np.where(inside[None, None], I["rpb_2"][:, :, dr, dc], np.float32(NEG))
    na = b.reshape(2, 4, NT, P, S).transpose(0, 3, 1, 2, 4).reshape(2, P, 4 * NT * S)
    x = I["x"][0].T.reshape(KT, P, S).transpose(1, 0, 2)
    c_ = np.ascontiguousarray
    return dict(x=c_(x), wa=c_(wa), wd=c_(wd), tab=constants(), vec=vec, na=c_(na.astype(np.float32)))


def kernel(**inputs):
    import concourse.bacc as bacc
    from concourse.bass_utils import run_bass_kernel_spmd
    nc = bacc.Bacc("TRN2", target_bir_lowering=False, num_devices=1)
    arrays = layout(FULL, {k: np.asarray(a) for k, a in inputs.items()})
    args = {n: nc.dram_tensor(n, a.shape, mybir.dt.from_np(a.dtype), kind="ExternalInput").ap()
            for n, a in arrays.items()}
    out = nc.dram_tensor("out", (P, KT, S), mybir.dt.float32, kind="ExternalOutput").ap()
    build_program(nc, FULL, args["x"], args["wa"], args["wd"], args["tab"], args["vec"], args["na"], out)
    r = run_bass_kernel_spmd(nc, [arrays], core_ids=[0])
    y = r.results[0]["out"]
    return np.ascontiguousarray(y.transpose(1, 0, 2).reshape(D, S).T)[None]
```
